# Optimizing a Trainium2 kernel written in Bass

```python
import math
import jax, jax.numpy as jnp
from jax import lax
import numpy as np

D_MODEL = 2048
BATCH = 1
SEQ = 256
DEPTH = 1
DEC_BATCH = 8
DEC_SEQ = 4
PAST_LEN = 2048
PAGE_SIZE = 128

SSD_HEAD_DIM = 64
SSD_INNER = D_MODEL
SSD_HEADS = SSD_INNER // SSD_HEAD_DIM
SSD_GROUPS = 4
SSD_HEADS_PER_GROUP = SSD_HEADS // SSD_GROUPS
SSD_STATE = 128
SSD_CONV = 4
SSD_CONV_CH = SSD_INNER + 2 * SSD_GROUPS * SSD_STATE
SSD_CHUNK = 128
CONF_CH = D_MODEL
CONF_KERNEL = 31
N_GROUPS = 4
EXPERTS_PER_GROUP = 8
N_EXPERTS = N_GROUPS * EXPERTS_PER_GROUP
TOP_K_IN_GROUP = 2
D_FF_EXPERT = D_MODEL // 8
IN_SPLITS = (SSD_INNER, SSD_CONV_CH, SSD_HEADS, 2 * CONF_CH, D_MODEL, D_MODEL)
IN_COLS = sum(IN_SPLITS)
EPS = 1e-6

kernel_name = "hybrid_ssd_conformer_hmoe_adaln_step"

def _rmsnorm(x, g):
    x32 = x.astype(jnp.float32)
    y = x32 * lax.rsqrt(jnp.mean(x32 * x32, axis=-1, keepdims=True) + EPS)
    return (y * g.astype(jnp.float32)).astype(x.dtype)

def _layernorm(x, g, b):
    x32 = x.astype(jnp.float32)
    mu = jnp.mean(x32, axis=-1, keepdims=True)
    var = jnp.mean(jnp.square(x32 - mu), axis=-1, keepdims=True)
    y = (x32 - mu) * lax.rsqrt(var + EPS)
    return (y * g.astype(jnp.float32) + b.astype(jnp.float32)).astype(x.dtype)

def _split(a, sizes):
    idx = np.cumsum(sizes)[:-1].tolist()
    return jnp.split(a, idx, axis=-1)

def _causal_dwconv(u, prev, w, b):
    k = w.shape[0]
    padded = jnp.concatenate([prev.astype(u.dtype), u], axis=1)
    out = lax.conv_general_dilated(
        padded, w[:, None, :].astype(u.dtype), window_strides=(1,), padding='VALID',
        dimension_numbers=('NWC', 'WIO', 'NWC'), feature_group_count=u.shape[-1])
    return out + b.astype(u.dtype), padded[:, padded.shape[1] - (k - 1):]

def _ssd(x, dt, a, bm, cm, s0):
    f32 = jnp.float32
    dtype = x.dtype
    bsz, t, g, k, p = x.shape
    n = bm.shape[-1]
    L = SSD_CHUNK if t % SSD_CHUNK == 0 else t
    nc = t // L
    x = x.astype(f32).reshape(bsz, nc, L, g, k, p)
    dt = dt.astype(f32).reshape(bsz, nc, L, g, k)
    bm = bm.astype(f32).reshape(bsz, nc, L, g, n)
    cm = cm.astype(f32).reshape(bsz, nc, L, g, n)
    acum = jnp.cumsum(dt * a.astype(f32), axis=2)
    causal = jnp.tril(jnp.ones((L, L), dtype=bool))[None, None, :, :, None, None]
    seg = acum[:, :, :, None] - acum[:, :, None, :]
    decay = jnp.exp(jnp.where(causal, seg, -jnp.inf))
    cb = jnp.einsum('bcign,bcjgn->bcijg', cm, bm)
    m = cb[..., None] * decay * dt[:, :, None]
    y = jnp.einsum('bcijgk,bcjgkp->bcigkp', m, x)
    w_end = jnp.exp(acum[:, :, -1:] - acum) * dt
    local = jnp.einsum('bclgn,bclgk,bclgkp->bcgkpn', bm, w_end, x)
    chunk_decay = jnp.exp(acum[:, :, -1])

    def step(s, inp):
        dec, loc = inp
        return dec[..., None, None] * s + loc, s

    s_last, s_prev = lax.scan(step, s0.astype(f32),
                              (jnp.moveaxis(chunk_decay, 1, 0), jnp.moveaxis(local, 1, 0)))
    s_prev = jnp.moveaxis(s_prev, 0, 1)
    y = y + jnp.einsum('bclgn,bcgkpn->bclgkp', cm, s_prev) * jnp.exp(acum)[..., None]
    return y.reshape(bsz, t, g, k, p).astype(dtype), s_last.astype(dtype)

def _hier_moe(h, w_gr, b_gr, w_er, b_er, w_gate, w_up, w_down):
    f32 = jnp.float32
    bsz, t, d = h.shape
    hf = h.reshape(bsz * t, d)
    g_prob = jax.nn.softmax((hf @ w_gr + b_gr).astype(f32), axis=-1)
    g_top, g_idx = lax.top_k(g_prob, 1)
    e_logit = (hf @ w_er + b_er).astype(f32).reshape(-1, N_GROUPS, EXPERTS_PER_GROUP)
    e_logit = jnp.take_along_axis(e_logit, g_idx[:, :, None], axis=1)[:, 0]
    e_top, e_idx = lax.top_k(jax.nn.softmax(e_logit, axis=-1), TOP_K_IN_GROUP)
    e_top = e_top / jnp.sum(e_top, axis=-1, keepdims=True)
    within = jnp.sum(jax.nn.one_hot(e_idx, EXPERTS_PER_GROUP, dtype=f32) * e_top[..., None], axis=1)
    gate = (jax.nn.one_hot(g_idx[:, 0], N_GROUPS, dtype=f32) * g_top)[:, :, None] * within[:, None, :]
    gate = gate.reshape(-1, N_EXPERTS).astype(h.dtype)
    hidden = jax.nn.silu(jnp.einsum('td,edf->tef', hf, w_gate)) * jnp.einsum('td,edf->tef', hf, w_up)
    out = jnp.einsum('tef,efd->td', hidden * gate[:, :, None], w_down)
    return out.reshape(bsz, t, d)

def _layer(x, c, ssm0, sconv0, cconv0, norm_mix_g, norm_ffn_g, w_ada, b_ada, w_in,
           ssd_conv_w, ssd_conv_b, ssd_dt_bias, ssd_a_log, ssd_d, ssd_norm_g, w_ssd_out,
           conf_conv_w, conf_conv_b, conf_ln_g, conf_ln_b, w_conf_out, w_o,
           w_group_router, b_group_router, w_expert_router, b_expert_router,
           w_exp_gate, w_exp_up, w_exp_down):
    bsz, t, _ = x.shape
    G, K, P, N = SSD_GROUPS, SSD_HEADS_PER_GROUP, SSD_HEAD_DIM, SSD_STATE
    mod = jax.nn.silu(c) @ w_ada + b_ada
    sh1, sc1, g1, sh2, sc2, g2 = jnp.split(mod[:, None, :], 6, axis=-1)
    h = _rmsnorm(x, norm_mix_g) * (1 + sc1) + sh1
    z, xbc, dt_raw, glu_in, gate_ssd, gate_conf = _split(h @ w_in, IN_SPLITS)
    xbc, sconv_new = _causal_dwconv(xbc, sconv0, ssd_conv_w, ssd_conv_b)
    xbc = jax.nn.silu(xbc)
    xs, bm, cm = _split(xbc, (SSD_INNER, G * N, G * N))
    xs = xs.reshape(bsz, t, G, K, P)
    bm = bm.reshape(bsz, t, G, N)
    cm = cm.reshape(bsz, t, G, N)
    dt = jax.nn.softplus(dt_raw.astype(jnp.float32) + ssd_dt_bias.astype(jnp.float32)).reshape(bsz, t, G, K)
    a = -jnp.exp(ssd_a_log.astype(jnp.float32)).reshape(G, K)
    y, s_last = _ssd(xs, dt, a, bm, cm, ssm0.reshape(bsz, G, K, P, N))
    y = y + ssd_d.reshape(G, K, 1).astype(y.dtype) * xs
    y = y.reshape(bsz, t, G, K * P) * jax.nn.silu(z.reshape(bsz, t, G, K * P))
    y = _rmsnorm(y, ssd_norm_g.reshape(G, K * P))
    ssd_branch = y.reshape(bsz, t, SSD_INNER) @ w_ssd_out
    u_a, u_g = jnp.split(glu_in, 2, axis=-1)
    u = u_a * jax.nn.sigmoid(u_g)
    v, cconv_new = _causal_dwconv(u, cconv0, conf_conv_w, conf_conv_b)
    v = jax.nn.silu(_layernorm(v, conf_ln_g, conf_ln_b))
    conf_branch = v @ w_conf_out
    mixed = (jax.nn.sigmoid(gate_ssd) * ssd_branch + jax.nn.sigmoid(gate_conf) * conf_branch) @ w_o
    x = x + g1 * mixed
    h2 = _rmsnorm(x, norm_ffn_g) * (1 + sc2) + sh2
    x = x + g2 * _hier_moe(h2, w_group_router, b_group_router, w_expert_router, b_expert_router,
                           w_exp_gate, w_exp_up, w_exp_down)
    return x, s_last.reshape(bsz, SSD_HEADS, P, N), sconv_new, cconv_new

def _trunk(x, c, ssm, sconv, cconv, weights, final_norm_g):
    ssm_out, sconv_out, cconv_out = [], [], []
    for l in range(DEPTH):
        x, s1, s2, s3 = _layer(x, c, ssm[l], sconv[l], cconv[l], *[w[l] for w in weights])
        ssm_out.append(s1)
        sconv_out.append(s2)
        cconv_out.append(s3)
    return (_rmsnorm(x, final_norm_g), jnp.stack(ssm_out), jnp.stack(sconv_out), jnp.stack(cconv_out))

def setup_inputs(seed: int = 0) -> dict:
    key = jax.random.key(seed)
    ks = iter(jax.random.split(key, 40))

    def nrm(shape, scale):
        return jax.random.normal(next(ks), shape, jnp.float32) * scale

    dt0 = jnp.exp(jax.random.uniform(next(ks), (DEPTH, SSD_HEADS), jnp.float32,
                                     minval=math.log(1e-3), maxval=math.log(1e-1)))
    inp = {
        "x_prompt": nrm((BATCH, SEQ, D_MODEL), 1.0),
        "x_sample": nrm((DEC_BATCH, DEC_SEQ, D_MODEL), 1.0),
        "c_prompt": nrm((BATCH, D_MODEL), 1.0),
        "c_sample": nrm((DEC_BATCH, D_MODEL), 1.0),
        "state_ssm": nrm((DEPTH, DEC_BATCH, SSD_HEADS, SSD_HEAD_DIM, SSD_STATE), 0.1),
        "state_ssd_conv": nrm((DEPTH, DEC_BATCH, SSD_CONV - 1, SSD_CONV_CH), 1.0),
        "state_conf_conv": nrm((DEPTH, DEC_BATCH, CONF_KERNEL - 1, CONF_CH), 0.5),
        "norm_mix_g": 1.0 + nrm((DEPTH, D_MODEL), 0.02),
        "norm_ffn_g": 1.0 + nrm((DEPTH, D_MODEL), 0.02),
        "w_ada": nrm((DEPTH, D_MODEL, 6 * D_MODEL), 0.5 * D_MODEL ** -0.5),
        "b_ada": nrm((DEPTH, 6 * D_MODEL), 0.02),
        "w_in": nrm((DEPTH, D_MODEL, IN_COLS), D_MODEL ** -0.5),
        "ssd_conv_w": nrm((DEPTH, SSD_CONV, SSD_CONV_CH), SSD_CONV ** -0.5),
        "ssd_conv_b": nrm((DEPTH, SSD_CONV_CH), 0.02),
        "ssd_dt_bias": dt0 + jnp.log(-jnp.expm1(-dt0)),
        "ssd_a_log": jnp.log(jax.random.uniform(next(ks), (DEPTH, SSD_HEADS), jnp.float32, minval=1.0, maxval=16.0)),
        "ssd_d": 1.0 + nrm((DEPTH, SSD_HEADS), 0.1),
        "ssd_norm_g": 1.0 + nrm((DEPTH, SSD_INNER), 0.02),
        "w_ssd_out": nrm((DEPTH, SSD_INNER, D_MODEL), SSD_INNER ** -0.5),
        "conf_conv_w": nrm((DEPTH, CONF_KERNEL, CONF_CH), CONF_KERNEL ** -0.5),
        "conf_conv_b": nrm((DEPTH, CONF_CH), 0.02),
        "conf_ln_g": 1.0 + nrm((DEPTH, CONF_CH), 0.02),
        "conf_ln_b": nrm((DEPTH, CONF_CH), 0.02),
        "w_conf_out": nrm((DEPTH, CONF_CH, D_MODEL), CONF_CH ** -0.5),
        "w_o": nrm((DEPTH, D_MODEL, D_MODEL), D_MODEL ** -0.5),
        "w_group_router": nrm((DEPTH, D_MODEL, N_GROUPS), D_MODEL ** -0.5),
        "b_group_router": nrm((DEPTH, N_GROUPS), 0.01),
        "w_expert_router": nrm((DEPTH, D_MODEL, N_EXPERTS), D_MODEL ** -0.5),
        "b_expert_router": nrm((DEPTH, N_EXPERTS), 0.01),
        "w_exp_gate": nrm((DEPTH, N_EXPERTS, D_MODEL, D_FF_EXPERT), D_MODEL ** -0.5),
        "w_exp_up": nrm((DEPTH, N_EXPERTS, D_MODEL, D_FF_EXPERT), D_MODEL ** -0.5),
        "w_exp_down": nrm((DEPTH, N_EXPERTS, D_FF_EXPERT, D_MODEL), D_FF_EXPERT ** -0.5),
        "final_norm_g": 1.0 + nrm((D_MODEL,), 0.02),
    }
    return inp

def reference(x_prompt, x_sample, c_prompt, c_sample, state_ssm, state_ssd_conv, state_conf_conv,
              norm_mix_g, norm_ffn_g, w_ada, b_ada, w_in, ssd_conv_w, ssd_conv_b, ssd_dt_bias,
              ssd_a_log, ssd_d, ssd_norm_g, w_ssd_out, conf_conv_w, conf_conv_b, conf_ln_g,
              conf_ln_b, w_conf_out, w_o, w_group_router, b_group_router, w_expert_router,
              b_expert_router, w_exp_gate, w_exp_up, w_exp_down, final_norm_g):
    weights = (norm_mix_g, norm_ffn_g, w_ada, b_ada, w_in, ssd_conv_w, ssd_conv_b, ssd_dt_bias,
               ssd_a_log, ssd_d, ssd_norm_g, w_ssd_out, conf_conv_w, conf_conv_b, conf_ln_g,
               conf_ln_b, w_conf_out, w_o, w_group_router, b_group_router, w_expert_router,
               b_expert_router, w_exp_gate, w_exp_up, w_exp_down)
    bp = x_prompt.shape[0]
    dtp = x_prompt.dtype
    ssm_p0 = jnp.zeros((DEPTH, bp, SSD_HEADS, SSD_HEAD_DIM, SSD_STATE), dtp)
    sconv_p0 = jnp.zeros((DEPTH, bp, SSD_CONV - 1, SSD_CONV_CH), dtp)
    cconv_p0 = jnp.zeros((DEPTH, bp, CONF_KERNEL - 1, CONF_CH), dtp)
    y_prompt, ssm_p, sconv_p, cconv_p = _trunk(x_prompt, c_prompt, ssm_p0, sconv_p0, cconv_p0,
                                               weights, final_norm_g)
    y_sample, ssm_s, sconv_s, cconv_s = _trunk(x_sample, c_sample, state_ssm, state_ssd_conv,
                                               state_conf_conv, weights, final_norm_g)
    return (y_prompt, y_sample, ssm_p, sconv_p, cconv_p, ssm_s, sconv_s, cconv_s)


_drawn_inputs = setup_inputs


def setup_inputs(seed=0):
    import zlib

    import numpy as np

    out = dict(_drawn_inputs(seed))
    spreads = {}
    factors = {'norm_ffn_g': 6.142,
     'ssd_d': 4.783,
     'ssd_norm_g': 8.0,
     'conf_conv_b': 5.803,
     'conf_ln_g': 8.0,
     'conf_ln_b': 8.0,
     'b_group_router': 64.0,
     'b_expert_router': 8.0,
     'final_norm_g': 7.515}
    for name, (base, spread) in spreads.items():
        noise = np.random.default_rng([zlib.crc32(name.encode()), seed]).standard_normal(out[name].shape)
        drawn = base * np.exp(spread * noise) if base else spread * noise
        out[name] = __import__('jax').numpy.asarray(drawn.astype(out[name].dtype))
    for name, factor in factors.items():
        out[name] = (out[name] * factor).astype(out[name].dtype)
    return out
```

```python
from contextlib import ExitStack, contextmanager, nullcontext

import concourse.bass as bass
from concourse import mybir

F32 = mybir.dt.float32
I32 = mybir.dt.int32
ALU = mybir.AluOpType
ACT = mybir.ActivationFunctionType
AX_X = mybir.AxisListType.X
ds = bass.ds

P = 128
D = 2048
KC = D // P
NP = 256
NB, NL = 8, 4
NS = NB * NL
T = NP + NS
NSEQ = 1 + NB
XC = 3072 // P
H = 32
G = 4
HD = 64
CK = 31
SK = 4
NE = 32
NG = 4
EG = 8
EPS = 1e-6
SLOTS = 2 * T
WIN = 128
UC = 256
RING = 4
TOK = [(0, P), (P, P), (NP, NS)]

Z0, X0, DT0, GLU0 = 0, D, D + 3072, D + 3072 + H
GS0, GC0 = GLU0 + 2 * D, GLU0 + 3 * D

GLU_N, XBC_N = 4, 3

MIXED = "pappappappap"
PHASES = [("ada", 5, "aaaa"), ("glu", 2, MIXED), ("gc", 1, MIXED), ("co", 1, MIXED), ("z", 1, MIXED),
          ("xbc", 3, "pppp"), ("gs", 1, MIXED), ("so", 1, MIXED), ("wo", 2, "pppp")]


def phase_uses(name):
    steps, units = {n: (s, u) for n, s, u in PHASES}[name]
    return {**{b: steps * units.count("p") // 2 for b in range(4)},
            **{b: steps * units.count("a") // 2 for b in range(4, 8)}}


class Count:

    def __init__(self, sem):
        self.sem, self.n, self.off = sem, 0, 0

    def mark(self, ins):
        ins.then_inc(self.sem, 1)
        self.n += 1

    def wait(self, eng, back=0):
        eng.wait_ge(self.sem, self.off + self.n - back)

    def link(self, eng, ins):
        self.mark(ins)
        self.wait(eng)

    @contextmanager
    def loop(self, i, trips, per):
        start = self.n
        self.off = i * per
        yield
        assert self.n == start + per, self.n - start
        self.n, self.off = start + trips * per, 0


USES = [
    ("x", {0: 4, 1: 4, 2: 4, 3: 4}), ("c", {4: 1}), ("vec", {5: 1, 6: 1}), ("cst", {4: 4, 5: 4, 6: 4, 7: 4}),
    ("ada", phase_uses("ada")), ("n1", {4: 1}), ("glu", phase_uses("glu")), ("tail", {4: 1, 5: 1, 6: 1, 7: 1}),
    ("gc", phase_uses("gc")), ("ln", {4: 1, 5: 1}), ("co", phase_uses("co")), ("dt", {6: 1}),
    ("z", phase_uses("z")), ("cum", {7: 1}), ("sst", {4: 1, 5: 1}), ("xbc", phase_uses("xbc")),
    ("xtail", {4: 2, 5: 2, 6: 1, 7: 1}), ("ssd", {0: 32, 1: 32, 2: 16, 3: 8, 4: 16, 5: 16, 6: 16, 7: 16}),
    ("gn", {4: 1, 5: 1, 6: 1, 7: 1}), ("gs", phase_uses("gs")), ("so", phase_uses("so")),
    ("wo", phase_uses("wo")), ("n2", {4: 1}), ("route", {5: 1, 6: 1, 7: 1}),
    ("gates", {0: 1, 1: 1, 2: 1, 3: 1}), ("gather", {b: 8 for b in range(6)}),
    ("pt", {4: 3, 5: 2}), ("unsort", {0: 4, 1: 4, 2: 4, 3: 4, 4: 8, 5: 8, 6: 8, 7: 8}),
    ("n3", {4: 1}), ("y", {4: 3, 5: 3, 6: 3, 7: 3}),
]


def uses_before():
    at, out = {b: 0 for b in range(8)}, {}
    for name, banks in USES:
        out[name] = dict(at)
        for b, n in banks.items():
            at[b] += n
    return out


def hybrid_step(nc, a, o):
    with ExitStack() as ctx:
        def sb(name, shape, dt=F32):
            return ctx.enter_context(nc.sbuf_tensor(name, shape, dt))

        def sem(name):
            return ctx.enter_context(nc.semaphore(name))

        ring = sb("ring", [P, RING, KC, UC])
        xT = sb("xT", [P, KC, T])
        hT = sb("hT", [P, KC, T])
        ident = sb("ident", [P, P])
        ones = sb("ones", [P, P])
        upper = sb("upper", [P, P])
        seqsel = sb("seqsel", [NS, NB])
        blk = sb("blk", [NS, NS])
        ublk = sb("ublk", [NS, NS])
        vcol = sb("vcol", [P, 7 * P])
        mod = sb("mod", [P, 6 * KC, NSEQ])
        scaleA = sb("scaleA", [P, KC, NSEQ])
        rs = sb("rs", [P, T])
        stat = sb("stat", [P, T])
        dcol = sb("dcol", [P, KC])
        dt_tok = sb("dt_tok", [P, 3, H])
        dtA = sb("dtA", [P, 3, H])
        acum = sb("acum", [P, 3, H])
        wend = sb("wend", [P, 4, H])
        rows_bc = sb("rows_bc", [P, 2, H])
        rbias = sb("rbias", [P, 36])
        meta_i = sb("meta_i", [P, 3, NE + 1], I32)
        WORK = 24000
        work = sb("work", [P, WORK])

        def carve(at, *dims):
            n = 1
            for x in dims:
                n *= x
            assert at + n <= WORK, (at, n)
            v = work[:, at:at + n]
            if len(dims) == 2:
                v = v.rearrange("p (a b) -> p a b", a=dims[0])
            if len(dims) == 3:
                v = v.rearrange("p (a b c) -> p a b c", a=dims[0], b=dims[1])
            if len(dims) == 4:
                v = v.rearrange("p (a b c d) -> p a b c d", a=dims[0], b=dims[1], c=dims[2])
            return v

        BIG = KC * T
        zb = carve(0, KC, T)
        vb = carve(BIG, KC, T)
        xbcT = carve(BIG, XC, T)
        gb = carve(BIG + XC * T, KC, T)
        TMP = BIG + XC * T + BIG
        sq = zb
        xrow = carve(0, 3, D)
        crow = carve(3 * D, D)
        vrow = carve(4 * D, 7, P)
        cstrow = carve(4 * D + 7 * P + KC * NSEQ, 2, D)
        t = TMP
        usamp = carve(t, KC, NB, CK - 1 + NL); t += KC * NB * (CK - 1 + NL)
        upad = carve(t, 4, CK - 1 + NP); t += 4 * (CK - 1 + NP)
        sgl = carve(t, 4, T); t += 4 * T
        utail = carve(t, KC, CK - 1 + NS); t += KC * (CK - 1 + NS)
        assert t == TMP + 7640
        cT = carve(t, KC, NSEQ); t += KC * NSEQ
        fold = carve(t, NSEQ)
        part_glu = carve(BIG + XC * T, 2, UC)
        part_mix = carve(TMP + 6862, 2, UC)
        tmpc = carve(0, KC, NS)
        uvs = carve(KC * NS, KC, NS)
        tailrow = carve(2 * KC * NS, D)
        wdt = carve(TMP, KC, H)
        t = TMP
        xsamp = carve(t, XC, NB, SK - 1 + NL); t += XC * NB * (SK - 1 + NL)
        xraw = carve(t, 2, SK - 1 + NP); t += 2 * (SK - 1 + NP)
        xtail = carve(t, XC, SK - 1 + NB * (SK - 1)); t += XC * (SK - 1) * (1 + NB)
        sstrow = carve(t, XC * P); t += XC * P
        acc = carve(t, 2, NP); t += 2 * NP
        tmps = carve(t, XC, NS); t += XC * NS
        uxs = carve(t, XC, NS); t += XC * NS
        t = TMP
        s0 = carve(t, 2, NB, P); t += 2 * NB * P
        s0T = carve(t, NB, P); t += NB * P
        bexp = carve(t, NB, P); t += NB * P
        xst = carve(t, T); t += T
        bst = carve(t, T); t += T
        xtok = carve(t, 3, P); t += 3 * P
        btok = carve(t, 3, P); t += 3 * P
        cbm = carve(t, 3, P); t += 3 * P
        mt = carve(t, 2, T); t += 2 * T
        cs = carve(t, 2, P + NS); t += 2 * (P + NS)
        xw = carve(t, 4, P); t += 4 * P
        s1T = carve(t, P); t += P
        sfin = carve(t, P); t += P
        dax = carve(t, P); t += P
        dec = carve(t, NB); t += NB
        ud = stat
        hs = carve(0, KC, SLOTS)
        ys = carve(KC * SLOTS, KC, SLOTS)
        t = 2 * KC * SLOTS
        gbc = carve(t, SLOTS); t += SLOTS
        ebc = carve(t, SLOTS); t += SLOTS
        pm = carve(t, 3, SLOTS); t += 3 * SLOTS
        iota_e = carve(t, NE); t += NE
        strict = carve(t, P); t += P
        meta = carve(t, 3, NE + 1); t += 3 * (NE + 1)
        rt = t
        htok = carve(t, 2, 3 * P); t += 2 * 3 * P
        gwin = carve(rt, T)
        sil = carve(rt + T, 2, T)
        hid = carve(rt + 3 * T, 2, T)
        assert rt + 5 * T <= WORK
        hwin = hT[:, :, 0:2 * WIN].rearrange("p k (two w) -> p two k w", two=2)
        t = KC * SLOTS
        wr = carve(t, KC, 36); t += KC * 36
        lg = carve(t, 3, 36); t += 108
        small = [carve(t + 96 * n, 3, 32) for n in range(14)]; t += 96 * 14
        tiny = [carve(t + 4 * n, 3) for n in range(20)]; t += 80
        iota_s = carve(t, SLOTS); t += SLOTS
        gt = carve(t, 3, SLOTS); t += 3 * SLOTS
        et = carve(t, 3, SLOTS); t += 3 * SLOTS
        tq = carve(t, SLOTS); t += SLOTS
        cntb = carve(t, P); t += P
        sel = carve(t, 3, EG); t += 3 * EG
        chosen = small[12]
        sp_abs, sp_e, sp_u, sp_ln, sp_d, sp_z, sp_m = [carve(TMP + KC * H + 96 * n, 3, H) for n in range(7)]
        grs = carve(TMP + 4096, G, T)
        pt = carve(0, 5, T)
        ytok = carve(5 * T, 2, 5 * P)
        yrow = carve(0, 3, D)
        assert 3 * D <= KC * SLOTS

        bank = [ctx.enter_context(nc.psum_tensor(f"bank{b}", [P, 512], F32)) for b in range(8)]

        slot_loaded = [sem(f"slot_loaded{s}") for s in range(RING)]
        bank_ready = [sem(f"bank_ready{b}") for b in range(8)]
        bank_free = [sem(f"bank_free{b}") for b in range(8)]
        base = uses_before()

        def use(name, b, k=0):
            return base[name][b] + 1 + k

        pool = Count(sem("pool_step"))
        dve = Count(sem("dve_step"))
        act = Count(sem("act_step"))
        S = {n: sem(n) for n in (
            "consts_ready x_loaded c_loaded v_loaded vrow_zero small_loaded cst_loaded usamp_ready silu_c c_ready "
            "squares_ready mean_ready root_ready h_ready conv_ready y_fin vsamp_ready tail_ready tail_out "
            "v_ready gc_ready centred wdt_loaded dt_abs dt_exp dt_log one_plus dta_ready w_arg w_exp w_ready a_exp sst_loaded "
            "xpad_ready acc_ready acc_free xbc_ready xtail_ready xrow_ready xtail_out bst_ready xst_ready "
            "ud_ready dax_ready seg_ready exp_ready m_ready xw_ready bexp_ready dec_free scaled sf_out "
            "y_done gs_ready gsq_ready gmean_ready groot_ready gn_ready y_ready merged x_mid "
            "wr_loaded logits_ready gexp eexp gates_ready cnt_ready meta_ready sort_ready ys_zero "
            "win_ready g_ready u_done sil_ready hid_ready d_ready ys_done wide_ready wide_free "
            "part_zero sf_free st_go moe_ready out_rows out_done pads_zero state_copy tail_rows e_arg pooled vb_free").split()}
        s0_loaded = [sem(f"s0_loaded{p}") for p in range(2)]
        st_out = [sem(f"st_out{p}") for p in range(2)]

        w_ada = a["w_ada"][0].rearrange("(k p) n -> p k n", p=P)
        w_in = a["w_in"][0].rearrange("(k p) n -> p k n", p=P)
        w_co = a["w_conf_out"][0].rearrange("(k p) n -> p k n", p=P)
        w_so = a["w_ssd_out"][0].rearrange("(k p) n -> p k n", p=P)
        w_o = a["w_o"][0].rearrange("(k p) n -> p k n", p=P)
        wg_e = a["w_exp_gate"][0].rearrange("e (k p) n -> p e k n", p=P)
        wu_e = a["w_exp_up"][0].rearrange("e (k p) n -> p e k n", p=P)
        wd_e = a["w_exp_down"][0].rearrange("e (f p) n -> p e f n", p=P)
        (y_p, y_s, ssm_p, sconv_p, cconv_p, ssm_s, sconv_s, cconv_s) = o
        s0_d = a["state_ssm"][0].rearrange("b (c h) q n -> (h q) c b n", h=2)
        s1_d = ssm_s[0].rearrange("b (c h) q n -> (h q) c b n", h=2)
        ssm_pd = ssm_p[0, 0].rearrange("(c h) q n -> (h q) c n", h=2)

        def bc(ap, *dims):
            shape = list(ap.shape)
            for d_ in dims:
                ap = ap.unsqueeze(len(shape))
                shape.append(d_)
            return ap.broadcast_to(shape)

        def vec(tile, at, n=KC):
            return vcol[:, tile * P + at:tile * P + at + n]

        B_ADA, G_MIX, G_FFN = vec(0, 0, 96), vec(0, 96), vec(0, 112)
        CONV_B, SSD_G, CONF_B = vec(1, 0, XC), vec(1, 24), vec(1, 40)
        LN_G, LN_B, FIN_G = vec(1, 56), vec(1, 72), vec(1, 88)
        SW0, CW0 = 2 * P, 3 * P

        def bl(ap):
            return ap.rearrange("p k (b l) -> p k b l", b=NB)

        VIEWS = {"gc": (w_in, GC0), "co": (w_co, 0), "z": (w_in, Z0), "xbc": (w_in, X0), "gs": (w_in, GS0),
                 "so": (w_so, 0), "wo": (w_o, 0)}
        ring0, ada0, rnd, au = {}, {}, 0, 0
        for name, steps, units in PHASES:
            ring0[name], ada0[name] = rnd, au
            rnd += steps * len(units) // RING
            au += steps * units.count("a")
        assert au == 6 * D // UC
        MOE_R = rnd

        def place(units, u):
            kind = units[u]
            n, many = units[:u].count(kind), units.count(kind)
            if kind == "p":
                return n, (2 * n + 1) % 4, (2 * n + 1) // 4, many // 2
            return n, 4 + n % 2, n // 2, many // 2

        def steps_of(eng, steps):
            return eng.Fori(0, steps) if steps > 1 else nullcontext(0)

        block = ctx.enter_context(nc.Block())

        @block.sync
        def _(sp):
            def unit(name, units, i, u):
                n, _, _, _ = place(units, u)
                if units[u] == "a":
                    src = w_ada[:, :, ds(i * (units.count("a") * UC) + (ada0[name] + n) * UC, UC)]
                elif name == "glu":
                    src = w_in[:, :, ds(i * (units.count("p") * UC // 2) + (GLU0 + (n % 2) * D + (n // 2) * UC), UC)]
                else:
                    w, c0 = VIEWS[name]
                    src = w[:, :, ds(i * (units.count("p") * UC) + (c0 + n * UC), UC)]
                sp.dma_start(ring[:, u % RING], src).then_inc(slot_loaded[u % RING], 16)

            def slot_used(name, units, i, u):
                _, b, k, per = place(units, u)
                sp.wait_ge(bank_ready[b], i * per + use(name, b, k))

            def stream(n, head=True, rest=True):
                name, steps, units = PHASES[n]
                if head:
                    for u in range(RING):
                        if n:
                            before, s_, u_ = PHASES[n - 1]
                            slot_used(before, u_, s_ - 1, len(u_) - RING + u)
                        unit(name, units, 0, u)
                if rest:
                    for u in range(RING, len(units)):
                        slot_used(name, units, 0, u - RING)
                        unit(name, units, 0, u)
                    if steps > 1:
                        with sp.Fori(1, steps) as i:
                            for u in range(len(units)):
                                if u < RING:
                                    _, b, k, per = place(units, len(units) - RING + u)
                                    sp.wait_ge(bank_ready[b], i * per + (use(name, b, k) - per))
                                else:
                                    slot_used(name, units, i, u - RING)
                                unit(name, units, i, u)

            sp.dma_start(xrow[:, 0:2], a["x_prompt"][0].rearrange("(q p) n -> p q n", p=P)).then_inc(S["x_loaded"], 16)
            sp.dma_start(xrow[0:NS, 2], a["x_sample"].rearrange("b l n -> (b l) n")).then_inc(S["x_loaded"], 16)
            sp.dma_start(crow[0:1], a["c_prompt"]).then_inc(S["c_loaded"], 16)
            sp.dma_start(crow[1:NSEQ], a["c_sample"]).then_inc(S["c_loaded"], 16)
            stream(0)
            stream(1)
            stream(2)
            sp.wait_ge(S["tail_rows"], 4)
            sp.dma_start(cconv_p[0, 0], tailrow[0:CK - 1]).then_inc(S["out_done"], 16)
            for b in range(NB):
                sp.dma_start(cconv_s[0, b, CK - 1 - NL:CK - 1],
                             tailrow[CK - 1 + NL * b:CK - 1 + NL * (b + 1)]).then_inc(S["tail_out"], 16)
            sp.wait_ge(S["vsamp_ready"], 1)
            sp.wait_ge(bank_free[7], use("tail", 7))
            sp.dma_start(wdt, w_in[:, :, DT0:DT0 + H], allow_slow_non_contiguous=True).then_inc(S["wdt_loaded"], 16)
            stream(3)
            stream(4, rest=False)
            sp.wait_ge(S["dta_ready"], 1)
            sp.dma_start(sstrow[0:NB * (SK - 1)], a["state_ssd_conv"][0].rearrange("b k n -> (b k) n")).then_inc(
                S["sst_loaded"], 16)
            stream(4, head=False)
            stream(5)
            sp.wait_ge(S["xrow_ready"], 6)
            sp.dma_start(sconv_p[0, 0], sstrow[0:SK - 1]).then_inc(S["xtail_out"], 16)
            sp.dma_start(sconv_s[0].rearrange("b k n -> (b k) n"),
                         sstrow[SK - 1:(SK - 1) * (1 + NB)]).then_inc(S["xtail_out"], 16)
            stream(6, rest=False)
            sp.wait_ge(S["xtail_out"], 32)
            sp.wait_ge(S["xbc_ready"], XC + 2)
            def load_state(par, chunk):
                sp.dma_start(s0[:, par], s0_d[:, chunk].rearrange("p c b n -> p (c b) n")).then_inc(s0_loaded[par], 16)

            for k in range(2):
                load_state(k, slice(k, k + 1))
            with sp.Fori(0, G - 1) as g:
                for k in range(4):
                    sp.wait_ge(st_out[k % 2], g * 32 + 16 * (k // 2 + 1))
                    load_state(k % 2, ds(g * 4 + (k + 2), 1))
            for k in range(2):
                sp.wait_ge(st_out[k], 32 * (G - 1) + 16)
                load_state(k, slice(KC - 2 + k, KC - 1 + k))
            stream(6, head=False)
            stream(7)
            stream(8)
            sp.wait_ge(S["merged"], KC)
            sp.wait_ge(bank_ready[3], use("wo", 3, 3))
            sp.dma_start(wr[:, :, 0:NG], a["w_group_router"][0].rearrange("(k p) n -> p k n", p=P),
                         allow_slow_non_contiguous=True).then_inc(S["wr_loaded"], 16)
            sp.dma_start(wr[:, :, NG:36], a["w_expert_router"][0].rearrange("(k p) n -> p k n", p=P),
                         allow_slow_non_contiguous=True).then_inc(S["wr_loaded"], 16)

            def expert_unit(e, kind, s):
                if kind < 2:
                    src = (wg_e, wu_e)[kind][:, ds(e, 1)].rearrange("p e k n -> p (e k) n")
                    dst = ring[:, s]
                else:
                    src = wd_e[:, ds(e, 1)].rearrange("p e f n -> p (e f) n")
                    dst = ring[:, s].rearrange("p k n -> p (k n)").rearrange("p (f n) -> p f n", f=2)
                sp.dma_start(dst, src).then_inc(slot_loaded[s], 16)

            used_by = [S["g_ready"], S["u_done"], S["ys_done"]]
            ahead = [0, 1, 1]
            for u in range(RING):
                slot_used("wo", "pppp", 1, u)
                expert_unit(u // 3, u % 3, u)
            for u in range(RING, 12):
                sp.wait_ge(used_by[(u - 4) % 3], (u - 4) // 3 + 1 + ahead[(u - 4) % 3])
                expert_unit(u // 3, u % 3, u % RING)
            with sp.Fori(1, 8) as i:
                for u in range(12):
                    sp.wait_ge(used_by[(u - 4) % 3], i * 4 + ((u - 4) // 3 + 1 + ahead[(u - 4) % 3]))
                    expert_unit(i * 4 + u // 3, u % 3, u % RING)

            sp.wait_ge(S["out_rows"], 12)
            sp.dma_start(y_p[0].rearrange("(q p) n -> p q n", p=P), yrow[:, 0:2]).then_inc(S["out_done"], 16)
            sp.dma_start(y_s.rearrange("b l n -> (b l) n"), yrow[0:NS, 2]).then_inc(S["out_done"], 16)
            sp.wait_ge(S["out_done"], 48)
            sp.wait_ge(S["tail_out"], 128)
            sp.wait_ge(S["state_copy"], 16)
            for par in range(2):
                sp.wait_ge(st_out[par], 128)
            sp.wait_ge(S["sf_out"], 16 * KC)

        @block.gpsimd
        def _(gp):
            gp.dma_start(cconv_s[0, :, 0:CK - 1 - NL], a["state_conf_conv"][0, :, NL:CK - 1]).then_inc(S["state_copy"], 16)
            gp.sem_inc(S["scaled"], 1)
            gp.sem_inc(S["sf_free"], 1)
            pool.mark(gp.memset(ones[:], 1.0))
            pool.mark(gp.memset(ident[:], 0.0))
            pool.link(gp, gp.memset(blk[:], 1.0))
            pool.mark(gp.affine_select(out=ident[:], in_=ident[:], compare_op=ALU.not_equal, fill=1.0, base=0,
                                       pattern=[[-1, P]], channel_multiplier=1))
            pool.mark(gp.affine_select(out=upper[:], in_=ones[:], compare_op=ALU.is_ge, fill=0.0, base=0,
                                       pattern=[[1, P]], channel_multiplier=-1))

            def by_seq(dst, src, inner):
                pool.link(gp, gp.affine_select(out=dst, in_=src, compare_op=ALU.is_ge, fill=0.0, base=0,
                                               pattern=[[-NL, NB], [0, inner]], channel_multiplier=1))
                pool.link(gp, gp.affine_select(out=dst, in_=dst, compare_op=ALU.is_ge, fill=0.0, base=NL - 1,
                                               pattern=[[NL, NB], [0, inner]], channel_multiplier=-1))

            blk3 = blk[:].rearrange("p (b l) -> p b l", b=NB)
            by_seq(blk3, blk3, NL)
            pool.link(gp, gp.tensor_copy(seqsel[:], blk3[:, :, 0]))
            pool.link(gp, gp.memset(fold, 0.0))
            for q in range(4):
                pool.link(gp, gp.affine_select(out=fold, in_=fold, compare_op=ALU.not_equal, fill=1.0, base=-32 * q,
                                               pattern=[[-1, NSEQ]], channel_multiplier=1))
            gp.tensor_tensor(ublk[:], blk[:], upper[0:NS, 0:NS], ALU.mult).then_inc(S["consts_ready"], 1)

            for j in range(2):
                gp.wait_ge(bank_free[j], use("glu", j, 2 * GLU_N - 1))
            gp.wait_ge(S["usamp_ready"], 1)
            acc_s = uvs[:, :, :]
            pool.link(gp, gp.tensor_copy(acc_s, bc(CONF_B, NS)))
            for k in range(CK):
                w = vcol[:, CW0 + k * KC:CW0 + (k + 1) * KC]
                pool.link(gp, gp.tensor_tensor(bl(tmpc), usamp[:, :, :, k:k + NL], bc(w, NB, NL), ALU.mult))
                pool.link(gp, gp.tensor_tensor(acc_s, acc_s, tmpc, ALU.add))
            gp.tensor_copy(vb[:, :, NP:T], acc_s).then_inc(S["vsamp_ready"], 1)

            gp.wait_ge(S["w_ready"], 1)
            gp.wait_ge(S["xtail_out"], 32)
            gp.wait_ge(S["xbc_ready"], XC + 2)
            with gp.Fori(0, G) as g:
                for k in range(4):
                    par = k % 2
                    gp.wait_ge(bank_ready[2], g * 4 + (use("ssd", 2) - 1 + k))
                    gp.tensor_copy(dax[0:NS].rearrange("p (h q) -> p h q", h=2),
                                   bc(dtA[0:NS, 2, ds(g * 8 + 2 * k, 2)], HD)).then_inc(S["dax_ready"], 1)
                    for h in range(2):
                        head = g * 8 + (2 * k + h)
                        if h == 0:
                            gp.wait_ge(bank_ready[6], g * 4 + (use("ssd", 6) - 1 + k))
                        else:
                            gp.wait_ge(bank_ready[5], g * 4 + (use("ssd", 5) + k))
                        gp.tensor_tensor(ud[:, 0:NP].rearrange("p (q i) -> p q i", q=2),
                                         upper[:].unsqueeze(1).broadcast_to([P, 2, P]),
                                         dtA[:, 0:2, ds(head, 1)].broadcast_to([P, 2, P]),
                                         ALU.mult).then_inc(S["ud_ready"], 1)
                        gp.tensor_tensor(ud[0:NS, NP:T], ublk[:],
                                         dtA[0:NS, 2, ds(head, 1)].broadcast_to([NS, NS]),
                                         ALU.mult).then_inc(S["ud_ready"], 1)
                    gp.wait_ge(bank_ready[1], g * 8 + (use("ssd", 1) + 2 * k))
                    gp.wait_ge(bank_free[2], g * 4 + (use("ssd", 2) + k))
                    gp.tensor_tensor(s0[:, par], s0[:, par], bc(dec, P), ALU.mult).then_inc(S["scaled"], 1)
                    gp.dma_start(ssm_pd[:, ds(g * 4 + k, 1)].rearrange("p c n -> p (c n)"), sfin).then_inc(S["sf_out"], 16)
                    for b in range(2):
                        gp.wait_ge(bank_free[b], g * 8 + (use("ssd", b) + 2 * k + 1))
                    gp.sem_inc(S["st_go"], 1)
                    gp.dma_start(s1_d[:, ds(g * 4 + k, 1)].rearrange("p c b n -> p (c b) n"), s0[:, par]).then_inc(
                        st_out[par], 16)
                    gp.wait_ge(S["sf_out"], g * 64 + 16 * (k + 1))
                    gp.sem_inc(S["sf_free"], 1)

            gp.wait_ge(S["merged"], KC)
            gp.wait_ge(bank_ready[3], use("wo", 3, 3))
            for par in range(2):
                gp.wait_ge(st_out[par], 128)
            gp.wait_ge(S["sf_out"], 16 * KC)
            gp.iota(iota_s, pattern=[[1, SLOTS]], base=0, channel_multiplier=0, allow_small_or_imprecise_dtypes=True)
            gp.iota(iota_e, pattern=[[1, NE]], base=0, channel_multiplier=0, allow_small_or_imprecise_dtypes=True)
            gp.affine_select(out=strict, in_=ones[:], compare_op=ALU.is_gt, fill=0.0, base=0,
                             pattern=[[1, P]], channel_multiplier=-1).then_inc(S["pooled"], 1)

        @block.scalar
        def _(ac):
            ac.wait_ge(S["vrow_zero"], 1)
            at = 0
            for tile, at, name, n in ((0, 0, "b_ada", 96), (0, 96, "norm_mix_g", KC), (0, 112, "norm_ffn_g", KC),
                                      (1, 0, "ssd_conv_b", XC), (1, 24, "ssd_norm_g", KC), (1, 40, "conf_conv_b", KC),
                                      (1, 56, "conf_ln_g", KC), (1, 72, "conf_ln_b", KC)):
                ac.dma_start(vrow[at:at + n, tile], a[name][0].rearrange("(r p) -> r p", p=P)).then_inc(S["v_loaded"], 16)
            ac.dma_start(vrow[88:104, 1], a["final_norm_g"].rearrange("(r p) -> r p", p=P)).then_inc(S["v_loaded"], 16)
            ac.dma_start(vrow[0:96, 2], a["ssd_conv_w"][0].rearrange("k (r p) -> (k r) p", p=P)).then_inc(S["v_loaded"], 16)
            cw = a["conf_conv_w"][0].rearrange("k (r p) -> (k r) p", p=P)
            for t_ in range(4):
                n = min(P, CK * KC - P * t_)
                ac.dma_start(vrow[0:n, 3 + t_], cw[P * t_:P * t_ + n]).then_inc(S["v_loaded"], 16)
            for half in range(2):
                ac.dma_start(cstrow[0:120, half],
                             a["state_conf_conv"][0, 4 * half:4 * half + 4].rearrange("b k n -> (b k) n")).then_inc(
                                 S["cst_loaded"], 16)
                ac.dma_start(dcol[HD * half:HD * half + HD, :],
                             a["ssd_d"][0].rearrange("(c h) -> h c", h=2)[half:half + 1].broadcast_to([HD, KC]),
                             allow_slow_non_contiguous=True).then_inc(S["small_loaded"], 16)
            ac.dma_start(rows_bc[:, 0], a["ssd_dt_bias"].broadcast_to([P, H])).then_inc(S["small_loaded"], 16)
            ac.dma_start(rows_bc[:, 1], a["ssd_a_log"].broadcast_to([P, H])).then_inc(S["small_loaded"], 16)
            ac.dma_start(rbias[:, 0:NG], a["b_group_router"].broadcast_to([P, NG])).then_inc(S["small_loaded"], 16)
            ac.dma_start(rbias[:, NG:36], a["b_expert_router"].broadcast_to([P, NE])).then_inc(S["small_loaded"], 16)

            ac.sem_inc(S["sil_ready"], 1)
            ac.sem_inc(S["xbc_ready"], 1)
            ac.wait_ge(bank_ready[4], use("c", 4))
            ac.activation(cT.rearrange("p k n -> p (k n)"), bank[4][:, 0:KC * NSEQ], ACT.Silu).then_inc(bank_free[4], 1)

            def walk(name, part, on_unit=None):
                steps, units = {n: (s_, u_) for n, s_, u_ in PHASES}[name]
                na = units.count("a")

                def modulation(i, n):
                    b = 6 + n % 2
                    ac.wait_ge(bank_ready[b], i * (na // 2) + use(name, b, n // 2))
                    for j in range(2):
                        c = i * (2 * na) + (2 * (ada0[name] + n) + j)
                        ins = ac.activation(mod[:, ds(c, 1)].rearrange("p k n -> p (k n)"),
                                            bank[b][:, NSEQ * j:NSEQ * (j + 1)], ACT.Identity, bias=vcol[:, ds(c, 1)])
                    ins.then_inc(bank_free[b], 1)

                with steps_of(ac, steps) as i:
                    owed = None
                    for u, kind in enumerate(units):
                        n, b, k, per = place(units, u)
                        if kind == "a":
                            ac.wait_ge(bank_ready[b], i * per + use(name, b, k))
                            ac.wait_ge(bank_ready[b + 2], i * per + (use(name, b + 2, k) - 1))
                            for q in range(4):
                                rows = slice(32 * q, 32 * q + NSEQ)
                                ins = ac.activation(part[rows, n % 2], bank[b][rows, 0:UC], ACT.Copy)
                            ins.then_inc(bank_free[b], 1)
                        elif on_unit:
                            on_unit(i, n)
                        if owed is not None:
                            modulation(i, owed)
                        owed = n if kind == "a" else None
                    if owed is not None:
                        modulation(i, owed)

            ac.wait_ge(S["part_zero"], 1)
            walk("ada", part_glu)

            def square(src, n):
                for q in range(4):
                    ac.activation(sq[:, 4 * q:4 * q + 4], src[:, 4 * q:4 * q + 4], ACT.Square).then_inc(
                        S["squares_ready"], 1)

            def root(n, src=stat, dst=rs):
                ac.wait_ge(S["mean_ready"], n)
                ac.activation(dst[:], src[:], ACT.Sqrt).then_inc(S["root_ready"], 1)

            for b in range(4):
                ac.wait_ge(bank_free[b], use("x", b, 3))
            ac.wait_ge(S["usamp_ready"], 1)
            square(xT, 0)
            root(1)

            def glu_gate(i, u):
                if u % 2 == 0:
                    return
                q = u // 2
                for j in range(2):
                    n = 2 * (q % 2) + j
                    ac.wait_ge(bank_ready[2 + j], i * 4 + (use("glu", 2 + j) + q))
                    ac.wait_ge(bank_free[j], i * 4 + (use("glu", j) - 2 + q))
                    ac.activation(sgl[:, n], bank[2 + j][:, 0:T], ACT.Sigmoid).then_inc(bank_free[2 + j], 1)

            def to_buffer(name, dst, func):
                def on_unit(i, u):
                    for j in range(2):
                        c = 2 * u + j
                        b = c % 4
                        ac.wait_ge(bank_ready[b], use(name, b, c // 4))
                        ac.activation(dst[:, c], bank[b][:, 0:T], func).then_inc(bank_free[b], 1)
                return on_unit

            walk("glu", part_glu, glu_gate)
            for q in range(4):
                ac.wait_ge(bank_ready[4 + q], use("tail", 4 + q))
                act.mark(ac.activation(tailrow[0:CK - 1 + NS, 512 * q:512 * q + 512], bank[4 + q][0:CK - 1 + NS], ACT.Copy))
                act.wait(ac)
                ac.sem_inc(bank_free[4 + q], 1)
                ac.sem_inc(S["tail_rows"], 1)
            ac.wait_ge(S["part_zero"], 2)
            walk("gc", part_mix, to_buffer("gc", gb, ACT.Sigmoid))
            ac.wait_ge(S["tail_out"], 128)
            ac.wait_ge(S["out_done"], 16)
            ac.wait_ge(S["centred"], 1)
            square(vb, 1)
            root(2)
            ac.wait_ge(S["v_ready"], 1)
            for c in range(KC):
                ac.activation(vb[:, c], vb[:, c], ACT.Silu, bias=LN_B[:, c:c + 1], scale=LN_G[:, c:c + 1]).then_inc(
                    S["vb_free"], 1)
            walk("co", part_mix)
            ac.wait_ge(S["small_loaded"], 96)
            ac.activation(rows_bc[:, 1], rows_bc[:, 1], ACT.Exp).then_inc(S["a_exp"], 1)
            ac.wait_ge(S["dt_abs"], 1)
            ac.activation(sp_e, sp_abs, ACT.Exp, scale=-1.0).then_inc(S["dt_exp"], 1)
            ac.wait_ge(S["one_plus"], 1)
            ac.activation(sp_ln, sp_u, ACT.Ln).then_inc(S["dt_log"], 1)
            walk("z", part_mix, to_buffer("z", zb, ACT.Silu))
            ac.wait_ge(S["w_arg"], 1)
            ac.activation(wend[:], wend[:], ACT.Exp).then_inc(S["w_exp"], 1)
            with ac.Fori(0, XBC_N) as i:
                for c in range(8):
                    ac.wait_ge(S["acc_ready"], i * 8 + c + 1)
                    ac.activation(xbcT[:, ds(i * 8 + c, 1), 0:NP].rearrange("p k n -> p (k n)"), acc[:, c % 2],
                                  ACT.Silu, bias=vcol[:, ds(P + i * 8 + c, 1)]).then_inc(S["xbc_ready"], 1)
            ac.wait_ge(S["xpad_ready"], 1)
            ac.activation(xbcT[:, :, NP:T], tmps, ACT.Silu).then_inc(S["xbc_ready"], 1)
            for n in range(6):
                b = 4 + n % 4
                ac.wait_ge(bank_ready[b], use("xtail", b, n // 4))
                act.mark(ac.activation(sstrow[0:(SK - 1) * (1 + NB), 512 * n:512 * n + 512],
                                       bank[b][0:(SK - 1) * (1 + NB)], ACT.Copy))
                act.wait(ac)
                ac.sem_inc(bank_free[b], 1)
                ac.sem_inc(S["xrow_ready"], 1)

            ac.wait_ge(S["xtail_out"], 32)
            ac.wait_ge(S["xbc_ready"], XC + 2)
            with ac.Fori(0, G) as g:
                ac.wait_ge(bank_ready[3], g * 2 + (use("ssd", 3) - 1))
                ac.activation(bst, xbcT[:, ds(KC + g, 1)].rearrange("p k n -> p (k n)"), ACT.Copy).then_inc(
                    S["bst_ready"], 1)
                for k in range(4):
                    ac.wait_ge(bank_ready[4], g * 4 + (use("ssd", 4) - 1 + k))
                    ac.activation(xst, xbcT[:, ds(g * 4 + k, 1)].rearrange("p k n -> p (k n)"), ACT.Copy).then_inc(
                        S["xst_ready"], 1)
                    ac.wait_ge(bank_ready[7], g * 4 + (use("ssd", 7) - 1 + k))
                    for b in range(2):
                        ac.wait_ge(bank_ready[b], g * 8 + (use("ssd", b) + 2 * k))
                        ac.activation(s0T[:, 4 * b:4 * b + 4], bank[b][:].rearrange("p (b n) -> p b n", b=4),
                                      ACT.Copy).then_inc(bank_free[b], 1)
                    for h in range(2):
                        ac.wait_ge(S["seg_ready"], g * 8 + (2 * k + h + 1))
                        ac.activation(mt[:, h, 0:NP], mt[:, h, 0:NP], ACT.Exp)
                        ac.activation(mt[0:NS, h, NP:T], mt[0:NS, h, NP:T], ACT.Exp).then_inc(S["exp_ready"], 1)
                        ac.activation(cs[:, h], bank[5 + h][:, P:T], ACT.Exp).then_inc(bank_free[5 + h], 1)
                    ac.wait_ge(bank_ready[2], g * 4 + (use("ssd", 2) + k))
                    ac.wait_ge(S["sf_free"], g * 4 + (k + 1))
                    ac.wait_ge(S["scaled"], g * 4 + k + 1)
                    ac.activation(s1T, bank[2][:, 0:P], ACT.Copy)
                    ac.activation(sfin, bank[2][:, P:2 * P], ACT.Copy)
                    ac.activation(dec, bank[2][:, 2 * P:2 * P + NB], ACT.Exp).then_inc(bank_free[2], 1)
            ac.wait_ge(S["y_done"], KC)
            for q in range(4):
                ac.activation(vb[:, 4 * q:4 * q + 4], zb[:, 4 * q:4 * q + 4], ACT.Square).then_inc(S["gsq_ready"], 1)
            for q in range(4):
                ac.wait_ge(S["gmean_ready"], q + 1)
                ac.activation(grs[:, q], grs[:, q], ACT.Sqrt).then_inc(S["groot_ready"], 1)
            for q in range(4):
                ac.wait_ge(bank_ready[4 + q], use("gn", 4 + q))
            ac.wait_ge(S["part_zero"], 3)
            walk("gs", part_mix, to_buffer("gs", vb, ACT.Sigmoid))
            walk("so", part_mix)
            ac.wait_ge(S["x_mid"], KC)
            ac.wait_ge(S["merged"], KC)
            square(xT, 2)
            root(3)
            ac.wait_ge(S["e_arg"], 1)
            ac.activation(lg[:, :, 0:NG], lg[:, :, 0:NG], ACT.Exp).then_inc(S["gexp"], 1)
            ac.wait_ge(S["e_arg"], 2)
            ac.activation(sel[:], sel[:], ACT.Exp).then_inc(S["eexp"], 1)
            for c in range(KC):
                ac.wait_ge(bank_ready[4 + c % 2], use("gather", 4 + c % 2, c // 2))
                if c >= 2:
                    ac.wait_ge(bank_ready[2 * (c % 2) + 1], use("gather", 2 * (c % 2) + 1, c // 2 - 1))
                ac.activation(htok[:, c % 2, 0:2 * P], bank[4 + c % 2][:, 0:2 * P], ACT.Copy)
                ac.activation(htok[0:NS, c % 2, 2 * P:3 * P], bank[4 + c % 2][0:NS, 2 * P:3 * P], ACT.Copy).then_inc(
                    bank_free[4 + c % 2], 1)
            with ac.Fori(0, 8) as i:
                for k in range(4):
                    ac.wait_ge(S["g_ready"], i * 4 + (k + 1))
                    ac.wait_ge(S["hid_ready"], i * 4 + (k + 1))
                    n_pairs = ac.value_load(meta_i[0:1, 0, ds(i * 4 + k, 1)], min_val=0, max_val=T)
                    with ac.If(n_pairs > WIN):
                        ac.activation(sil[:, 0], bank[4][:, 0:T], ACT.Silu)
                        ac.activation(sil[:, 1], bank[6][:, 0:T], ACT.Silu).then_inc(S["sil_ready"], 1)
                    with ac.Else():
                        ac.activation(sil[:, :, 0:WIN], bank[4][:, 0:2 * WIN].rearrange("p (f w) -> p f w", f=2),
                                      ACT.Silu).then_inc(S["sil_ready"], 1)
            for c in range(KC):
                for b in range(2):
                    n = (3, 2)[b]
                    bb = 4 + 2 * (c % 2) + b
                    ac.wait_ge(bank_ready[bb], use("unsort", bb, c // 2))
                    if c >= 2:
                        ac.wait_ge(bank_ready[(c - 2) % 4], use("unsort", (c - 2) % 4, (c - 2) // 4))
                    if b == 0:
                        ac.activation(ytok[:, c % 2, 0:3 * P], bank[bb][:, 0:3 * P], ACT.Copy).then_inc(bank_free[bb], 1)
                    else:
                        ac.activation(ytok[:, c % 2, 3 * P:4 * P], bank[bb][:, 0:P], ACT.Copy)
                        ac.activation(ytok[0:HD, c % 2, 4 * P:5 * P], bank[bb][0:HD, P:2 * P], ACT.Copy).then_inc(
                            bank_free[bb], 1)
            ac.wait_ge(S["moe_ready"], KC)
            for q in range(4):
                ac.activation(hT[:, 4 * q:4 * q + 4], xT[:, 4 * q:4 * q + 4], ACT.Square).then_inc(S["squares_ready"], 1)
            root(4)
            for n in range(12):
                b = 4 + n % 4
                rows, q, c4 = (P, P, NS)[n // 4], n // 4, n % 4
                ac.wait_ge(bank_ready[b], use("y", b, n // 4))
                act.mark(ac.activation(yrow[0:rows, q, 512 * c4:512 * c4 + 512], bank[b][0:rows], ACT.Copy))
                act.wait(ac)
                ac.sem_inc(bank_free[b], 1)
                ac.sem_inc(S["out_rows"], 1)

        @block.tensor
        def _(pe):
            def fill(name, b, k=0):
                pe.wait_ge(bank_free[b], use(name, b, k) - 1)

            def project(name, rhs=None):
                steps, units = {n: (s_, u_) for n, s_, u_ in PHASES}[name]

                def fold_sums(i, n):
                    b = 6 + n % 2
                    per = units.count("a") // 2
                    pe.wait_ge(bank_free[b - 2], i * per + use(name, b - 2, n // 2))
                    pe.wait_ge(bank_free[b], i * per + (use(name, b, n // 2) - 1))
                    part = part_glu if name in ("ada", "glu") else part_mix
                    for j in range(2):
                        mm = nc.tensor.matmul(bank[b][:, NSEQ * j:NSEQ * (j + 1)], part[:, n % 2, j * P:(j + 1) * P],
                                              fold, start=True, stop=True)
                    mm.then_inc(bank_ready[b], 1)

                with steps_of(pe, steps) as i:
                    owed = None
                    for u, kind in enumerate(units):
                        s, r = u % RING, u // RING
                        n, last, k, per = place(units, u)
                        pe.wait_ge(slot_loaded[s], i * (16 * len(units) // RING) + 16 * (ring0[name] + r + 1))
                        if kind == "p":
                            for j in range(2):
                                c = 2 * n + j
                                b = c % 4
                                pe.wait_ge(bank_free[b], i * per + (use(name, b, c // 4) - 1))
                                for kk in range(KC):
                                    mm = nc.tensor.matmul(bank[b][:, 0:T], ring[:, s, kk, j * P:(j + 1) * P], rhs[:, kk],
                                                          start=(kk == 0), stop=(kk == KC - 1))
                                mm.then_inc(bank_ready[b], 1)
                        else:
                            pe.wait_ge(bank_free[last], i * per + (use(name, last, k) - 1))
                            for kk in range(KC):
                                q = kk % 4
                                mm = nc.tensor.matmul(bank[last][32 * q:32 * q + NSEQ, 0:UC], cT[:, kk], ring[:, s, kk],
                                                      start=(kk < 4), stop=(kk >= KC - 4))
                            mm.then_inc(bank_ready[last], 1)
                        if owed is not None:
                            fold_sums(i, owed)
                        owed = n if kind == "a" else None
                    if owed is not None:
                        fold_sums(i, owed)

            def ones_sum(name, src, b, chunks, k=0):
                fill(name, b, k)
                for n, c in enumerate(chunks):
                    mm = nc.tensor.matmul(bank[b][:, 0:T], ones[:], src[:, c], start=(n == 0), stop=(n == len(chunks) - 1))
                mm.then_inc(bank_ready[b], 1)

            pe.sem_inc(S["u_done"], 1)
            pe.wait_ge(S["consts_ready"], 1)
            pe.wait_ge(S["x_loaded"], 32)
            for c in range(KC):
                b = c % 4
                fill("x", b, c // 4)
                for q, (t0, rows) in enumerate(TOK):
                    mm = nc.tensor.transpose(bank[b][:, t0:t0 + rows], xrow[0:rows, q, c * P:(c + 1) * P],
                                             ident[0:rows, 0:rows])
                mm.then_inc(bank_ready[b], 1)
            pe.wait_ge(S["c_loaded"], 32)
            fill("c", 4)
            for c in range(KC):
                mm = nc.tensor.transpose(bank[4][:, NSEQ * c:NSEQ * (c + 1)], crow[0:NSEQ, c * P:(c + 1) * P],
                                         ident[0:NSEQ, 0:NSEQ])
            mm.then_inc(bank_ready[4], 1)
            pe.wait_ge(S["v_loaded"], 14 * 16)
            for b, tiles in ((5, range(4)), (6, range(4, 7))):
                fill("vec", b)
                for n, t_ in enumerate(tiles):
                    mm = nc.tensor.transpose(bank[b][:, n * P:(n + 1) * P], vrow[:, t_], ident[:])
                mm.then_inc(bank_ready[b], 1)
            pe.wait_ge(S["cst_loaded"], 32)
            for c in range(KC):
                b = 4 + c % 4
                fill("cst", b, c // 4)
                for half in range(2):
                    mm = nc.tensor.transpose(bank[b][:, 120 * half:120 * half + 120],
                                             cstrow[0:120, half, c * P:(c + 1) * P], ident[0:120, 0:120])
                mm.then_inc(bank_ready[b], 1)
            pe.wait_ge(bank_free[4], use("c", 4))
            project("ada")
            pe.wait_ge(S["squares_ready"], 4)
            ones_sum("n1", sq, 4, range(KC))
            pe.wait_ge(S["h_ready"], 1)
            project("glu", hT)
            for j in range(2):
                pe.wait_ge(bank_free[j], use("glu", j, 2 * GLU_N - 1))
            for q in range(4):
                fill("tail", 4 + q)
                for n in range(4):
                    mm = nc.tensor.transpose(bank[4 + q][0:CK - 1 + NS, n * P:(n + 1) * P], utail[:, 4 * q + n], ident[:])
                mm.then_inc(bank_ready[4 + q], 1)
            project("gc", hT)
            pe.wait_ge(S["conv_ready"], 1)
            pe.wait_ge(S["vsamp_ready"], 1)
            ones_sum("ln", vb, 4, range(KC))
            pe.wait_ge(S["squares_ready"], 8)
            ones_sum("ln", sq, 5, range(KC))
            pe.wait_ge(S["vb_free"], KC)
            project("co", vb)
            pe.wait_ge(S["wdt_loaded"], 16)
            fill("dt", 6)
            for q, (t0, rows) in enumerate(TOK):
                for k in range(KC):
                    mm = nc.tensor.matmul(bank[6][0:rows, H * q:H * (q + 1)], hT[:, k, t0:t0 + rows], wdt[:, k],
                                          start=(k == 0), stop=(k == KC - 1))
            mm.then_inc(bank_ready[6], 1)
            project("z", hT)
            pe.wait_ge(S["dta_ready"], 1)
            fill("cum", 7)
            for q, (lhs, rows) in enumerate(((upper[:], P), (upper[:], P), (ublk[:], NS))):
                nc.tensor.matmul(bank[7][0:rows, H * q:H * (q + 1)], lhs, dtA[0:rows, q], start=True, stop=True)
            for q, (lhs, rows) in enumerate(((ones[:], P), (ones[:], P), (blk[:], NS))):
                mm = nc.tensor.matmul(bank[7][0:rows, H * (3 + q):H * (4 + q)], lhs, dtA[0:rows, q], start=True, stop=True)
            mm.then_inc(bank_ready[7], 1)
            pe.wait_ge(S["sst_loaded"], 16)
            R = NB * (SK - 1)
            for half in range(2):
                fill("sst", 4 + half)
                for n in range(12):
                    c = 12 * half + n
                    mm = nc.tensor.transpose(bank[4 + half][:, R * n:R * (n + 1)], sstrow[0:R, c * P:(c + 1) * P],
                                             ident[0:R, 0:R])
                mm.then_inc(bank_ready[4 + half], 1)
            project("xbc", hT)
            pe.wait_ge(S["xtail_ready"], 1)
            R = (SK - 1) * (1 + NB)
            for n in range(6):
                b = 4 + n % 4
                fill("xtail", b, n // 4)
                for j in range(4):
                    mm = nc.tensor.transpose(bank[b][0:R, j * P:(j + 1) * P], xtail[:, 4 * n + j], ident[:])
                mm.then_inc(bank_ready[b], 1)

            pe.wait_ge(S["w_ready"], 1)
            pe.wait_ge(S["xbc_ready"], XC + 2)
            with pe.Fori(0, G) as g:
                pe.wait_ge(S["bst_ready"], g + 1)
                pe.wait_ge(bank_free[3], g * 2 + (use("ssd", 3) - 1))
                for q, (t0, rows) in enumerate(TOK):
                    mm = nc.tensor.transpose(bank[3][0:rows, q * P:(q + 1) * P], bst[:, t0:t0 + rows], ident[:])
                mm.then_inc(bank_ready[3], 1)
                pe.wait_ge(bank_free[3], g * 2 + use("ssd", 3))
                for q, (t0, rows) in enumerate(TOK):
                    mm = nc.tensor.matmul(bank[3][0:rows, q * P:q * P + rows], bst[:, t0:t0 + rows],
                                          xbcT[:, ds(KC + G + g, 1), t0:t0 + rows].rearrange("p k n -> p (k n)"),
                                          start=True, stop=True)
                mm.then_inc(bank_ready[3], 1)
                for k in range(4):
                    par = k % 2
                    pe.wait_ge(S["xst_ready"], g * 4 + k + 1)
                    pe.wait_ge(bank_free[4], g * 4 + (use("ssd", 4) - 1 + k))
                    for q, (t0, rows) in enumerate(TOK):
                        mm = nc.tensor.transpose(bank[4][0:rows, q * P:(q + 1) * P], xst[:, t0:t0 + rows], ident[:])
                    mm.then_inc(bank_ready[4], 1)
                    pe.wait_ge(s0_loaded[par], g * 32 + (16 * (k // 2) + 16))
                    for b in range(2):
                        pe.wait_ge(bank_free[b], g * 8 + (use("ssd", b) - 1 + 2 * k))
                        for n in range(4):
                            mm = nc.tensor.transpose(bank[b][:, n * P:(n + 1) * P], s0[:, par, 4 * b + n], ident[:])
                        mm.then_inc(bank_ready[b], 1)
                    for h in range(2):
                        pe.wait_ge(S["ud_ready"], g * 16 + 4 * k + 2 * h + 2)
                        pe.wait_ge(bank_free[5 + h], g * 4 + (use("ssd", 5 + h) - 1 + k))
                        nc.tensor.matmul(bank[5 + h][:, 0:NP], ones[:], ud[:, 0:NP], start=True, stop=True)
                        nc.tensor.matmul(bank[5 + h][:, NP:T], ones[0:NS, :], ud[0:NS, NP:T],
                                         start=True, stop=True).then_inc(bank_ready[5 + h], 1)
                    pe.wait_ge(S["xw_ready"], g * 4 + k + 1)
                    pe.wait_ge(S["dax_ready"], g * 4 + k + 1)
                    pe.wait_ge(bank_free[2], g * 4 + (use("ssd", 2) - 1 + k))
                    nc.tensor.matmul(bank[2][:, 0:P], btok[:, 0], xw[:, 0], start=True, stop=True)
                    nc.tensor.matmul(bank[2][:, P:2 * P], xw[:, 1], btok[:, 0], start=True, stop=False)
                    nc.tensor.matmul(bank[2][:, P:2 * P], xw[:, 2], btok[:, 1], start=False, stop=True)
                    nc.tensor.matmul(bank[2][:, 2 * P:2 * P + NB], dax[0:NS], seqsel[:], start=True,
                                     stop=True).then_inc(bank_ready[2], 1)
                    pe.wait_ge(S["bexp_ready"], g + 1)
                    for b in range(2):
                        pe.wait_ge(bank_free[b], g * 8 + (use("ssd", b) + 2 * k))
                        nc.tensor.matmul(bank[b][:], xw[0:NS, 3], bexp[0:NS, 4 * b:4 * b + 4], start=True,
                                         stop=True).then_inc(bank_ready[b], 1)
                    pe.wait_ge(S["m_ready"], g * 8 + 2 * k + 2)
                    pe.wait_ge(bank_free[2], g * 4 + (use("ssd", 2) + k))
                    pe.wait_ge(bank_free[7], g * 4 + (use("ssd", 7) - 1 + k))
                    for h in range(2):
                        hc = slice(HD * h, HD * (h + 1))
                        y = bank[7][hc]
                        nc.tensor.matmul(y[:, 0:P], xtok[:, 0, hc], mt[:, h, 0:P], start=True, stop=True)
                        nc.tensor.matmul(y[:, P:NP], xtok[:, 1, hc], mt[:, h, P:NP], start=True, stop=False)
                        nc.tensor.matmul(y[:, P:NP], s1T[:, hc], cs[:, h, 0:P], start=False, stop=True)
                        nc.tensor.matmul(y[:, NP:T], xtok[0:NS, 2, hc], mt[0:NS, h, NP:T], start=True, stop=True)
                        for b in range(NB):
                            mm = nc.tensor.matmul(y[:, NP + NL * b:NP + NL * (b + 1)], s0T[:, b, hc],
                                                  cs[:, h, P + NL * b:P + NL * (b + 1)], start=False,
                                                  stop=True, skip_group_check=True)
                    mm.then_inc(bank_ready[7], 1)
            for q in range(G):
                pe.wait_ge(S["gsq_ready"], q + 1)
                ones_sum("gn", vb, 4 + q, range(4 * q, 4 * q + 4))
            project("gs", hT)
            pe.wait_ge(S["y_ready"], 1)
            project("so", zb)
            pe.wait_ge(S["merged"], KC)
            project("wo", gb)
            pe.wait_ge(S["squares_ready"], 12)
            ones_sum("n2", sq, 4, range(KC))
            pe.wait_ge(S["h_ready"], 2)
            pe.wait_ge(S["wr_loaded"], 32)
            fill("route", 5)
            for q, (t0, rows) in enumerate(TOK):
                for k in range(KC):
                    mm = nc.tensor.matmul(bank[5][0:rows, 36 * q:36 * (q + 1)], hT[:, k, t0:t0 + rows], wr[:, k],
                                          start=(k == 0), stop=(k == KC - 1))
            mm.then_inc(bank_ready[5], 1)
            pe.wait_ge(S["cnt_ready"], 1)
            pe.wait_ge(S["pooled"], 1)
            fill("route", 6)
            for q, (t0, rows) in enumerate(TOK):
                mm = nc.tensor.matmul(bank[6][0:NE, 0:1], chosen[0:rows, q], ones[0:rows, 0:1], start=(q == 0), stop=(q == 2))
            mm.then_inc(bank_ready[6], 1)
            pe.wait_ge(S["cnt_ready"], 2)
            fill("route", 7)
            for q, (t0, rows) in enumerate(TOK):
                out = bank[7][0:rows, NE * q:NE * (q + 1)]
                nc.tensor.matmul(out, cntb[0:NE, 0:rows], strict[0:NE, 0:NE], start=True, stop=False)
                for q2 in range(q):
                    nc.tensor.matmul(out, ones[:, 0:rows], chosen[:, q2], start=False, stop=False)
                nc.tensor.matmul(out, strict[0:rows, 0:rows], chosen[0:rows, q], start=False, stop=True)
            nc.tensor.matmul(bank[7][:, 96:128], cntb[0:NE], strict[0:NE, 0:NE], start=True, stop=True)
            nc.tensor.matmul(bank[7][:, 128:160], cntb[0:NE], ident[0:NE, 0:NE], start=True, stop=True).then_inc(
                bank_ready[7], 1)
            pe.wait_ge(S["sort_ready"], 1)
            for b in range(4):
                fill("gates", b)
                src = (gt, et)[b // 2]
                for q, (t0, rows) in enumerate(TOK):
                    mm = nc.tensor.matmul(bank[b][:, 0:T], ones[0:rows, :], src[0:rows, q, T * (b % 2):T * (b % 2 + 1)],
                                          start=(q == 0), stop=(q == 2))
                mm.then_inc(bank_ready[b], 1)

            def to_rows(c):
                b = 4 + c % 2
                fill("gather", b, c // 2)
                for q, (t0, rows) in enumerate(TOK):
                    mm = nc.tensor.transpose(bank[b][0:rows, q * P:(q + 1) * P], hT[:, c, t0:t0 + rows], ident[:])
                mm.then_inc(bank_ready[b], 1)

            to_rows(0)
            for c in range(KC):
                if c + 1 < KC:
                    to_rows(c + 1)
                pe.wait_ge(bank_free[4 + c % 2], use("gather", 4 + c % 2, c // 2))
                for half in range(2):
                    b = 2 * (c % 2) + half
                    fill("gather", b, c // 2)
                    for q, (t0, rows) in enumerate(TOK):
                        mm = nc.tensor.matmul(bank[b][:, 0:T], htok[0:rows, c % 2, q * P:(q + 1) * P],
                                              pm[0:rows, q, T * half:T * (half + 1)], start=(q == 0), stop=(q == 2))
                    mm.then_inc(bank_ready[b], 1)

            for b in range(4):
                fill("unsort", b)
            for b in (4, 5):
                fill("pt", b)
            pe.wait_ge(S["meta_ready"], 1)
            with pe.Fori(0, 8) as i:
                for k in range(4):
                    u = 3 * k
                    slots = [(u + n) % RING for n in range(3)]
                    landed = [i * 48 + (MOE_R + (u + n) // RING + 1) * 16 for n in range(3)]
                    n_pairs = pe.value_load(meta_i[0:1, 0, ds(i * 4 + k, 1)], min_val=0, max_val=T)
                    w_gate, w_up = ring[:, slots[0]], ring[:, slots[1]]
                    w_down = ring[:, slots[2]].rearrange("p k n -> p (k n)").rearrange("p (f n) -> p f n", f=2)
                    pe.wait_ge(slot_loaded[slots[0]], landed[0])
                    pe.wait_ge(S["win_ready"], i * 4 + (k + 1))
                    pe.wait_ge(S["sil_ready"], i * 4 + (k + 1))
                    with pe.If(n_pairs > WIN):
                        w0 = pe.value_load(meta_i[0:1, 2, ds(i * 4 + k, 1)], min_val=0, max_val=SLOTS - T)
                        for n, (w, done, gone) in enumerate(((w_gate, "g_ready", "sil_ready"), (w_up, "u_done", "hid_ready"))):
                            if n:
                                pe.wait_ge(slot_loaded[slots[1]], landed[1])
                                pe.wait_ge(S["hid_ready"], i * 4 + (k + 1))
                            for f in range(2):
                                for kk in range(KC):
                                    mm = nc.tensor.matmul(bank[4 + n + 2 * f][:, 0:T], w[:, kk, f * P:(f + 1) * P],
                                                          hs[:, kk, ds(w0, T)], start=(kk == 0), stop=(kk == KC - 1))
                            mm.then_inc(S[done], 1)
                        pe.wait_ge(slot_loaded[slots[2]], landed[2])
                        pe.wait_ge(S["hid_ready"], i * 4 + (k + 2))
                        pe.wait_ge(S["ys_done"], i * 4 + (k + 1))
                        for c in range(KC):
                            if c >= 4:
                                pe.wait_ge(S["wide_free"], i * 64 + (16 * k + c - 3))
                            for f in range(2):
                                mm = nc.tensor.matmul(bank[c % 4][:, 0:T], w_down[:, f, c * P:(c + 1) * P], hid[:, f],
                                                      start=(f == 0), stop=(f == 1))
                            mm.then_inc(S["wide_ready"], 1)
                        pe.sem_inc(S["d_ready"], 1)
                    with pe.Else():
                        for n, (w, done) in enumerate(((w_gate, "g_ready"), (w_up, "u_done"))):
                            if n:
                                pe.wait_ge(slot_loaded[slots[1]], landed[1])
                                pe.wait_ge(S["hid_ready"], i * 4 + (k + 1))
                            for f in range(2):
                                for kk in range(KC):
                                    mm = nc.tensor.matmul(bank[4 + n][:, f * WIN:(f + 1) * WIN], w[:, kk, f * P:(f + 1) * P],
                                                          hwin[:, k % 2, kk], start=(kk == 0), stop=(kk == KC - 1))
                            mm.then_inc(S[done], 1)
                        pe.wait_ge(slot_loaded[slots[2]], landed[2])
                        pe.wait_ge(S["hid_ready"], i * 4 + (k + 2))
                        pe.wait_ge(S["ys_done"], i * 4 + (k + 1))
                        for c in range(KC):
                            for f in range(2):
                                mm = nc.tensor.matmul(bank[c // 4][:, (c % 4) * WIN:(c % 4 + 1) * WIN],
                                                      w_down[:, f, c * P:(c + 1) * P], hid[:, f, 0:WIN],
                                                      start=(f == 0), stop=(f == 1))
                        mm.then_inc(S["d_ready"], 1)
                        pe.sem_inc(S["wide_ready"], 16)

            pe.wait_ge(S["ys_done"], NE + 1)
            PT = [(P * j, min(P, SLOTS - P * j)) for j in range(5)]
            for j, (s_, n) in enumerate(PT):
                b = 4 + j % 2
                fill("pt", b, j // 2)
                for q, (t0, rows) in enumerate(TOK):
                    mm = nc.tensor.transpose(bank[b][0:n, t0:t0 + rows], pm[0:rows, q, s_:s_ + n], ident[0:rows, 0:rows])
                mm.then_inc(bank_ready[b], 1)

            def y_rows(c):
                for half, tiles in ((0, PT[0:3]), (1, PT[3:5])):
                    b = 4 + 2 * (c % 2) + half
                    fill("unsort", b, c // 2)
                    for m, (s_, n) in enumerate(tiles):
                        mm = nc.tensor.transpose(bank[b][0:n, m * P:(m + 1) * P], ys[:, c, s_:s_ + n], ident[:])
                    mm.then_inc(bank_ready[b], 1)

            y_rows(0)
            pe.wait_ge(bank_free[4], use("pt", 4, 2))
            pe.wait_ge(bank_free[5], use("pt", 5, 1))
            for c in range(KC):
                if c + 1 < KC:
                    y_rows(c + 1)
                for half in range(2):
                    b = 4 + 2 * (c % 2) + half
                    pe.wait_ge(bank_free[b], use("unsort", b, c // 2))
                fill("unsort", c % 4, c // 4)
                for j, (s_, n) in enumerate(PT):
                    mm = nc.tensor.matmul(bank[c % 4][:, 0:T], ytok[0:n, c % 2, j * P:(j + 1) * P], pt[0:n, j],
                                          start=(j == 0), stop=(j == 4))
                mm.then_inc(bank_ready[c % 4], 1)
            pe.wait_ge(S["squares_ready"], 16)
            ones_sum("n3", hT, 4, range(KC))
            pe.wait_ge(S["y_fin"], KC)
            for n in range(12):
                q, c4, b = n // 4, n % 4, 4 + n % 4
                t0, rows = TOK[q]
                fill("y", b, n // 4)
                for j in range(4):
                    mm = nc.tensor.transpose(bank[b][0:rows, j * P:(j + 1) * P], xT[:, 4 * c4 + j, t0:t0 + rows], ident[:])
                mm.then_inc(bank_ready[b], 1)

        @block.vector
        def _(ve):
            def flat(ap):
                return ap.rearrange("p k n -> p (k n)")

            def take(name, b, k=0):
                ve.wait_ge(bank_ready[b], use(name, b, k))

            ve.sem_inc(S["hid_ready"], 1)
            ve.sem_inc(S["ys_done"], 1)
            dve.mark(ve.memset(dt_tok[:], 0.0))
            dve.mark(ve.memset(wend[:], 0.0))
            ve.memset(vrow, 0.0).then_inc(S["vrow_zero"], 1)
            for c in range(KC):
                b = c % 4
                take("x", b, c // 4)
                ve.tensor_copy(xT[:, c], bank[b][:, 0:T]).then_inc(bank_free[b], 1)
            take("vec", 5)
            ve.tensor_copy(vcol[:, 0:512], bank[5][:]).then_inc(bank_free[5], 1)
            take("vec", 6)
            ve.tensor_copy(vcol[:, 512:896], bank[6][:, 0:384]).then_inc(bank_free[6], 1)
            for c in range(KC):
                b = 4 + c % 4
                take("cst", b, c // 4)
                ve.tensor_copy(usamp[:, c, :, 0:CK - 1],
                               bank[b][:, 0:240].rearrange("p (b l) -> p b l", b=NB)).then_inc(bank_free[b], 1)
            ve.wait_ge(bank_free[7], use("cst", 7, 3))
            ve.sem_inc(S["usamp_ready"], 1)
            dve.mark(ve.memset(upad[:, :, 0:CK - 1], 0.0))
            dve.link(ve, ve.memset(part_glu, 0.0))
            ve.sem_inc(S["part_zero"], 1)

            def inv_rms(name, b, n, width):
                take(name, b)
                ve.tensor_scalar(stat[:], bank[b][:, 0:T], 1.0 / width, EPS, ALU.mult, ALU.add).then_inc(S["mean_ready"], 1)
                ve.wait_ge(S["root_ready"], n)
                ve.sem_inc(bank_free[b], 1)
                dve.link(ve, ve.reciprocal(rs[:], rs[:]))

            def modulate(gvec, shift, scale):
                dve.link(ve, ve.scalar_tensor_tensor(out=scaleA[:], in0=mod[:, scale:scale + KC], scalar=1.0,
                                                     in1=bc(gvec, NSEQ), op0=ALU.add, op1=ALU.mult))
                dve.link(ve, ve.tensor_tensor(hT[:], xT[:], rs[:].unsqueeze(1).broadcast_to([P, KC, T]), ALU.mult))
                hs_ = bl(hT[:, :, NP:T])
                dve.link(ve, ve.tensor_tensor(hs_, hs_, bc(scaleA[:, :, 1:NSEQ], NL), ALU.mult))
                dve.mark(ve.tensor_tensor(hs_, hs_, bc(mod[:, shift:shift + KC, 1:NSEQ], NL), ALU.add))
                with ve.Fori(0, 4) as i:
                    with dve.loop(i, 4, 4):
                        for n in range(4):
                            c = i * 4 + n
                            dve.mark(ve.tensor_scalar(flat(hT[:, ds(c, 1), 0:NP]), flat(hT[:, ds(c, 1), 0:NP]),
                                                      scaleA[:, ds(c, 1), 0:1], mod[:, ds(c + shift, 1), 0:1],
                                                      ALU.mult, ALU.add))
                dve.wait(ve)
                ve.sem_inc(S["h_ready"], 1)

            inv_rms("n1", 4, 1, D)
            for b in (6, 7):
                ve.wait_ge(bank_free[b], use("ada", b, 9))
            modulate(G_MIX, 0, KC)

            cacc = [stat, rs]
            with ve.Fori(0, GLU_N) as i:
                with dve.loop(i, GLU_N, 2 * (2 + 2 * CK)):
                    for q in range(2):
                        for j in range(2):
                            n, c = 2 * q + j, i * 4 + (2 * q + j)
                            ve.wait_ge(bank_ready[j], i * 2 + (use("glu", j) + q))
                            ve.wait_ge(bank_free[2 + j], i * 2 + (use("glu", 2 + j) + q))
                            dve.mark(ve.tensor_tensor(upad[:, n, CK - 1:], bank[j][:, 0:NP], sgl[:, n, 0:NP], ALU.mult))
                            ve.tensor_tensor(flat(utail[:, ds(c, 1), 0:CK - 1]), bank[j][:, NP - CK + 1:NP],
                                             sgl[:, n, NP - CK + 1:NP], ALU.mult)
                            ve.tensor_tensor(flat(utail[:, ds(c, 1), CK - 1:]), bank[j][:, NP:T], sgl[:, n, NP:T], ALU.mult)
                            ve.tensor_tensor(usamp[:, ds(c, 1), :, CK - 1:].rearrange("p k b l -> p (k b) l"),
                                             bank[j][:, NP:T].rearrange("p (b l) -> p b l", b=NB),
                                             sgl[:, n, NP:T].rearrange("p (b l) -> p b l", b=NB),
                                             ALU.mult).then_inc(bank_free[j], 1)
                        for k in range(CK):
                            for j in range(2):
                                n, c = 2 * q + j, i * 4 + (2 * q + j)
                                tap = vcol[:, ds(c + (CW0 + k * KC), 1)]
                                u = upad[:, n, k:k + NP]
                                dve.wait(ve, back=1)
                                if k == 0:
                                    ins = ve.tensor_scalar(cacc[j][:, 0:NP], u, tap, vcol[:, ds(c + (P + 40), 1)],
                                                           ALU.mult, ALU.add)
                                else:
                                    out = cacc[j][:, 0:NP] if k < CK - 1 else flat(vb[:, ds(c, 1), 0:NP])
                                    ins = ve.scalar_tensor_tensor(out=out, in0=u, scalar=tap, in1=cacc[j][:, 0:NP],
                                                                  op0=ALU.mult, op1=ALU.add)
                                dve.mark(ins)
            dve.wait(ve)
            ve.sem_inc(S["conv_ready"], 1)

            take("tail", 7)
            dve.link(ve, ve.memset(part_mix, 0.0))
            ve.sem_inc(S["part_zero"], 1)
            take("ln", 4)
            dve.link(ve, ve.tensor_scalar(stat[:], bank[4][:, 0:T], 1.0 / D, None, ALU.mult))
            ve.sem_inc(bank_free[4], 1)
            ve.wait_ge(S["vsamp_ready"], 1)
            ve.tensor_tensor(vb, vb, stat[:].unsqueeze(1).broadcast_to([P, KC, T]), ALU.subtract).then_inc(S["centred"], 1)
            inv_rms("ln", 5, 2, D)
            ve.tensor_tensor(vb, vb, rs[:].unsqueeze(1).broadcast_to([P, KC, T]), ALU.mult).then_inc(S["v_ready"], 1)
            for b in range(4):
                ve.wait_ge(bank_free[b], use("gc", b, 3))
            with ve.Fori(0, 2) as i:
                for c in range(8):
                    b = c % 4
                    ve.wait_ge(bank_ready[b], i * 2 + (use("co", b) + c // 4))
                    g_ = flat(gb[:, ds(i * 8 + c, 1)])
                    ve.tensor_tensor(g_, g_, bank[b][:, 0:T], ALU.mult).then_inc(bank_free[b], 1)

            take("dt", 6)
            ve.wait_ge(S["small_loaded"], 96)
            dve.mark(ve.tensor_tensor(dt_tok[:, 0:2], bank[6][:, 0:2 * H].rearrange("p (q h) -> p q h", q=2),
                                      rows_bc[:, 0:1].broadcast_to([P, 2, H]), ALU.add))
            dve.link(ve, ve.tensor_tensor(dt_tok[0:NS, 2], bank[6][0:NS, 2 * H:3 * H], rows_bc[0:NS, 0], ALU.add))
            ve.sem_inc(bank_free[6], 1)
            ve.scalar_tensor_tensor(out=sp_abs, in0=dt_tok[:], scalar=-1.0, in1=dt_tok[:], op0=ALU.mult,
                                    op1=ALU.max).then_inc(S["dt_abs"], 1)
            ve.wait_ge(S["dt_exp"], 1)
            dve.link(ve, ve.tensor_scalar(sp_u, sp_e, 1.0, None, ALU.add))
            ve.sem_inc(S["one_plus"], 1)
            dve.link(ve, ve.tensor_scalar(sp_d, sp_u, -1.0, None, ALU.add))
            dve.link(ve, ve.tensor_scalar(sp_z, sp_d, 0.0, None, ALU.is_equal))
            dve.link(ve, ve.tensor_tensor(sp_z, sp_z, sp_e, ALU.mult))
            dve.link(ve, ve.tensor_scalar(sp_d, sp_d, 1e-30, None, ALU.max))
            dve.link(ve, ve.reciprocal(sp_d, sp_d))
            dve.link(ve, ve.tensor_tensor(sp_m, sp_e, sp_d, ALU.mult))
            ve.wait_ge(S["dt_log"], 1)
            dve.link(ve, ve.tensor_tensor(sp_m, sp_m, sp_ln, ALU.mult))
            dve.link(ve, ve.tensor_tensor(sp_m, sp_m, sp_z, ALU.add))
            dve.link(ve, ve.scalar_tensor_tensor(out=dt_tok[:], in0=dt_tok[:], scalar=0.0, in1=sp_m, op0=ALU.max,
                                                 op1=ALU.add))
            ve.wait_ge(S["a_exp"], 1)
            ve.scalar_tensor_tensor(out=dtA[:], in0=dt_tok[:], scalar=-1.0, in1=rows_bc[:, 1:2].broadcast_to([P, 3, H]),
                                    op0=ALU.mult, op1=ALU.mult).then_inc(S["dta_ready"], 1)
            take("cum", 7)
            cum = bank[7][:, 0:192].rearrange("p (q h) -> p q h", q=6)
            dve.mark(ve.tensor_copy(acum[:, 0:2], cum[:, 0:2]))
            dve.link(ve, ve.tensor_copy(acum[0:NS, 2], cum[0:NS, 2]))
            dve.mark(ve.tensor_tensor(wend[:, 0], cum[:, 3], acum[:, 0], ALU.subtract))
            dve.mark(ve.tensor_tensor(wend[:, 2], cum[:, 4], acum[:, 1], ALU.subtract))
            dve.link(ve, ve.tensor_tensor(wend[0:NS, 3], cum[0:NS, 5], acum[0:NS, 2], ALU.subtract))
            dve.link(ve, ve.tensor_tensor(wend[:, 1], wend[:, 0], cum[:, 4], ALU.add))
            ve.sem_inc(S["w_arg"], 1)
            ve.sem_inc(bank_free[7], 1)
            ve.wait_ge(S["w_exp"], 1)
            dve.mark(ve.tensor_tensor(wend[:, 0:2], wend[:, 0:2], dt_tok[:, 0:1].broadcast_to([P, 2, H]), ALU.mult))
            dve.link(ve, ve.tensor_tensor(wend[:, 2:4], wend[:, 2:4], dt_tok[:, 1:3], ALU.mult))
            ve.sem_inc(S["w_ready"], 1)

            dve.mark(ve.memset(xraw[:, :, 0:SK - 1], 0.0))
            for half in range(2):
                take("sst", 4 + half)
                ve.tensor_copy(xsamp[:, 12 * half:12 * half + 12, :, 0:SK - 1],
                               bank[4 + half][:, 0:288].rearrange("p (k b l) -> p k b l", k=12, b=NB)).then_inc(
                                   bank_free[4 + half], 1)
            dve.wait(ve)
            with ve.Fori(0, XBC_N) as i:
                with dve.loop(i, XBC_N, 8 * 4):
                    for n in range(8):
                        b, par, c = n % 4, n % 2, i * 8 + n
                        ve.wait_ge(bank_ready[b], i * 2 + (use("xbc", b) + n // 4))
                        dve.mark(ve.tensor_copy(xraw[:, par, SK - 1:], bank[b][:, 0:NP]))
                        ve.tensor_copy(flat(xtail[:, ds(c, 1), 0:SK - 1]), bank[b][:, NP - SK + 1:NP])
                        ve.tensor_copy(xsamp[:, ds(c, 1), :, SK - 1:].rearrange("p k b l -> p (k b) l"),
                                       bank[b][:, NP:T].rearrange("p (b l) -> p b l", b=NB)).then_inc(bank_free[b], 1)
                        if n >= 2:
                            ve.wait_ge(S["xbc_ready"], i * 8 + n)
                        else:
                            ve.wait_ge(S["xbc_ready"], i * 8 + 1)
                        for k in range(SK):
                            tap = vcol[:, ds(c + (SW0 + k * XC), 1)]
                            u = xraw[:, par, k:k + NP]
                            dve.wait(ve)
                            if k == 0:
                                dve.mark(ve.tensor_scalar(acc[:, par], u, tap, None, ALU.mult))
                            else:
                                ins = ve.scalar_tensor_tensor(out=acc[:, par], in0=u, scalar=tap, in1=acc[:, par],
                                                              op0=ALU.mult, op1=ALU.add)
                                if k < SK - 1:
                                    dve.mark(ins)
                                else:
                                    ins.then_inc(S["acc_ready"], 1)
            for b in range(4):
                ve.wait_ge(bank_free[b], use("xbc", b, 2 * XBC_N - 1))
            dve.link(ve, ve.tensor_copy(xtail[:, :, SK - 1:].rearrange("p k (b l) -> p k b l", b=NB),
                                        xsamp[:, :, :, NL:NL + SK - 1]))
            ve.sem_inc(S["xtail_ready"], 1)
            dve.link(ve, ve.tensor_copy(tmps, bc(CONV_B, NS)))
            for k in range(SK):
                w = vcol[:, SW0 + k * XC:SW0 + (k + 1) * XC]
                dve.link(ve, ve.tensor_tensor(bl(uxs), xsamp[:, :, :, k:k + NL], bc(w, NB, NL), ALU.mult))
                dve.link(ve, ve.tensor_tensor(tmps, tmps, uxs, ALU.add))
            ve.sem_inc(S["xpad_ready"], 1)

            ve.wait_ge(S["xtail_out"], 32)
            ve.wait_ge(S["xbc_ready"], XC + 2)
            for b in range(4):
                ve.wait_ge(bank_free[b], use("z", b, 3))
            with ve.Fori(0, G) as g:
                with dve.loop(g, G, 4 + 4 * 2):
                    ve.wait_ge(bank_ready[3], g * 2 + use("ssd", 3))
                    ve.wait_ge(bank_ready[1], g * 8 + (use("ssd", 1) - 1))
                    dve.mark(ve.tensor_copy(btok[:, 0:2], bank[3][:, 0:NP].rearrange("p (q n) -> p q n", q=2)))
                    ve.tensor_copy(btok[0:NS, 2], bank[3][0:NS, 2 * P:3 * P]).then_inc(bank_free[3], 1)
                    ve.wait_ge(bank_free[3], g * 2 + use("ssd", 3))
                    ve.tensor_tensor(bexp[0:NS], btok[0:NS, 2:3].broadcast_to([NS, NB, P]), bc(seqsel[:], P),
                                     ALU.mult).then_inc(S["bexp_ready"], 1)
                    ve.wait_ge(bank_ready[3], g * 2 + use("ssd", 3, 1))
                    dve.mark(ve.tensor_tensor(cbm[:, 0:2], bank[3][:, 0:NP].rearrange("p (q n) -> p q n", q=2),
                                              upper[:].unsqueeze(1).broadcast_to([P, 2, P]), ALU.mult))
                    dve.mark(ve.tensor_tensor(cbm[0:NS, 2, 0:NS], bank[3][0:NS, 2 * P:2 * P + NS], ublk[:], ALU.mult))
                    dve.link(ve, ve.memset(rs[:, 0:1], 0.0))
                    ve.sem_inc(bank_free[3], 1)
                    for k in range(4):
                        par, c = k % 2, g * 4 + k
                        ve.wait_ge(bank_ready[4], g * 4 + (use("ssd", 4) + k))
                        ve.wait_ge(bank_ready[7], g * 4 + (use("ssd", 7) - 1 + k))
                        dve.mark(ve.tensor_copy(xtok[:, 0:2], bank[4][:, 0:NP].rearrange("p (q n) -> p q n", q=2)))
                        ve.tensor_copy(xtok[0:NS, 2], bank[4][0:NS, 2 * P:3 * P]).then_inc(bank_free[4], 1)
                        ve.wait_ge(bank_free[4], g * 4 + (use("ssd", 4) + k))
                        dve.wait(ve)
                        ve.wait_ge(bank_ready[1], g * 8 + (use("ssd", 1) - 1 + 2 * k))
                        for w, q, rows in ((0, 0, P), (1, 0, P), (2, 1, P), (3, 2, NS)):
                            ins = ve.tensor_tensor(xw[0:rows, w].rearrange("p (h q) -> p h q", h=2),
                                                   xtok[0:rows, q].rearrange("p (h q) -> p h q", h=2),
                                                   bc(wend[0:rows, w, ds(g * 8 + 2 * k, 2)], HD), ALU.mult)
                        ins.then_inc(S["xw_ready"], 1)
                        for h in range(2):
                            head = g * 8 + (2 * k + h)
                            ve.wait_ge(bank_ready[5 + h], g * 4 + (use("ssd", 5 + h) + k))
                            for q, (t0, rows) in enumerate(TOK):
                                ins = ve.tensor_scalar(mt[0:rows, h, t0:t0 + rows], bank[5 + h][0:rows, t0:t0 + rows],
                                                       acum[0:rows, q, ds(head, 1)], 0.0, ALU.subtract, ALU.min)
                            ins.then_inc(S["seg_ready"], 1)
                        for h in range(2):
                            head = g * 8 + (2 * k + h)
                            ve.wait_ge(S["exp_ready"], g * 8 + (2 * k + h + 1))
                            for q, (t0, rows) in enumerate(TOK):
                                ve.scalar_tensor_tensor(out=mt[0:rows, h, t0:t0 + rows], in0=mt[0:rows, h, t0:t0 + rows],
                                                        scalar=dt_tok[0:rows, q, ds(head, 1)],
                                                        in1=cbm[0:rows, q, 0:rows], op0=ALU.mult, op1=ALU.mult)
                            ve.wait_ge(bank_free[5 + h], g * 4 + (use("ssd", 5 + h) + k))
                            ve.tensor_tensor(cs[:, h], cs[:, h], flat(xbcT[:, ds(g + (KC + G), 1), P:T]),
                                             ALU.mult).then_inc(S["m_ready"], 1)
                        ve.wait_ge(S["scaled"], g * 4 + (k + 2))
                        for b in range(2):
                            ve.wait_ge(bank_ready[b], g * 8 + (use("ssd", b) + 2 * k + 1))
                            ve.tensor_tensor(s0[:, par, 4 * b:4 * b + 4], s0[:, par, 4 * b:4 * b + 4],
                                             bank[b][:].rearrange("p (b n) -> p b n", b=4), ALU.add).then_inc(
                                                 bank_free[b], 1)
                        ve.wait_ge(bank_ready[7], g * 4 + (use("ssd", 7) + k))
                        dve.link(ve, ve.scalar_tensor_tensor(out=rs[:], in0=flat(xbcT[:, ds(c, 1)]),
                                                             scalar=dcol[:, ds(c, 1)], in1=bank[7][:, 0:T],
                                                             op0=ALU.mult, op1=ALU.add))
                        ve.sem_inc(bank_free[7], 1)
                        ve.tensor_tensor(flat(zb[:, ds(c, 1)]), flat(zb[:, ds(c, 1)]), rs[:], ALU.mult).then_inc(
                            S["y_done"], 1)
            ve.wait_ge(S["sf_out"], 16 * KC)
            dve.link(ve, ve.memset(part_mix, 0.0))
            ve.sem_inc(S["part_zero"], 1)
            for q in range(G):
                take("gn", 4 + q)
                ve.tensor_scalar(grs[:, q], bank[4 + q][:, 0:T], 1.0 / (D // G), EPS, ALU.mult, ALU.add).then_inc(
                    S["gmean_ready"], 1)
            ve.wait_ge(S["y_done"], KC)
            for q in range(G):
                ve.wait_ge(S["groot_ready"], q + 1)
                ve.sem_inc(bank_free[4 + q], 1)
                dve.link(ve, ve.reciprocal(grs[:, q], grs[:, q]))
                for c in range(4 * q, 4 * q + 4):
                    dve.mark(ve.scalar_tensor_tensor(out=zb[:, c], in0=zb[:, c], scalar=SSD_G[:, c:c + 1],
                                                     in1=grs[:, q], op0=ALU.mult, op1=ALU.mult))
            dve.wait(ve)
            ve.sem_inc(S["y_ready"], 1)
            for b in range(4):
                ve.wait_ge(bank_free[b], use("gs", b, 3))
            with ve.Fori(0, 2) as i:
                with dve.loop(i, 2, 8):
                    for c in range(8):
                        b = c % 4
                        ve.wait_ge(bank_ready[b], i * 2 + (use("so", b) + c // 4))
                        v_, g_ = flat(vb[:, ds(i * 8 + c, 1)]), flat(gb[:, ds(i * 8 + c, 1)])
                        dve.link(ve, ve.tensor_tensor(v_, v_, bank[b][:, 0:T], ALU.mult))
                        ve.sem_inc(bank_free[b], 1)
                        ve.tensor_tensor(g_, g_, v_, ALU.add).then_inc(S["merged"], 1)

            def add_gated(b, c, gate, done):
                g_ = mod[:, ds(gate, 1)] if not isinstance(gate, int) else mod[:, gate:gate + 1]
                x_ = xT[:, ds(c, 1)] if not isinstance(c, int) else xT[:, c:c + 1]
                x_p, x_s = flat(x_[:, :, 0:NP]), flat(x_[:, :, NP:T])
                dve.mark(ve.scalar_tensor_tensor(out=x_p, in0=bank[b][:, 0:NP], scalar=g_[:, :, 0:1], in1=x_p,
                                                 op0=ALU.mult, op1=ALU.add))
                tmp = (rs, stat)[b % 2][:, NP:T]
                dve.link(ve, ve.tensor_tensor(tmp.rearrange("p (b l) -> p b l", b=NB),
                                              bank[b][:, NP:T].rearrange("p (b l) -> p b l", b=NB),
                                              bc(flat(g_[:, :, 1:NSEQ]), NL), ALU.mult))
                ve.sem_inc(bank_free[b], 1)
                ve.tensor_tensor(x_s, x_s, tmp, ALU.add).then_inc(S[done], 1)

            with ve.Fori(0, 2) as i:
                with dve.loop(i, 2, 16):
                    for c in range(8):
                        b = c % 4
                        ve.wait_ge(bank_ready[b], i * 2 + (use("wo", b) + c // 4))
                        add_gated(b, i * 8 + c, i * 8 + (2 * KC + c), "x_mid")
            ve.wait_ge(S["x_mid"], KC)
            inv_rms("n2", 4, 3, D)
            modulate(G_FFN, 3 * KC, 4 * KC)

            neg, m1_, m2_ = small[0], small[1], small[2]
            for par in range(2):
                ve.wait_ge(st_out[par], 128)
            ve.wait_ge(S["sf_out"], 16 * KC)
            dve.link(ve, ve.memset(lg, 0.0))
            take("route", 5)
            dve.mark(ve.tensor_tensor(lg[:, 0:2], bank[5][:, 0:72].rearrange("p (q n) -> p q n", q=2),
                                      rbias[:].unsqueeze(1).broadcast_to([P, 2, 36]), ALU.add))
            dve.link(ve, ve.tensor_tensor(lg[0:NS, 2], bank[5][0:NS, 72:108], rbias[0:NS], ALU.add))
            ve.sem_inc(bank_free[5], 1)
            ve.wait_ge(S["pooled"], 1)
            gmax, gsum, gtop, gfirst, emax, esum, p1, p2, first1, first2, ptot, gA, gB, sA, sB, eA, eB = tiny[:17]
            cand, ohg = small[3][:, :, 0:NG], small[4][:, :, 0:NG]
            oh1, oh2, prob, left, cand8 = [small[5 + n][:, :, 0:EG] for n in range(5)]

            def iota(n):
                return iota_e[:, 0:n].unsqueeze(1).broadcast_to([P, 3, n])

            def first_of(onehot, cnd, values, top, idx, n):
                dve.link(ve, ve.tensor_tensor(cnd, values, bc(top, n), ALU.is_equal))
                dve.link(ve, ve.scalar_tensor_tensor(out=cnd, in0=cnd, scalar=-64.0, in1=iota(n), op0=ALU.mult,
                                                     op1=ALU.add))
                dve.link(ve, ve.tensor_reduce(idx, cnd, AX_X, ALU.min))
                dve.link(ve, ve.tensor_tensor(onehot, cnd, bc(idx, n), ALU.is_equal))

            dve.link(ve, ve.tensor_reduce(gmax, lg[:, :, 0:NG], AX_X, ALU.max))
            first_of(ohg, cand, lg[:, :, 0:NG], gmax, gfirst, NG)
            dve.link(ve, ve.tensor_tensor(lg[:, :, 0:NG], lg[:, :, 0:NG], bc(gmax, NG), ALU.subtract))
            ve.sem_inc(S["e_arg"], 1)
            chosen_l = small[10].rearrange("p q (g e) -> p q g e", g=NG)
            dve.link(ve, ve.tensor_tensor(chosen_l, lg[:, :, NG:36].rearrange("p q (g e) -> p q g e", g=NG),
                                          bc(ohg, EG), ALU.mult))
            dve.link(ve, ve.tensor_reduce(sel, chosen_l.rearrange("p q g e -> p q e g"), AX_X, ALU.add))
            dve.link(ve, ve.tensor_reduce(emax, sel, AX_X, ALU.max))
            dve.link(ve, ve.tensor_tensor(sel, sel, bc(emax, EG), ALU.subtract))
            ve.sem_inc(S["e_arg"], 1)
            ve.wait_ge(S["gexp"], 1)
            dve.link(ve, ve.tensor_reduce(gsum, lg[:, :, 0:NG], AX_X, ALU.add))
            dve.link(ve, ve.reciprocal(gtop, gsum))
            ve.wait_ge(S["eexp"], 1)
            dve.link(ve, ve.tensor_reduce(esum, sel, AX_X, ALU.add))
            dve.link(ve, ve.reciprocal(esum, esum))
            dve.link(ve, ve.tensor_tensor(prob, sel, bc(esum, EG), ALU.mult))
            dve.link(ve, ve.tensor_reduce(p1, prob, AX_X, ALU.max))
            first_of(oh1, cand8, prob, p1, first1, EG)
            dve.link(ve, ve.scalar_tensor_tensor(out=left, in0=oh1, scalar=-2.0, in1=prob, op0=ALU.mult, op1=ALU.add))
            dve.link(ve, ve.tensor_reduce(p2, left, AX_X, ALU.max))
            first_of(oh2, cand8, left, p2, first2, EG)
            dve.link(ve, ve.tensor_tensor(ptot, p1, p2, ALU.add))
            dve.link(ve, ve.reciprocal(ptot, ptot))
            dve.link(ve, ve.tensor_tensor(ptot, ptot, gtop, ALU.mult))
            dve.mark(ve.tensor_tensor(gA, p1, ptot, ALU.mult))
            dve.mark(ve.tensor_tensor(gB, p2, ptot, ALU.mult))
            for m_, oh in ((m1_, oh1), (m2_, oh2)):
                dve.mark(ve.tensor_tensor(m_.rearrange("p q (g e) -> p q g e", g=NG), bc(ohg, EG),
                                          oh.unsqueeze(2).broadcast_to([P, 3, NG, EG]), ALU.mult))
            dve.wait(ve)
            ve.tensor_tensor(chosen, m1_, m2_, ALU.add).then_inc(S["cnt_ready"], 1)
            take("route", 6)
            dve.link(ve, ve.tensor_copy(cntb[0:NE], bank[6][0:NE, 0:1].broadcast_to([NE, P])))
            ve.sem_inc(bank_free[6], 1)
            ve.sem_inc(S["cnt_ready"], 1)
            pos = small[11]
            dve.mark(ve.memset(pos, 0.0))
            dve.link(ve, ve.memset(meta, 0.0))
            take("route", 7)
            dve.mark(ve.tensor_copy(pos[:, 0:2], bank[7][:, 0:64].rearrange("p (q e) -> p q e", q=2)))
            dve.mark(ve.tensor_copy(pos[0:NS, 2], bank[7][0:NS, 64:96]))
            dve.mark(ve.tensor_copy(meta[:, 0, 0:NE], bank[7][:, 128:160]))
            dve.mark(ve.tensor_scalar(meta[:, 1, 0:NE], bank[7][:, 96:128], float(SLOTS - WIN), None, ALU.min))
            dve.link(ve, ve.tensor_scalar(meta[:, 2, 0:NE], bank[7][:, 96:128], float(SLOTS - T), None, ALU.min))
            ve.sem_inc(bank_free[7], 1)
            dve.link(ve, ve.tensor_copy(meta_i[:], meta))
            ve.sem_inc(S["meta_ready"], 1)
            for m_, s_, e_ in ((m1_, sA, eA), (m2_, sB, eB)):
                dve.link(ve, ve.tensor_tensor(neg, pos, m_, ALU.mult))
                dve.link(ve, ve.tensor_reduce(s_, neg, AX_X, ALU.add))
                dve.link(ve, ve.tensor_tensor(neg, m_, iota(NE), ALU.mult))
                dve.link(ve, ve.tensor_reduce(e_, neg, AX_X, ALU.add))
            for q, (t0, rows) in enumerate(TOK):
                def at_pair(out, s_, val=None):
                    ins = ve.tensor_scalar(out[0:rows, q] if out is not tq else tq[0:rows], iota_s[0:rows],
                                           s_[0:rows, q:q + 1], None if val is None else val[0:rows, q:q + 1],
                                           ALU.is_equal, *(() if val is None else (ALU.mult,)))
                    dve.link(ve, ins)

                at_pair(pm, sA)
                dve.mark(ve.scalar_tensor_tensor(out=pm[0:rows, q], in0=iota_s[0:rows], scalar=sB[0:rows, q:q + 1],
                                                 in1=pm[0:rows, q], op0=ALU.is_equal, op1=ALU.add))
                for out, vA, vB in ((gt, gA, gB), (et, eA, eB)):
                    at_pair(out, sA, vA)
                    at_pair(tq, sB, vB)
                    dve.link(ve, ve.tensor_tensor(out[0:rows, q], out[0:rows, q], tq[0:rows], ALU.add))
            ve.sem_inc(S["sort_ready"], 1)
            for b, dst in enumerate((gbc[:, 0:T], gbc[:, T:], ebc[:, 0:T], ebc[:, T:])):
                take("gates", b)
                ve.tensor_copy(dst, bank[b][:, 0:T]).then_inc(bank_free[b], 1)
            dve.mark(ve.memset(ys, 0.0))
            for c in range(KC):
                for half in range(2):
                    b = 2 * (c % 2) + half
                    take("gather", b, c // 2)
                    ve.tensor_copy(hs[:, c, T * half:T * (half + 1)], bank[b][:, 0:T]).then_inc(bank_free[b], 1)
            dve.wait(ve)
            for b in range(4):
                ve.wait_ge(bank_free[b], use("gather", b, 7))

            def window(e):
                w0 = ve.value_load(meta_i[0:1, 1, ds(e, 1)], min_val=0, max_val=SLOTS - WIN)
                return w0

            w_first = ve.value_load(meta_i[0:1, 1, 0:1], min_val=0, max_val=SLOTS - WIN)
            ve.tensor_copy(hwin[:, 0], hs[:, :, ds(w_first, WIN)]).then_inc(S["win_ready"], 1)
            with ve.Fori(0, 8) as i:
                with dve.loop(i, 8, 4 * 3):
                    for k in range(4):
                        nxt = ve.value_load(meta_i[0:1, 1, ds(i * 4 + (k + 1), 1)], min_val=0, max_val=SLOTS - WIN)
                        ve.wait_ge(S["u_done"], i * 4 + (k + 1))
                        ve.tensor_copy(hwin[:, (k + 1) % 2], hs[:, :, ds(nxt, WIN)]).then_inc(S["win_ready"], 1)
                        n_pairs = ve.value_load(meta_i[0:1, 0, ds(i * 4 + k, 1)], min_val=0, max_val=T)
                        wn = ve.value_load(meta_i[0:1, 1, ds(i * 4 + k, 1)], min_val=0, max_val=SLOTS - WIN)
                        ww = ve.value_load(meta_i[0:1, 2, ds(i * 4 + k, 1)], min_val=0, max_val=SLOTS - T)
                        mine = iota_e[:, ds(i * 4 + k, 1)]
                        count = dve.n
                        with ve.If(n_pairs > WIN):
                            dve.link(ve, ve.scalar_tensor_tensor(out=gwin, in0=ebc[:, ds(ww, T)], scalar=mine,
                                                                 in1=gbc[:, ds(ww, T)], op0=ALU.is_equal, op1=ALU.mult))
                            ve.wait_ge(S["u_done"], i * 4 + (k + 2))
                            dve.mark(ve.tensor_tensor(hid[:, 0], bank[5][:, 0:T], gwin, ALU.mult))
                            dve.link(ve, ve.tensor_tensor(hid[:, 1], bank[7][:, 0:T], gwin, ALU.mult))
                            ve.wait_ge(S["sil_ready"], i * 4 + (k + 2))
                            ve.tensor_tensor(hid, hid, sil, ALU.mult).then_inc(S["hid_ready"], 1)
                            ve.wait_ge(S["ys_done"], i * 4 + (k + 1))
                            for c in range(KC):
                                ve.wait_ge(S["wide_ready"], i * 64 + (16 * k + c + 1))
                                y_ = ys[:, c, ds(ww, T)]
                                ve.tensor_tensor(y_, y_, bank[c % 4][:, 0:T], ALU.add).then_inc(S["wide_free"], 1)
                            ve.wait_ge(S["wide_free"], i * 64 + 16 * (k + 1))
                            ve.sem_inc(S["ys_done"], 1)
                        n_after, dve.n = dve.n, count
                        with ve.Else():
                            dve.link(ve, ve.scalar_tensor_tensor(out=gwin[:, 0:WIN], in0=ebc[:, ds(wn, WIN)], scalar=mine,
                                                                 in1=gbc[:, ds(wn, WIN)], op0=ALU.is_equal, op1=ALU.mult))
                            ve.wait_ge(S["u_done"], i * 4 + (k + 2))
                            dve.mark(ve.tensor_tensor(hid[:, 0, 0:WIN], bank[5][:, 0:WIN], gwin[:, 0:WIN], ALU.mult))
                            dve.link(ve, ve.tensor_tensor(hid[:, 1, 0:WIN], bank[5][:, WIN:2 * WIN], gwin[:, 0:WIN], ALU.mult))
                            ve.wait_ge(S["sil_ready"], i * 4 + (k + 2))
                            ve.tensor_tensor(hid[:, :, 0:WIN], hid[:, :, 0:WIN], sil[:, :, 0:WIN], ALU.mult).then_inc(
                                S["hid_ready"], 1)
                            ve.wait_ge(S["ys_done"], i * 4 + (k + 1))
                            ve.wait_ge(S["d_ready"], i * 4 + (k + 1))
                            for q in range(4):
                                y_ = ys[:, 4 * q:4 * q + 4, ds(wn, WIN)]
                                ins = ve.tensor_tensor(y_, y_, bank[q][:].rearrange("p (c w) -> p c w", c=4), ALU.add)
                            ins.then_inc(S["ys_done"], 1)
                            ve.sem_inc(S["wide_free"], 16)
                        assert dve.n == n_after

            for j in range(5):
                n = min(P, SLOTS - P * j)
                take("pt", 4 + j % 2, j // 2)
                ve.tensor_copy(pt[0:n, j], bank[4 + j % 2][0:n, 0:T]).then_inc(bank_free[4 + j % 2], 1)
            for c in range(KC):
                take("unsort", c % 4, c // 4)
                add_gated(c % 4, c, 5 * KC + c, "moe_ready")
            ve.wait_ge(S["moe_ready"], KC)
            inv_rms("n3", 4, 4, D)
            for c in range(KC):
                ve.scalar_tensor_tensor(out=xT[:, c], in0=xT[:, c], scalar=FIN_G[:, c:c + 1], in1=rs[:],
                                        op0=ALU.mult, op1=ALU.mult).then_inc(S["y_fin"], 1)


_OUTS = [
    (1, NP, D), (NB, NL, D), (1, 1, H, HD, P), (1, 1, SK - 1, 3072), (1, 1, CK - 1, D),
    (1, NB, H, HD, P), (1, NB, SK - 1, 3072), (1, NB, CK - 1, D),
]


def kernel(**inputs):
    import numpy as _np
    import concourse.bacc as _bacc
    from concourse import mybir as _mybir
    from concourse.bass_utils import run_bass_kernel_spmd as _run

    nc = _bacc.Bacc("TRN2", target_bir_lowering=False, num_devices=1)
    arrays, a = {}, {}
    for name, x in inputs.items():
        x = _np.ascontiguousarray(x)
        arrays[f"in_{name}"] = x
        a[name] = nc.dram_tensor(f"in_{name}", x.shape, _mybir.dt.from_np(x.dtype), kind="ExternalInput").ap()
    outs = [nc.dram_tensor(f"out_{i}", shape, _mybir.dt.float32, kind="ExternalOutput").ap()
            for i, shape in enumerate(_OUTS)]
    hybrid_step(nc, a, outs)
    r = _run(nc, [arrays], core_ids=[0])
    return tuple(r.results[0][f"out_{i}"] for i in range(len(_OUTS)))
```

```python
from contextlib import ExitStack, contextmanager, nullcontext

import concourse.bass as bass
from concourse import mybir

F32 = mybir.dt.float32
I32 = mybir.dt.int32
ALU = mybir.AluOpType
ACT = mybir.ActivationFunctionType
AX_X = mybir.AxisListType.X
ds = bass.ds

P = 128
D = 2048
KC = D // P
NP = 256
NB, NL = 8, 4
NS = NB * NL
T = NP + NS
NSEQ = 1 + NB
XC = 3072 // P
H = 32
G = 4
HD = 64
CK = 31
SK = 4
NE = 32
NG = 4
EG = 8
EPS = 1e-6
SLOTS = 2 * T
WIN = 64
UC = 256
RING = 4
TOK = [(0, P), (P, P), (NP, NS)]

Z0, X0, DT0, GLU0 = 0, D, D + 3072, D + 3072 + H
GS0, GC0 = GLU0 + 2 * D, GLU0 + 3 * D

GLU_N, XBC_N = 4, 3

MIXED = "pappappappap"
PHASES = [("ada", 4, "aaaa"), ("glu", 2, MIXED), ("gc", 1, MIXED), ("z1", 1, "papapapa"), ("co", 1, MIXED),
          ("xbc", 3, "pppp"), ("z2", 1, "pppp"), ("gs", 2, "pppp"), ("so", 1, MIXED), ("wo", 1, "papapapapapapapa")]


def phase_uses(name):
    steps, units = {n: (s, u) for n, s, u in PHASES}[name]
    return {**{b: steps * units.count("p") // 2 for b in range(4)},
            **{b: steps * units.count("a") // 2 for b in range(4, 8)}}


class Count:

    def __init__(self, sem):
        self.sem, self.n, self.off = sem, 0, 0

    def mark(self, ins):
        ins.then_inc(self.sem, 1)
        self.n += 1

    def wait(self, eng, back=0):
        eng.wait_ge(self.sem, self.off + self.n - back)

    def link(self, eng, ins):
        self.mark(ins)
        self.wait(eng)

    def skip(self, eng, n):
        eng.sem_inc(self.sem, n)
        self.n += n

    @contextmanager
    def loop(self, i, trips, per):
        start = self.n
        self.off = i * per
        yield
        assert self.n == start + per, self.n - start
        self.n, self.off = start + trips * per, 0


USES = [
    ("x", {0: 4, 1: 4, 2: 4, 3: 4}), ("c", {4: 1}), ("vec", {5: 1, 6: 1}), ("cst", {4: 4, 5: 4, 6: 4, 7: 4}),
    ("n1", {4: 1}), ("ada", phase_uses("ada")), ("glu", phase_uses("glu")), ("tail", {4: 1, 5: 1, 6: 1, 7: 1}),
    ("gc", phase_uses("gc")), ("ln", {4: 1}), ("z1", phase_uses("z1")), ("lnsq", {5: 1}), ("dt", {6: 1}),
    ("co", phase_uses("co")), ("cum", {7: 1}), ("sst", {4: 1, 5: 1}), ("xbc", phase_uses("xbc")),
    ("z2", phase_uses("z2")), ("xtail", {4: 2, 5: 2, 6: 1, 7: 1}), ("ssd", {0: 32, 1: 32, 2: 20, 3: 20, 4: 16, 5: 16, 6: 16, 7: 16}),
    ("gn", {4: 1, 5: 1, 6: 1, 7: 1}), ("so", phase_uses("so")),
    ("wo", phase_uses("wo")), ("n2", {4: 1}), ("route", {5: 1, 6: 1, 7: 1}),
    ("gates", {0: 1, 1: 1, 2: 1, 3: 1}), ("gather", {b: 8 for b in range(6)}),
    ("pt", {4: 3, 5: 2}), ("unsort", {0: 4, 1: 4, 2: 4, 3: 4, 4: 8, 5: 8, 6: 8, 7: 8}),
    ("n3", {4: 1}), ("y", {4: 3, 5: 3, 6: 3, 7: 3}),
]


def uses_before():
    at, out = {b: 0 for b in range(8)}, {}
    for name, banks in USES:
        out[name] = dict(at)
        for b, n in banks.items():
            at[b] += n
    return out


def hybrid_step(nc, a, o):
    with ExitStack() as ctx:
        def sb(name, shape, dt=F32):
            return ctx.enter_context(nc.sbuf_tensor(name, shape, dt))

        def sem(name):
            return ctx.enter_context(nc.semaphore(name))

        ring = sb("ring", [P, RING, KC, UC])
        xT = sb("xT", [P, KC, T])
        hT = sb("hT", [P, KC, T])
        ident = sb("ident", [P, P])
        ones = sb("ones", [P, P])
        upper = sb("upper", [P, P])
        seqsel = sb("seqsel", [NS, NB])
        blk = sb("blk", [NS, NS])
        ublk = sb("ublk", [NS, NS])
        vcol = sb("vcol", [P, 7 * P])
        mod = sb("mod", [P, 6 * KC, NSEQ])
        scaleA = sb("scaleA", [P, KC, NSEQ])
        rs = sb("rs", [P, T])
        stat = sb("stat", [P, T])
        dcol = sb("dcol", [P, KC])
        dt_tok = sb("dt_tok", [P, 3, H])
        dtA = sb("dtA", [P, 3, H])
        acum = sb("acum", [P, 3, H])
        wend = sb("wend", [P, 4, H])
        rows_bc = sb("rows_bc", [P, 2, H])
        rbias = sb("rbias", [P, 36])
        meta_i = sb("meta_i", [P, 3, NE + 1], I32)
        WORK = 24000
        work = sb("work", [P, WORK])

        def carve(at, *dims):
            n = 1
            for x in dims:
                n *= x
            assert at + n <= WORK, (at, n)
            v = work[:, at:at + n]
            if len(dims) == 2:
                v = v.rearrange("p (a b) -> p a b", a=dims[0])
            if len(dims) == 3:
                v = v.rearrange("p (a b c) -> p a b c", a=dims[0], b=dims[1])
            if len(dims) == 4:
                v = v.rearrange("p (a b c d) -> p a b c d", a=dims[0], b=dims[1], c=dims[2])
            return v

        BIG = KC * T
        zb = carve(0, KC, T)
        vb = carve(BIG, KC, T)
        xbcT = carve(BIG, XC, T)
        gb = carve(BIG + XC * T, KC, T)
        TMP = BIG + XC * T + BIG
        sq = zb
        xrow = carve(0, 3, D)
        crow = carve(3 * D, D)
        vrow = carve(4 * D, 7, P)
        cstrow = carve(4 * D + 7 * P + KC * NSEQ, 2, D)
        t = TMP
        usamp = carve(t, KC, NB, CK - 1 + NL); t += KC * NB * (CK - 1 + NL)
        upad = carve(t, 4, CK - 1 + NP); t += 4 * (CK - 1 + NP)
        sgl = carve(t, 4, T); t += 4 * T
        utail = carve(t, KC, CK - 1 + NS); t += KC * (CK - 1 + NS)
        assert t == TMP + 7640
        cT = carve(t, KC, NSEQ); t += KC * NSEQ
        fold = carve(t, NSEQ)
        part_glu = carve(BIG + XC * T, 2, UC)
        part_mix = carve(TMP + 6862, 2, UC)
        tmpc = carve(0, KC, NS)
        uvs = carve(KC * NS, KC, NS)
        tailrow = carve(2 * KC * NS, D)
        sq_ln = carve(TMP, KC, T)
        wdt = carve(TMP + KC * T, KC, H)
        t = TMP
        xsamp = carve(t, XC, NB, SK - 1 + NL); t += XC * NB * (SK - 1 + NL)
        xraw = carve(t, 2, SK - 1 + NP); t += 2 * (SK - 1 + NP)
        xtail = carve(t, XC, SK - 1 + NB * (SK - 1)); t += XC * (SK - 1) * (1 + NB)
        sstrow = carve(t, XC * P); t += XC * P
        acc = carve(t, 2, NP); t += 2 * NP
        tmps = carve(t, XC, NS); t += XC * NS
        uxs = carve(t, XC, NS); t += XC * NS
        t = TMP
        s0 = carve(t, 2, NB, P); t += 2 * NB * P
        s0T = carve(t, NB, P); t += NB * P
        bexp = carve(t, NB, P); t += NB * P
        xst = carve(t, T); t += T
        bst = carve(t, T); t += T
        xtok = carve(t, 3, P); t += 3 * P
        btok = carve(t, 3, P); t += 3 * P
        cbm = carve(t, 3, P); t += 3 * P
        mt = carve(t, 2, T); t += 2 * T
        cs = carve(t, 2, P + NS); t += 2 * (P + NS)
        xw = carve(t, 4, P); t += 4 * P
        s1T = carve(t, P); t += P
        sfin = carve(t, P); t += P
        dax = carve(t, P); t += P
        dec = carve(t, NB); t += NB
        ud = stat
        hs = carve(0, KC, SLOTS)
        ys = carve(KC * SLOTS, KC, SLOTS)
        t = 2 * KC * SLOTS
        gbc = carve(t, SLOTS); t += SLOTS
        ebc = carve(t, SLOTS); t += SLOTS
        pm = carve(t, 3, SLOTS); t += 3 * SLOTS
        iota_e = carve(t, NE); t += NE
        strict = carve(t, P); t += P
        meta = carve(t, 3, NE + 1); t += 3 * (NE + 1)
        rt = t
        htok = carve(t, 2, 3 * P); t += 2 * 3 * P
        gwin = carve(rt, T)
        sil = carve(rt + T, 2, T)
        hid = carve(rt + 3 * T, 2, T)
        assert rt + 5 * T <= WORK
        hwin = hT[:, :, 0:2 * WIN].rearrange("p k (two w) -> p two k w", two=2)
        t = KC * SLOTS
        wr = carve(t, KC, 36); t += KC * 36
        lg = carve(t, 3, 36); t += 108
        small = [carve(t + 96 * n, 3, 32) for n in range(14)]; t += 96 * 14
        tiny = [carve(t + 4 * n, 3) for n in range(20)]; t += 80
        iota_s = carve(t, SLOTS); t += SLOTS
        gt = carve(t, 3, SLOTS); t += 3 * SLOTS
        et = carve(t, 3, SLOTS); t += 3 * SLOTS
        tq = carve(t, SLOTS); t += SLOTS
        cntb = carve(t, P); t += P
        sel = carve(t, 3, EG); t += 3 * EG
        chosen = small[12]
        sp_abs, sp_e, sp_u, sp_ln, sp_d, sp_z, sp_m = [carve(TMP + KC * T + KC * H + 96 * n, 3, H) for n in range(7)]
        grs = carve(TMP + 4096, G, T)
        pt = carve(0, 5, T)
        ytok = carve(5 * T, 2, 5 * P)
        yrow = carve(0, 3, D)
        assert 3 * D <= KC * SLOTS

        bank = [ctx.enter_context(nc.psum_tensor(f"bank{b}", [P, 512], F32)) for b in range(8)]

        slot_loaded = [sem(f"slot_loaded{s}") for s in range(RING)]
        bank_ready = [sem(f"bank_ready{b}") for b in range(8)]
        bank_free = [sem(f"bank_free{b}") for b in range(8)]
        base = uses_before()

        def use(name, b, k=0):
            return base[name][b] + 1 + k

        pool = Count(sem("pool_step"))
        dve = Count(sem("dve_step"))
        act = Count(sem("act_step"))
        S = {n: sem(n) for n in (
            "consts_ready x_loaded c_loaded v_loaded vrow_zero small_loaded cst_loaded usamp_ready silu_c c_ready "
            "squares_ready mean_ready root_ready h_ready conv_ready y_fin vsamp_ready tail_ready tail_out "
            "v_ready gc_ready centred wdt_loaded dt_abs dt_exp dt_log one_plus dta_ready w_arg w_exp w_ready a_exp sst_loaded "
            "xpad_ready acc_ready acc_free xbc_ready xtail_ready xrow_ready xtail_out bst_ready xst_ready "
            "ud_ready dax_ready seg_ready exp_ready m_ready xw_ready bexp_ready dec_free scaled sf_out "
            "y_done x_used prod_ready prod_turned scale_ready hn_ready hs_ready gsq_ready gmean_ready groot_ready gn_ready y_ready merged x_mid "
            "wr_loaded logits_ready gexp eexp gates_ready cnt_ready meta_ready sort_ready ys_zero "
            "win_ready g_ready u_done sil_ready hid_ready d_ready ys_done wide_ready wide_free "
            "part_zero sf_free moe_ready out_rows out_done pads_zero state_copy tail_rows e_arg pooled vb_free").split()}
        s0_loaded = [sem(f"s0_loaded{p}") for p in range(2)]
        st_out = [sem(f"st_out{p}") for p in range(2)]

        w_ada = a["w_ada"][0].rearrange("(k p) n -> p k n", p=P)
        w_in = a["w_in"][0].rearrange("(k p) n -> p k n", p=P)
        w_co = a["w_conf_out"][0].rearrange("(k p) n -> p k n", p=P)
        w_so = a["w_ssd_out"][0].rearrange("(k p) n -> p k n", p=P)
        w_o = a["w_o"][0].rearrange("(k p) n -> p k n", p=P)
        wg_e = a["w_exp_gate"][0].rearrange("e (k p) n -> p e k n", p=P)
        wu_e = a["w_exp_up"][0].rearrange("e (k p) n -> p e k n", p=P)
        wd_e = a["w_exp_down"][0].rearrange("e (f p) n -> p e f n", p=P)
        (y_p, y_s, ssm_p, sconv_p, cconv_p, ssm_s, sconv_s, cconv_s) = o
        s0_d = a["state_ssm"][0].rearrange("b (c h) q n -> (h q) c b n", h=2)
        s1_d = ssm_s[0].rearrange("b (c h) q n -> (h q) c b n", h=2)
        ssm_pd = ssm_p[0, 0].rearrange("(c h) q n -> (h q) c n", h=2)

        def bc(ap, *dims):
            shape = list(ap.shape)
            for d_ in dims:
                ap = ap.unsqueeze(len(shape))
                shape.append(d_)
            return ap.broadcast_to(shape)

        def vec(tile, at, n=KC):
            return vcol[:, tile * P + at:tile * P + at + n]

        B_ADA, G_MIX, G_FFN = vec(0, 0, 96), vec(0, 96), vec(0, 112)
        CONV_B, SSD_G, CONF_B = vec(1, 0, XC), vec(1, 24), vec(1, 40)
        LN_G, LN_B, FIN_G = vec(1, 56), vec(1, 72), vec(1, 88)
        SW0, CW0 = 2 * P, 3 * P

        def bl(ap):
            return ap.rearrange("p k (b l) -> p k b l", b=NB)

        VIEWS = {"gc": (w_in, GC0), "co": (w_co, 0), "z1": (w_in, Z0), "z2": (w_in, Z0 + D // 2), "xbc": (w_in, X0), "gs": (w_in, GS0),
                 "so": (w_so, 0), "wo": (w_o, 0)}
        ring0, ada0, rnd, au = {}, {}, 0, 0
        for name, steps, units in PHASES:
            ring0[name], ada0[name] = rnd, au
            rnd += steps * len(units) // RING
            au += steps * units.count("a")
        assert au == 6 * D // UC
        MOE_R = rnd

        def place(units, u):
            kind = units[u]
            n, many = units[:u].count(kind), units.count(kind)
            if kind == "p":
                return n, (2 * n + 1) % 4, (2 * n + 1) // 4, many // 2
            return n, 4 + n % 2, n // 2, many // 2

        def steps_of(eng, steps):
            return eng.Fori(0, steps) if steps > 1 else nullcontext(0)

        block = ctx.enter_context(nc.Block())

        @block.sync
        def _(sp):
            def unit(name, units, i, u):
                n, _, _, _ = place(units, u)
                if units[u] == "a":
                    src = w_ada[:, :, ds(i * (units.count("a") * UC) + (ada0[name] + n) * UC, UC)]
                elif name == "glu":
                    src = w_in[:, :, ds(i * (units.count("p") * UC // 2) + (GLU0 + (n % 2) * D + (n // 2) * UC), UC)]
                else:
                    w, c0 = VIEWS[name]
                    src = w[:, :, ds(i * (units.count("p") * UC) + (c0 + n * UC), UC)]
                sp.dma_start(ring[:, u % RING], src).then_inc(slot_loaded[u % RING], 16)

            def slot_used(name, units, i, u):
                _, b, k, per = place(units, u)
                sp.wait_ge(bank_ready[b], i * per + use(name, b, k))

            def stream(n, head=True, rest=True):
                name, steps, units = PHASES[n]
                if head:
                    for u in range(RING):
                        if n:
                            before, s_, u_ = PHASES[n - 1]
                            slot_used(before, u_, s_ - 1, len(u_) - RING + u)
                        unit(name, units, 0, u)
                if rest:
                    for u in range(RING, len(units)):
                        slot_used(name, units, 0, u - RING)
                        unit(name, units, 0, u)
                    if steps > 1:
                        with sp.Fori(1, steps) as i:
                            for u in range(len(units)):
                                if u < RING:
                                    _, b, k, per = place(units, len(units) - RING + u)
                                    sp.wait_ge(bank_ready[b], i * per + (use(name, b, k) - per))
                                else:
                                    slot_used(name, units, i, u - RING)
                                unit(name, units, i, u)

            sp.dma_start(xrow[:, 0:2], a["x_prompt"][0].rearrange("(q p) n -> p q n", p=P)).then_inc(S["x_loaded"], 16)
            sp.dma_start(xrow[0:NS, 2], a["x_sample"].rearrange("b l n -> (b l) n")).then_inc(S["x_loaded"], 16)
            sp.dma_start(crow[0:1], a["c_prompt"]).then_inc(S["c_loaded"], 16)
            sp.dma_start(crow[1:NSEQ], a["c_sample"]).then_inc(S["c_loaded"], 16)
            stream(0)
            stream(1)
            stream(2)
            sp.wait_ge(S["tail_rows"], 4)
            sp.dma_start(cconv_p[0, 0], tailrow[0:CK - 1]).then_inc(S["out_done"], 16)
            for b in range(NB):
                sp.dma_start(cconv_s[0, b, CK - 1 - NL:CK - 1],
                             tailrow[CK - 1 + NL * b:CK - 1 + NL * (b + 1)]).then_inc(S["tail_out"], 16)
            stream(3, rest=False)
            sp.wait_ge(S["vsamp_ready"], 1)
            sp.wait_ge(S["conv_ready"], 1)
            sp.wait_ge(bank_free[7], use("tail", 7))
            sp.dma_start(wdt, w_in[:, :, DT0:DT0 + H], allow_slow_non_contiguous=True).then_inc(S["wdt_loaded"], 16)
            stream(3, head=False)
            stream(4, rest=False)
            sp.wait_ge(S["dta_ready"], 1)
            sp.dma_start(sstrow[0:NB * (SK - 1)], a["state_ssd_conv"][0].rearrange("b k n -> (b k) n")).then_inc(
                S["sst_loaded"], 16)
            stream(4, head=False)
            stream(5)
            stream(6)
            sp.wait_ge(S["xrow_ready"], 6)
            sp.dma_start(sconv_p[0, 0], sstrow[0:SK - 1]).then_inc(S["xtail_out"], 16)
            sp.dma_start(sconv_s[0].rearrange("b k n -> (b k) n"),
                         sstrow[SK - 1:(SK - 1) * (1 + NB)]).then_inc(S["xtail_out"], 16)
            stream(7, rest=False)
            sp.wait_ge(S["xtail_out"], 32)
            sp.wait_ge(S["xbc_ready"], XC + 2)

            def load_state(c):
                sp.dma_start(s0[:, c % 2], s0_d[:, c:c + 1].rearrange("p c b n -> p (c b) n")).then_inc(
                    s0_loaded[c % 2], 16)

            load_state(0)
            load_state(1)
            for c in range(KC):
                sp.wait_ge(bank_free[2], use("ssd", 2, c + c // 4 + 1))
                sp.dma_start(ssm_pd[:, c:c + 1].rearrange("p c n -> p (c n)"), sfin).then_inc(S["sf_out"], 16)
                for b in range(2):
                    sp.wait_ge(bank_free[b], use("ssd", b, 2 * c + 1))
                sp.dma_start(s1_d[:, c:c + 1].rearrange("p c b n -> p (c b) n"), s0[:, c % 2]).then_inc(st_out[c % 2], 16)
                if c % 2 == 1:
                    sp.wait_ge(bank_ready[4], use("ssd", 4, c))
                    u = c // 2
                    unit(*(("gs", "pppp", 1, u) if u < RING else ("so", MIXED, 0, u - RING)))
                if c + 2 < KC:
                    sp.wait_ge(st_out[c % 2], 16 * (c // 2 + 1))
                    load_state(c + 2)
                sp.wait_ge(S["sf_out"], 16 * (c + 1))
                sp.sem_inc(S["sf_free"], 1)
            stream(8, head=False)
            stream(9)
            sp.wait_ge(S["merged"], KC)
            sp.wait_ge(bank_ready[3], use("wo", 3, 3))
            sp.dma_start(wr[:, :, 0:NG], a["w_group_router"][0].rearrange("(k p) n -> p k n", p=P),
                         allow_slow_non_contiguous=True).then_inc(S["wr_loaded"], 16)
            sp.dma_start(wr[:, :, NG:36], a["w_expert_router"][0].rearrange("(k p) n -> p k n", p=P),
                         allow_slow_non_contiguous=True).then_inc(S["wr_loaded"], 16)

            def expert_unit(e, kind, s):
                if kind < 2:
                    src = (wg_e, wu_e)[kind][:, ds(e, 1)].rearrange("p e k n -> p (e k) n")
                    dst = ring[:, s]
                else:
                    src = wd_e[:, ds(e, 1)].rearrange("p e f n -> p (e f) n")
                    dst = ring[:, s].rearrange("p k n -> p (k n)").rearrange("p (f n) -> p f n", f=2)
                sp.dma_start(dst, src).then_inc(slot_loaded[s], 16)

            used_by = [S["g_ready"], S["u_done"], S["ys_done"]]
            ahead = [0, 1, 1]
            for u in range(RING):
                units = PHASES[-1][2]
                slot_used("wo", units, 0, len(units) - RING + u)
                expert_unit(u // 3, u % 3, u)
            for u in range(RING, 12):
                sp.wait_ge(used_by[(u - 4) % 3], (u - 4) // 3 + 1 + ahead[(u - 4) % 3])
                expert_unit(u // 3, u % 3, u % RING)
            with sp.Fori(1, 8) as i:
                for u in range(12):
                    sp.wait_ge(used_by[(u - 4) % 3], i * 4 + ((u - 4) // 3 + 1 + ahead[(u - 4) % 3]))
                    expert_unit(i * 4 + u // 3, u % 3, u % RING)

            sp.wait_ge(S["out_rows"], 12)
            sp.dma_start(y_p[0].rearrange("(q p) n -> p q n", p=P), yrow[:, 0:2]).then_inc(S["out_done"], 16)
            sp.dma_start(y_s.rearrange("b l n -> (b l) n"), yrow[0:NS, 2]).then_inc(S["out_done"], 16)
            sp.wait_ge(S["out_done"], 48)
            sp.wait_ge(S["tail_out"], 128)
            sp.wait_ge(S["state_copy"], 16)
            for par in range(2):
                sp.wait_ge(st_out[par], 128)
            sp.wait_ge(S["sf_out"], 16 * KC)

        @block.gpsimd
        def _(gp):
            gp.dma_start(cconv_s[0, :, 0:CK - 1 - NL], a["state_conf_conv"][0, :, NL:CK - 1]).then_inc(S["state_copy"], 16)
            gp.sem_inc(S["scaled"], 1)
            pool.mark(gp.memset(ones[:], 1.0))
            pool.mark(gp.memset(ident[:], 0.0))
            pool.link(gp, gp.memset(blk[:], 1.0))
            pool.mark(gp.affine_select(out=ident[:], in_=ident[:], compare_op=ALU.not_equal, fill=1.0, base=0,
                                       pattern=[[-1, P]], channel_multiplier=1))
            pool.mark(gp.affine_select(out=upper[:], in_=ones[:], compare_op=ALU.is_ge, fill=0.0, base=0,
                                       pattern=[[1, P]], channel_multiplier=-1))

            def by_seq(dst, src, inner):
                pool.link(gp, gp.affine_select(out=dst, in_=src, compare_op=ALU.is_ge, fill=0.0, base=0,
                                               pattern=[[-NL, NB], [0, inner]], channel_multiplier=1))
                pool.link(gp, gp.affine_select(out=dst, in_=dst, compare_op=ALU.is_ge, fill=0.0, base=NL - 1,
                                               pattern=[[NL, NB], [0, inner]], channel_multiplier=-1))

            blk3 = blk[:].rearrange("p (b l) -> p b l", b=NB)
            by_seq(blk3, blk3, NL)
            pool.link(gp, gp.tensor_copy(seqsel[:], blk3[:, :, 0]))
            pool.link(gp, gp.memset(fold, 0.0))
            for q in range(4):
                pool.link(gp, gp.affine_select(out=fold, in_=fold, compare_op=ALU.not_equal, fill=1.0, base=-32 * q,
                                               pattern=[[-1, NSEQ]], channel_multiplier=1))
            gp.tensor_tensor(ublk[:], blk[:], upper[0:NS, 0:NS], ALU.mult).then_inc(S["consts_ready"], 1)

            for j in range(2):
                gp.wait_ge(bank_free[j], use("glu", j, 2 * GLU_N - 1))
            gp.wait_ge(S["usamp_ready"], 1)
            acc_s = uvs[:, :, :]
            pool.link(gp, gp.tensor_copy(acc_s, bc(CONF_B, NS)))
            for k in range(CK):
                w = vcol[:, CW0 + k * KC:CW0 + (k + 1) * KC]
                pool.link(gp, gp.tensor_tensor(bl(tmpc), usamp[:, :, :, k:k + NL], bc(w, NB, NL), ALU.mult))
                pool.link(gp, gp.tensor_tensor(acc_s, acc_s, tmpc, ALU.add))
            gp.tensor_copy(vb[:, :, NP:T], acc_s).then_inc(S["vsamp_ready"], 1)

            gp.wait_ge(S["w_ready"], 1)
            gp.wait_ge(S["xtail_out"], 32)
            gp.wait_ge(S["xbc_ready"], XC + 2)
            with gp.Fori(0, G) as g:
                for k in range(4):
                    par = k % 2
                    gp.wait_ge(bank_ready[2], g * 5 + (use("ssd", 2) + k))
                    gp.tensor_copy(dax[0:NS].rearrange("p (h q) -> p h q", h=2),
                                   bc(dtA[0:NS, 2, ds(g * 8 + 2 * k, 2)], HD)).then_inc(S["dax_ready"], 1)
                    for h in range(2):
                        head = g * 8 + (2 * k + h)
                        if h == 0:
                            gp.wait_ge(bank_ready[6], g * 4 + (use("ssd", 6) - 1 + k))
                        else:
                            gp.wait_ge(bank_ready[5], g * 4 + (use("ssd", 5) + k))
                        gp.tensor_tensor(ud[:, 0:NP].rearrange("p (q i) -> p q i", q=2),
                                         upper[:].unsqueeze(1).broadcast_to([P, 2, P]),
                                         dtA[:, 0:2, ds(head, 1)].broadcast_to([P, 2, P]),
                                         ALU.mult).then_inc(S["ud_ready"], 1)
                        gp.tensor_tensor(ud[0:NS, NP:T], ublk[:],
                                         dtA[0:NS, 2, ds(head, 1)].broadcast_to([NS, NS]),
                                         ALU.mult).then_inc(S["ud_ready"], 1)
                    gp.wait_ge(bank_ready[1], g * 8 + (use("ssd", 1) + 2 * k))
                    gp.wait_ge(bank_free[2], g * 5 + (use("ssd", 2) + 1 + k))
                    gp.tensor_tensor(s0[:, par], s0[:, par], bc(dec, P), ALU.mult).then_inc(S["scaled"], 1)

            gp.wait_ge(S["merged"], KC)
            gp.wait_ge(bank_ready[3], use("wo", 3, 3))
            for b in (6, 7):
                gp.wait_ge(bank_free[b], use("wo", b, 3))
            for par in range(2):
                gp.wait_ge(st_out[par], 128)
            gp.wait_ge(S["sf_out"], 16 * KC)
            gp.iota(iota_s, pattern=[[1, SLOTS]], base=0, channel_multiplier=0, allow_small_or_imprecise_dtypes=True)
            gp.iota(iota_e, pattern=[[1, NE]], base=0, channel_multiplier=0, allow_small_or_imprecise_dtypes=True)
            gp.affine_select(out=strict, in_=ones[:], compare_op=ALU.is_gt, fill=0.0, base=0,
                             pattern=[[1, P]], channel_multiplier=-1).then_inc(S["pooled"], 1)

        @block.scalar
        def _(ac):
            ac.wait_ge(S["vrow_zero"], 1)
            at = 0
            for tile, at, name, n in ((0, 0, "b_ada", 96), (0, 96, "norm_mix_g", KC), (0, 112, "norm_ffn_g", KC),
                                      (1, 0, "ssd_conv_b", XC), (1, 24, "ssd_norm_g", KC), (1, 40, "conf_conv_b", KC),
                                      (1, 56, "conf_ln_g", KC), (1, 72, "conf_ln_b", KC)):
                ac.dma_start(vrow[at:at + n, tile], a[name][0].rearrange("(r p) -> r p", p=P)).then_inc(S["v_loaded"], 16)
            ac.dma_start(vrow[88:104, 1], a["final_norm_g"].rearrange("(r p) -> r p", p=P)).then_inc(S["v_loaded"], 16)
            ac.dma_start(vrow[0:96, 2], a["ssd_conv_w"][0].rearrange("k (r p) -> (k r) p", p=P)).then_inc(S["v_loaded"], 16)
            cw = a["conf_conv_w"][0].rearrange("k (r p) -> (k r) p", p=P)
            for t_ in range(4):
                n = min(P, CK * KC - P * t_)
                ac.dma_start(vrow[0:n, 3 + t_], cw[P * t_:P * t_ + n]).then_inc(S["v_loaded"], 16)
            for half in range(2):
                ac.dma_start(cstrow[0:120, half],
                             a["state_conf_conv"][0, 4 * half:4 * half + 4].rearrange("b k n -> (b k) n")).then_inc(
                                 S["cst_loaded"], 16)
                ac.dma_start(dcol[HD * half:HD * half + HD, :],
                             a["ssd_d"][0].rearrange("(c h) -> h c", h=2)[half:half + 1].broadcast_to([HD, KC]),
                             allow_slow_non_contiguous=True).then_inc(S["small_loaded"], 16)
            ac.dma_start(rows_bc[:, 0], a["ssd_dt_bias"].broadcast_to([P, H])).then_inc(S["small_loaded"], 16)
            ac.dma_start(rows_bc[:, 1], a["ssd_a_log"].broadcast_to([P, H])).then_inc(S["small_loaded"], 16)
            ac.dma_start(rbias[:, 0:NG], a["b_group_router"].broadcast_to([P, NG])).then_inc(S["small_loaded"], 16)
            ac.dma_start(rbias[:, NG:36], a["b_expert_router"].broadcast_to([P, NE])).then_inc(S["small_loaded"], 16)

            ac.sem_inc(S["sil_ready"], 1)
            ac.sem_inc(S["xbc_ready"], 1)
            ac.wait_ge(bank_ready[4], use("c", 4))
            ac.activation(cT.rearrange("p k n -> p (k n)"), bank[4][:, 0:KC * NSEQ], ACT.Silu).then_inc(bank_free[4], 1)

            def walk(name, part, on_unit=None):
                steps, units = {n: (s_, u_) for n, s_, u_ in PHASES}[name]
                na = units.count("a")

                def modulation(i, n):
                    b = 6 + n % 2
                    ac.wait_ge(bank_ready[b], i * (na // 2) + use(name, b, n // 2))
                    for j in range(2):
                        c = i * (2 * na) + (2 * (ada0[name] + n) + j)
                        ins = ac.activation(mod[:, ds(c, 1)].rearrange("p k n -> p (k n)"),
                                            bank[b][:, NSEQ * j:NSEQ * (j + 1)], ACT.Identity, bias=vcol[:, ds(c, 1)])
                    ins.then_inc(bank_free[b], 1)

                with steps_of(ac, steps) as i:
                    owed = None
                    for u, kind in enumerate(units):
                        n, b, k, per = place(units, u)
                        if kind == "a":
                            ac.wait_ge(bank_ready[b], i * per + use(name, b, k))
                            ac.wait_ge(bank_ready[b + 2], i * per + (use(name, b + 2, k) - 1))
                            for q in range(4):
                                rows = slice(32 * q, 32 * q + NSEQ)
                                ins = ac.activation(part[rows, n % 2], bank[b][rows, 0:UC], ACT.Copy)
                            ins.then_inc(bank_free[b], 1)
                        elif on_unit:
                            on_unit(i, n)
                        if owed is not None:
                            modulation(i, owed)
                        owed = n if kind == "a" else None
                    if owed is not None:
                        modulation(i, owed)

            def square(src, dst, of_quarter=None, done=0):
                for q in range(4):
                    if of_quarter:
                        ac.wait_ge(S[of_quarter[0]], done + of_quarter[1] * (q + 1))
                    ac.activation(dst[:, 4 * q:4 * q + 4], src[:, 4 * q:4 * q + 4], ACT.Square).then_inc(
                        S["squares_ready"], 1)

            def root(n, src=stat, dst=rs):
                ac.wait_ge(S["mean_ready"], n)
                ac.activation(dst[:], src[:], ACT.Sqrt).then_inc(S["root_ready"], 1)

            for b in range(4):
                ac.wait_ge(bank_free[b], use("x", b, 3))
            square(xT, sq)
            root(1)
            ac.wait_ge(S["part_zero"], 1)
            walk("ada", part_glu)

            def modulate_prompt(n, shift):
                ac.wait_ge(S["scale_ready"], n + 1)
                for c in range(KC):
                    if c % 4 == 0:
                        ac.wait_ge(S["hn_ready"], 4 * n + c // 4 + 1)
                    ac.activation(hT[:, c, 0:NP], hT[:, c, 0:NP], ACT.Identity, scale=scaleA[:, c, 0:1],
                                  bias=mod[:, shift + c, 0:1]).then_inc(S["h_ready"], 1)

            modulate_prompt(0, 0)

            def glu_gate(i, u):
                if u % 2 == 0:
                    return
                q = u // 2
                for j in range(2):
                    n = 2 * (q % 2) + j
                    ac.wait_ge(bank_ready[2 + j], i * 4 + (use("glu", 2 + j) + q))
                    ac.wait_ge(bank_free[j], i * 4 + (use("glu", j) - 2 + q))
                    ac.activation(sgl[:, n], bank[2 + j][:, 0:T], ACT.Sigmoid).then_inc(bank_free[2 + j], 1)

            def to_buffer(name, dst, func):
                def on_unit(i, u):
                    for j in range(2):
                        c = 2 * u + j
                        b = c % 4
                        ac.wait_ge(bank_ready[b], use(name, b, c // 4))
                        ac.activation(dst[:, c], bank[b][:, 0:T], func).then_inc(bank_free[b], 1)
                return on_unit

            walk("glu", part_glu, glu_gate)
            for q in range(4):
                ac.wait_ge(bank_ready[4 + q], use("tail", 4 + q))
                act.mark(ac.activation(tailrow[0:CK - 1 + NS, 512 * q:512 * q + 512], bank[4 + q][0:CK - 1 + NS], ACT.Copy))
                act.wait(ac)
                ac.sem_inc(bank_free[4 + q], 1)
                ac.sem_inc(S["tail_rows"], 1)
            ac.wait_ge(S["part_zero"], 2)
            walk("gc", part_mix, to_buffer("gc", gb, ACT.Sigmoid))
            ac.wait_ge(S["tail_out"], 128)
            ac.wait_ge(S["out_done"], 16)
            square(vb, sq_ln, ("centred", 1))
            walk("z1", part_mix, to_buffer("z1", zb, ACT.Silu))
            root(2)
            for c in range(KC):
                if c % 4 == 0:
                    ac.wait_ge(S["v_ready"], c // 4 + 1)
                ac.activation(vb[:, c], vb[:, c], ACT.Silu, bias=LN_B[:, c:c + 1], scale=LN_G[:, c:c + 1]).then_inc(
                    S["vb_free"], 1)
            ac.wait_ge(S["small_loaded"], 96)
            ac.activation(rows_bc[:, 1], rows_bc[:, 1], ACT.Exp).then_inc(S["a_exp"], 1)
            ac.wait_ge(S["dt_abs"], 1)
            ac.activation(sp_e, sp_abs, ACT.Exp, scale=-1.0).then_inc(S["dt_exp"], 1)
            ac.wait_ge(S["one_plus"], 1)
            ac.activation(sp_ln, sp_u, ACT.Ln).then_inc(S["dt_log"], 1)
            walk("co", part_mix)
            ac.wait_ge(S["w_arg"], 1)
            ac.activation(wend[:], wend[:], ACT.Exp).then_inc(S["w_exp"], 1)
            with ac.Fori(0, XBC_N) as i:
                for c in range(8):
                    ac.wait_ge(S["acc_ready"], i * 8 + c + 1)
                    ac.activation(xbcT[:, ds(i * 8 + c, 1), 0:NP].rearrange("p k n -> p (k n)"), acc[:, c % 2],
                                  ACT.Silu, bias=vcol[:, ds(P + i * 8 + c, 1)]).then_inc(S["xbc_ready"], 1)
            ac.wait_ge(S["xpad_ready"], 1)
            ac.activation(xbcT[:, :, NP:T], tmps, ACT.Silu).then_inc(S["xbc_ready"], 1)
            def xtail_rows():
                for n in range(6):
                    b = 4 + n % 4
                    ac.wait_ge(bank_ready[b], use("xtail", b, n // 4))
                    act.mark(ac.activation(sstrow[0:(SK - 1) * (1 + NB), 512 * n:512 * n + 512],
                                           bank[b][0:(SK - 1) * (1 + NB)], ACT.Copy))
                    act.wait(ac)
                    ac.sem_inc(bank_free[b], 1)
                    ac.sem_inc(S["xrow_ready"], 1)

            z2_silu = to_buffer("z2", zb[:, KC // 2:], ACT.Silu)

            def z2_unit(i, n):
                if n == 2:
                    xtail_rows()
                z2_silu(i, n)

            walk("z2", None, z2_unit)

            ac.wait_ge(S["xtail_out"], 32)
            ac.wait_ge(S["xbc_ready"], XC + 2)

            def copy_x(g, k, transposed):
                ac.wait_ge(bank_ready[3], transposed)
                ac.activation(xst, xbcT[:, ds(g * 4 + k, 1)].rearrange("p k n -> p (k n)"), ACT.Copy).then_inc(
                    S["xst_ready"], 1)

            def copy_b(g):
                ac.activation(bst, xbcT[:, ds(KC + g, 1)].rearrange("p k n -> p (k n)"), ACT.Copy).then_inc(
                    S["bst_ready"], 1)

            ac.sem_inc(S["sf_free"], 1)
            copy_b(0)
            copy_x(0, 0, use("ssd", 3) - 1)
            with ac.Fori(0, G) as g:
                for k in range(4):
                    ac.wait_ge(bank_ready[7], g * 4 + (use("ssd", 7) - 1 + k))
                    for b in range(2):
                        ac.wait_ge(bank_ready[b], g * 8 + (use("ssd", b) + 2 * k))
                        ac.activation(s0T[:, 4 * b:4 * b + 4], bank[b][:].rearrange("p (b n) -> p b n", b=4),
                                      ACT.Copy).then_inc(bank_free[b], 1)
                    for h in range(2):
                        ac.wait_ge(S["seg_ready"], g * 8 + (2 * k + h + 1))
                        ac.activation(mt[:, h, 0:NP], mt[:, h, 0:NP], ACT.Exp)
                        ac.activation(mt[0:NS, h, NP:T], mt[0:NS, h, NP:T], ACT.Exp).then_inc(S["exp_ready"], 1)
                        ac.activation(cs[:, h], bank[5 + h][:, P:T], ACT.Exp).then_inc(bank_free[5 + h], 1)
                    if k == 3:
                        copy_b(g + 1)
                    ac.wait_ge(bank_ready[2], g * 5 + (use("ssd", 2) + 1 + k))
                    ac.wait_ge(S["sf_free"], g * 4 + (k + 1))
                    ac.wait_ge(S["scaled"], g * 4 + k + 1)
                    ac.activation(s1T, bank[2][:, 0:P], ACT.Copy)
                    ac.activation(sfin, bank[2][:, P:2 * P], ACT.Copy)
                    ac.activation(dec, bank[2][:, 2 * P:2 * P + NB], ACT.Exp).then_inc(bank_free[2], 1)
                    copy_x(g, k + 1, g * 5 + (use("ssd", 3) + 1 + k))
                    ac.wait_ge(bank_ready[4], g * 4 + (use("ssd", 4) + k))
                    ac.wait_ge(S["y_done"], g * 4 + (k + 1))
                    ac.sem_inc(S["x_used"], 1)
                    ac.activation(vb[:, ds(g * 4 + k, 1)].rearrange("p k n -> p (k n)"), bank[4][:, 0:T],
                                  ACT.Sigmoid).then_inc(bank_free[4], 1)
            ac.wait_ge(S["y_done"], KC)
            for q in range(4):
                ac.activation(hT[:, 4 * q:4 * q + 4], zb[:, 4 * q:4 * q + 4], ACT.Square).then_inc(S["gsq_ready"], 1)
            for q in range(4):
                ac.wait_ge(S["gmean_ready"], q + 1)
                ac.activation(grs[:, q], grs[:, q], ACT.Sqrt).then_inc(S["groot_ready"], 1)
            for q in range(4):
                ac.wait_ge(bank_ready[4 + q], use("gn", 4 + q))
            ac.wait_ge(S["part_zero"], 3)
            walk("so", part_mix)
            walk("wo", part_mix)
            ac.wait_ge(S["merged"], KC)
            square(xT, sq, ("x_mid", 4))
            root(3)
            modulate_prompt(1, 3 * KC)
            ac.wait_ge(S["e_arg"], 1)
            ac.activation(lg[:, :, 0:NG], lg[:, :, 0:NG], ACT.Exp).then_inc(S["gexp"], 1)
            ac.wait_ge(S["e_arg"], 2)
            ac.activation(sel[:], sel[:], ACT.Exp).then_inc(S["eexp"], 1)
            for c in range(KC):
                ac.wait_ge(bank_ready[4 + c % 2], use("gather", 4 + c % 2, c // 2))
                if c >= 2:
                    ac.wait_ge(bank_ready[2 * (c % 2) + 1], use("gather", 2 * (c % 2) + 1, c // 2 - 1))
                ac.activation(htok[:, c % 2, 0:2 * P], bank[4 + c % 2][:, 0:2 * P], ACT.Copy)
                ac.activation(htok[0:NS, c % 2, 2 * P:3 * P], bank[4 + c % 2][0:NS, 2 * P:3 * P], ACT.Copy).then_inc(
                    bank_free[4 + c % 2], 1)
            with ac.Fori(0, 8) as i:
                for k in range(4):
                    ac.wait_ge(S["g_ready"], i * 4 + (k + 1))
                    ac.wait_ge(S["hid_ready"], i * 4 + (k + 1))
                    n_pairs = ac.value_load(meta_i[0:1, 0, ds(i * 4 + k, 1)], min_val=0, max_val=T)
                    with ac.If(n_pairs > WIN):
                        ac.activation(sil[:, 0], bank[4][:, 0:T], ACT.Silu)
                        ac.activation(sil[:, 1], bank[6][:, 0:T], ACT.Silu).then_inc(S["sil_ready"], 1)
                    with ac.Else():
                        ac.activation(sil[:, 0, 0:P], bank[4][:, 0:P], ACT.Silu).then_inc(S["sil_ready"], 1)
            for c in range(KC):
                for b in range(2):
                    n = (3, 2)[b]
                    bb = 4 + 2 * (c % 2) + b
                    ac.wait_ge(bank_ready[bb], use("unsort", bb, c // 2))
                    if c >= 2:
                        ac.wait_ge(bank_ready[(c - 2) % 4], use("unsort", (c - 2) % 4, (c - 2) // 4))
                    if b == 0:
                        ac.activation(ytok[:, c % 2, 0:3 * P], bank[bb][:, 0:3 * P], ACT.Copy).then_inc(bank_free[bb], 1)
                    else:
                        ac.activation(ytok[:, c % 2, 3 * P:4 * P], bank[bb][:, 0:P], ACT.Copy)
                        ac.activation(ytok[0:HD, c % 2, 4 * P:5 * P], bank[bb][0:HD, P:2 * P], ACT.Copy).then_inc(
                            bank_free[bb], 1)
            square(xT, hT, ("moe_ready", 4))
            root(4)
            for n in range(12):
                b = 4 + n % 4
                rows, q, c4 = (P, P, NS)[n // 4], n // 4, n % 4
                ac.wait_ge(bank_ready[b], use("y", b, n // 4))
                act.mark(ac.activation(yrow[0:rows, q, 512 * c4:512 * c4 + 512], bank[b][0:rows], ACT.Copy))
                act.wait(ac)
                ac.sem_inc(bank_free[b], 1)
                ac.sem_inc(S["out_rows"], 1)

        @block.tensor
        def _(pe):
            def fill(name, b, k=0):
                pe.wait_ge(bank_free[b], use(name, b, k) - 1)

            def project(name, rhs=None, before=None):
                steps, units = {n: (s_, u_) for n, s_, u_ in PHASES}[name]

                def fold_sums(i, n):
                    b = 6 + n % 2
                    per = units.count("a") // 2
                    pe.wait_ge(bank_free[b - 2], i * per + use(name, b - 2, n // 2))
                    pe.wait_ge(bank_free[b], i * per + (use(name, b, n // 2) - 1))
                    part = part_glu if name in ("ada", "glu") else part_mix
                    for j in range(2):
                        mm = nc.tensor.matmul(bank[b][:, NSEQ * j:NSEQ * (j + 1)], part[:, n % 2, j * P:(j + 1) * P],
                                              fold, start=True, stop=True)
                    mm.then_inc(bank_ready[b], 1)

                with steps_of(pe, steps) as i:
                    owed = None
                    for u, kind in enumerate(units):
                        if before:
                            before(u)
                        s, r = u % RING, u // RING
                        n, last, k, per = place(units, u)
                        pe.wait_ge(slot_loaded[s], i * (16 * len(units) // RING) + 16 * (ring0[name] + r + 1))
                        if kind == "p":
                            for j in range(2):
                                c = 2 * n + j
                                b = c % 4
                                pe.wait_ge(bank_free[b], i * per + (use(name, b, c // 4) - 1))
                                for kk in range(KC):
                                    mm = nc.tensor.matmul(bank[b][:, 0:T], ring[:, s, kk, j * P:(j + 1) * P], rhs[:, kk],
                                                          start=(kk == 0), stop=(kk == KC - 1))
                                mm.then_inc(bank_ready[b], 1)
                        else:
                            pe.wait_ge(bank_free[last], i * per + (use(name, last, k) - 1))
                            for kk in range(KC):
                                q = kk % 4
                                mm = nc.tensor.matmul(bank[last][32 * q:32 * q + NSEQ, 0:UC], cT[:, kk], ring[:, s, kk],
                                                      start=(kk < 4), stop=(kk >= KC - 4))
                            mm.then_inc(bank_ready[last], 1)
                        if owed is not None:
                            fold_sums(i, owed)
                        owed = n if kind == "a" else None
                    if owed is not None:
                        fold_sums(i, owed)

            def ones_sum(name, src, b, chunks, squares=None):
                fill(name, b)
                for n, c in enumerate(chunks):
                    if squares is not None and c % 4 == 0:
                        pe.wait_ge(S["squares_ready"], squares + c // 4 + 1)
                    mm = nc.tensor.matmul(bank[b][:, 0:T], ones[:], src[:, c], start=(n == 0), stop=(n == len(chunks) - 1))
                mm.then_inc(bank_ready[b], 1)

            pe.sem_inc(S["u_done"], 1)
            pe.wait_ge(S["consts_ready"], 1)
            pe.wait_ge(S["x_loaded"], 32)
            for c in range(KC):
                b = c % 4
                fill("x", b, c // 4)
                for q, (t0, rows) in enumerate(TOK):
                    mm = nc.tensor.transpose(bank[b][:, t0:t0 + rows], xrow[0:rows, q, c * P:(c + 1) * P],
                                             ident[0:rows, 0:rows])
                mm.then_inc(bank_ready[b], 1)
            pe.wait_ge(S["c_loaded"], 32)
            fill("c", 4)
            for c in range(KC):
                mm = nc.tensor.transpose(bank[4][:, NSEQ * c:NSEQ * (c + 1)], crow[0:NSEQ, c * P:(c + 1) * P],
                                         ident[0:NSEQ, 0:NSEQ])
            mm.then_inc(bank_ready[4], 1)
            pe.wait_ge(S["v_loaded"], 14 * 16)
            for b, tiles in ((5, range(4)), (6, range(4, 7))):
                fill("vec", b)
                for n, t_ in enumerate(tiles):
                    mm = nc.tensor.transpose(bank[b][:, n * P:(n + 1) * P], vrow[:, t_], ident[:])
                mm.then_inc(bank_ready[b], 1)
            pe.wait_ge(S["cst_loaded"], 32)
            for c in range(KC):
                b = 4 + c % 4
                fill("cst", b, c // 4)
                for half in range(2):
                    mm = nc.tensor.transpose(bank[b][:, 120 * half:120 * half + 120],
                                             cstrow[0:120, half, c * P:(c + 1) * P], ident[0:120, 0:120])
                mm.then_inc(bank_ready[b], 1)
            pe.wait_ge(bank_free[4], use("c", 4))
            ones_sum("n1", sq, 4, range(KC), squares=0)
            project("ada")
            pe.wait_ge(S["h_ready"], KC)
            pe.wait_ge(S["hs_ready"], 4)
            project("glu", hT)
            for j in range(2):
                pe.wait_ge(bank_free[j], use("glu", j, 2 * GLU_N - 1))
            for q in range(4):
                fill("tail", 4 + q)
                for n in range(4):
                    mm = nc.tensor.transpose(bank[4 + q][0:CK - 1 + NS, n * P:(n + 1) * P], utail[:, 4 * q + n], ident[:])
                mm.then_inc(bank_ready[4 + q], 1)
            project("gc", hT)
            pe.wait_ge(S["conv_ready"], 1)
            pe.wait_ge(S["vsamp_ready"], 1)
            ones_sum("ln", vb, 4, range(KC))
            project("z1", hT)
            ones_sum("lnsq", sq_ln, 5, range(KC), squares=4)
            pe.wait_ge(S["wdt_loaded"], 16)
            fill("dt", 6)
            for q, (t0, rows) in enumerate(TOK):
                for k in range(KC):
                    mm = nc.tensor.matmul(bank[6][0:rows, H * q:H * (q + 1)], hT[:, k, t0:t0 + rows], wdt[:, k],
                                          start=(k == 0), stop=(k == KC - 1))
            mm.then_inc(bank_ready[6], 1)
            pe.wait_ge(S["vb_free"], KC)
            project("co", vb)
            pe.wait_ge(S["dta_ready"], 1)
            fill("cum", 7)
            for q, (lhs, rows) in enumerate(((upper[:], P), (upper[:], P), (ublk[:], NS))):
                nc.tensor.matmul(bank[7][0:rows, H * q:H * (q + 1)], lhs, dtA[0:rows, q], start=True, stop=True)
            for q, (lhs, rows) in enumerate(((ones[:], P), (ones[:], P), (blk[:], NS))):
                mm = nc.tensor.matmul(bank[7][0:rows, H * (3 + q):H * (4 + q)], lhs, dtA[0:rows, q], start=True, stop=True)
            mm.then_inc(bank_ready[7], 1)
            pe.wait_ge(S["sst_loaded"], 16)
            R = NB * (SK - 1)
            for half in range(2):
                fill("sst", 4 + half)
                for n in range(12):
                    c = 12 * half + n
                    mm = nc.tensor.transpose(bank[4 + half][:, R * n:R * (n + 1)], sstrow[0:R, c * P:(c + 1) * P],
                                             ident[0:R, 0:R])
                mm.then_inc(bank_ready[4 + half], 1)
            project("xbc", hT)
            def xtail_to_rows(u):
                if u != 2:
                    return
                pe.wait_ge(S["xtail_ready"], 1)
                R = (SK - 1) * (1 + NB)
                for n in range(6):
                    b = 4 + n % 4
                    fill("xtail", b, n // 4)
                    for j in range(4):
                        mm = nc.tensor.transpose(bank[b][0:R, j * P:(j + 1) * P], xtail[:, 4 * n + j], ident[:])
                    mm.then_inc(bank_ready[b], 1)

            project("z2", hT, before=xtail_to_rows)

            pe.wait_ge(S["w_ready"], 1)
            pe.wait_ge(S["xbc_ready"], XC + 2)
            def of(g, per, at):
                return g[0] * (2 * per) + (g[1] * per + at)

            with pe.Fori(0, G // 2) as i:
                for gg in range(2):
                    g = (i, gg)
                    pe.wait_ge(S["bst_ready"], of(g, 1, 1))
                    pe.wait_ge(bank_free[3], of(g, 5, use("ssd", 3) - 1))
                    for q, (t0, rows) in enumerate(TOK):
                        mm = nc.tensor.matmul(bank[3][0:rows, q * P:q * P + rows], bst[:, t0:t0 + rows],
                                              xbcT[:, ds(of(g, 1, KC + G), 1), t0:t0 + rows].rearrange("p k n -> p (k n)"),
                                              start=True, stop=True)
                    mm.then_inc(bank_ready[3], 1)
                    pe.wait_ge(bank_free[2], of(g, 5, use("ssd", 2) - 1))
                    for q, (t0, rows) in enumerate(TOK):
                        mm = nc.tensor.transpose(bank[2][0:rows, q * P:(q + 1) * P], bst[:, t0:t0 + rows], ident[:])
                    mm.then_inc(bank_ready[2], 1)
                    for k in range(4):
                        par = k % 2
                        pe.wait_ge(S["xst_ready"], of(g, 4, k + 1))
                        pe.wait_ge(bank_free[3], of(g, 5, use("ssd", 3) + k))
                        for q, (t0, rows) in enumerate(TOK):
                            mm = nc.tensor.transpose(bank[3][0:rows, q * P:(q + 1) * P], xst[:, t0:t0 + rows], ident[:])
                        mm.then_inc(bank_ready[3], 1)
                        pe.wait_ge(s0_loaded[par], of(g, 32, 16 * (k // 2) + 16))
                        for b in range(2):
                            pe.wait_ge(bank_free[b], of(g, 8, use("ssd", b) - 1 + 2 * k))
                            for n in range(4):
                                mm = nc.tensor.transpose(bank[b][:, n * P:(n + 1) * P], s0[:, par, 4 * b + n], ident[:])
                            mm.then_inc(bank_ready[b], 1)
                        for h in range(2):
                            pe.wait_ge(S["ud_ready"], of(g, 16, 4 * k + 2 * h + 2))
                            pe.wait_ge(bank_free[5 + h], of(g, 4, use("ssd", 5 + h) - 1 + k))
                            nc.tensor.matmul(bank[5 + h][:, 0:NP], ones[:], ud[:, 0:NP], start=True, stop=True)
                            nc.tensor.matmul(bank[5 + h][:, NP:T], ones[0:NS, :], ud[0:NS, NP:T],
                                             start=True, stop=True).then_inc(bank_ready[5 + h], 1)
                        if k % 2 == 0:
                            pe.wait_ge(slot_loaded[2 * gg + k // 2], i * 16 + 16 * (ring0["gs"] + 1))
                        pe.wait_ge(bank_free[4], of(g, 4, use("ssd", 4) - 1 + k))
                        for kk in range(KC):
                            mm = nc.tensor.matmul(bank[4][:, 0:T], ring[:, 2 * gg + k // 2, kk, par * P:(par + 1) * P],
                                                  hT[:, kk], start=(kk == 0), stop=(kk == KC - 1))
                        mm.then_inc(bank_ready[4], 1)
                        pe.wait_ge(S["xw_ready"], of(g, 4, k + 1))
                        pe.wait_ge(S["dax_ready"], of(g, 4, k + 1))
                        pe.wait_ge(bank_free[2], of(g, 5, use("ssd", 2) + k))
                        nc.tensor.matmul(bank[2][:, 0:P], btok[:, 0], xw[:, 0], start=True, stop=True)
                        nc.tensor.matmul(bank[2][:, P:2 * P], xw[:, 1], btok[:, 0], start=True, stop=False)
                        nc.tensor.matmul(bank[2][:, P:2 * P], xw[:, 2], btok[:, 1], start=False, stop=True)
                        nc.tensor.matmul(bank[2][:, 2 * P:2 * P + NB], dax[0:NS], seqsel[:], start=True,
                                         stop=True).then_inc(bank_ready[2], 1)
                        pe.wait_ge(S["bexp_ready"], of(g, 1, 1))
                        for b in range(2):
                            pe.wait_ge(bank_free[b], of(g, 8, use("ssd", b) + 2 * k))
                            nc.tensor.matmul(bank[b][:], xw[0:NS, 3], bexp[0:NS, 4 * b:4 * b + 4], start=True,
                                             stop=True).then_inc(bank_ready[b], 1)
                        pe.wait_ge(S["m_ready"], of(g, 8, 2 * k + 2))
                        pe.wait_ge(bank_free[2], of(g, 5, use("ssd", 2) + 1 + k))
                        pe.wait_ge(bank_free[7], of(g, 4, use("ssd", 7) - 1 + k))
                        for h in range(2):
                            hc = slice(HD * h, HD * (h + 1))
                            y = bank[7][hc]
                            nc.tensor.matmul(y[:, 0:P], xtok[:, 0, hc], mt[:, h, 0:P], start=True, stop=True)
                            nc.tensor.matmul(y[:, P:NP], xtok[:, 1, hc], mt[:, h, P:NP], start=True, stop=False)
                            nc.tensor.matmul(y[:, P:NP], s1T[:, hc], cs[:, h, 0:P], start=False, stop=True)
                            nc.tensor.matmul(y[:, NP:T], xtok[0:NS, 2, hc], mt[0:NS, h, NP:T], start=True, stop=True)
                            for b in range(NB):
                                mm = nc.tensor.matmul(y[:, NP + NL * b:NP + NL * (b + 1)], s0T[:, b, hc],
                                                      cs[:, h, P + NL * b:P + NL * (b + 1)], start=False,
                                                      stop=True, skip_group_check=True)
                        mm.then_inc(bank_ready[7], 1)
            for q in range(G):
                pe.wait_ge(S["gsq_ready"], q + 1)
                ones_sum("gn", hT, 4 + q, range(4 * q, 4 * q + 4))
            pe.wait_ge(S["y_ready"], 1)
            project("so", zb)
            pe.wait_ge(S["merged"], KC)
            project("wo", gb)
            ones_sum("n2", sq, 4, range(KC), squares=8)
            pe.wait_ge(S["wr_loaded"], 32)
            fill("route", 5)
            for q, (t0, rows) in enumerate(TOK):
                if q == 2:
                    pe.wait_ge(S["hs_ready"], 8)
                for k in range(KC):
                    if q == 0 and k % 4 == 0:
                        pe.wait_ge(S["h_ready"], KC + k + 4)
                    mm = nc.tensor.matmul(bank[5][0:rows, 36 * q:36 * (q + 1)], hT[:, k, t0:t0 + rows], wr[:, k],
                                          start=(k == 0), stop=(k == KC - 1))
            mm.then_inc(bank_ready[5], 1)
            pe.wait_ge(S["cnt_ready"], 1)
            pe.wait_ge(S["pooled"], 1)
            fill("route", 6)
            for q, (t0, rows) in enumerate(TOK):
                mm = nc.tensor.matmul(bank[6][0:NE, 0:1], chosen[0:rows, q], ones[0:rows, 0:1], start=(q == 0), stop=(q == 2))
            mm.then_inc(bank_ready[6], 1)
            pe.wait_ge(S["cnt_ready"], 2)
            fill("route", 7)
            for q, (t0, rows) in enumerate(TOK):
                out = bank[7][0:rows, NE * q:NE * (q + 1)]
                nc.tensor.matmul(out, cntb[0:NE, 0:rows], strict[0:NE, 0:NE], start=True, stop=False)
                for q2 in range(q):
                    nc.tensor.matmul(out, ones[:, 0:rows], chosen[:, q2], start=False, stop=False)
                nc.tensor.matmul(out, strict[0:rows, 0:rows], chosen[0:rows, q], start=False, stop=True)
            nc.tensor.matmul(bank[7][:, 96:128], cntb[0:NE], strict[0:NE, 0:NE], start=True, stop=True)
            nc.tensor.matmul(bank[7][:, 128:160], cntb[0:NE], ident[0:NE, 0:NE], start=True, stop=True).then_inc(
                bank_ready[7], 1)
            pe.wait_ge(S["sort_ready"], 1)
            for b in range(4):
                fill("gates", b)
                src = (gt, et)[b // 2]
                for q, (t0, rows) in enumerate(TOK):
                    mm = nc.tensor.matmul(bank[b][:, 0:T], ones[0:rows, :], src[0:rows, q, T * (b % 2):T * (b % 2 + 1)],
                                          start=(q == 0), stop=(q == 2))
                mm.then_inc(bank_ready[b], 1)

            def to_rows(c):
                b = 4 + c % 2
                fill("gather", b, c // 2)
                for q, (t0, rows) in enumerate(TOK):
                    mm = nc.tensor.transpose(bank[b][0:rows, q * P:(q + 1) * P], hT[:, c, t0:t0 + rows], ident[:])
                mm.then_inc(bank_ready[b], 1)

            to_rows(0)
            for c in range(KC):
                if c + 1 < KC:
                    to_rows(c + 1)
                pe.wait_ge(bank_free[4 + c % 2], use("gather", 4 + c % 2, c // 2))
                for half in range(2):
                    b = 2 * (c % 2) + half
                    fill("gather", b, c // 2)
                    for q, (t0, rows) in enumerate(TOK):
                        mm = nc.tensor.matmul(bank[b][:, 0:T], htok[0:rows, c % 2, q * P:(q + 1) * P],
                                              pm[0:rows, q, T * half:T * (half + 1)], start=(q == 0), stop=(q == 2))
                    mm.then_inc(bank_ready[b], 1)

            for b in range(4):
                fill("unsort", b)
            for b in (4, 5):
                fill("pt", b)
            pe.wait_ge(S["meta_ready"], 1)
            with pe.Fori(0, 8) as i:
                for k in range(4):
                    u = 3 * k
                    slots = [(u + n) % RING for n in range(3)]
                    landed = [i * 48 + (MOE_R + (u + n) // RING + 1) * 16 for n in range(3)]
                    n_pairs = pe.value_load(meta_i[0:1, 0, ds(i * 4 + k, 1)], min_val=0, max_val=T)
                    w_gate, w_up = ring[:, slots[0]], ring[:, slots[1]]
                    w_down = ring[:, slots[2]].rearrange("p k n -> p (k n)").rearrange("p (f n) -> p f n", f=2)
                    pe.wait_ge(slot_loaded[slots[0]], landed[0])
                    pe.wait_ge(S["win_ready"], i * 4 + (k + 1))
                    pe.wait_ge(S["sil_ready"], i * 4 + (k + 1))
                    with pe.If(n_pairs > WIN):
                        w0 = pe.value_load(meta_i[0:1, 2, ds(i * 4 + k, 1)], min_val=0, max_val=SLOTS - T)
                        for n, (w, done, gone) in enumerate(((w_gate, "g_ready", "sil_ready"), (w_up, "u_done", "hid_ready"))):
                            if n:
                                pe.wait_ge(slot_loaded[slots[1]], landed[1])
                                pe.wait_ge(S["hid_ready"], i * 4 + (k + 1))
                            for f in range(2):
                                for kk in range(KC):
                                    mm = nc.tensor.matmul(bank[4 + n + 2 * f][:, 0:T], w[:, kk, f * P:(f + 1) * P],
                                                          hs[:, kk, ds(w0, T)], start=(kk == 0), stop=(kk == KC - 1))
                            mm.then_inc(S[done], 1)
                        pe.wait_ge(slot_loaded[slots[2]], landed[2])
                        pe.wait_ge(S["hid_ready"], i * 4 + (k + 2))
                        pe.wait_ge(S["ys_done"], i * 4 + (k + 1))
                        for c in range(KC):
                            if c >= 4:
                                pe.wait_ge(S["wide_free"], i * 64 + (16 * k + c - 3))
                            for f in range(2):
                                mm = nc.tensor.matmul(bank[c % 4][:, 0:T], w_down[:, f, c * P:(c + 1) * P], hid[:, f],
                                                      start=(f == 0), stop=(f == 1))
                            mm.then_inc(S["wide_ready"], 1)
                        pe.sem_inc(S["d_ready"], 1)
                        pe.sem_inc(S["prod_turned"], 1)
                    with pe.Else():
                        for n, (w, done) in enumerate(((w_gate, "g_ready"), (w_up, "u_done"))):
                            if n:
                                pe.wait_ge(slot_loaded[slots[1]], landed[1])
                                pe.wait_ge(S["hid_ready"], i * 4 + (k + 1))
                            for kk in range(KC):
                                for f in range(2):
                                    mm = nc.tensor.matmul(bank[4 + n][f * WIN:(f + 1) * WIN, 0:P], hwin[:, k % 2, kk],
                                                          w[:, kk, f * P:(f + 1) * P], start=(kk == 0), stop=(kk == KC - 1))
                            mm.then_inc(S[done], 1)
                        pe.wait_ge(S["prod_ready"], i * 4 + (k + 1))
                        nc.tensor.transpose(bank[6][:, 0:P], sil[:, 1, 0:P], ident[:]).then_inc(S["prod_turned"], 1)
                        pe.wait_ge(slot_loaded[slots[2]], landed[2])
                        pe.wait_ge(S["hid_ready"], i * 4 + (k + 2))
                        pe.wait_ge(S["ys_done"], i * 4 + (k + 1))
                        for c in range(KC):
                            for f in range(2):
                                mm = nc.tensor.matmul(bank[c // 4][:, (c % 4) * P:(c % 4 + 1) * P],
                                                      w_down[:, f, c * P:(c + 1) * P], hid[:, f, 0:P],
                                                      start=(f == 0), stop=(f == 1))
                        mm.then_inc(S["d_ready"], 1)
                        pe.sem_inc(S["wide_ready"], 16)

            pe.wait_ge(S["ys_done"], NE + 1)
            PT = [(P * j, min(P, SLOTS - P * j)) for j in range(5)]
            for j, (s_, n) in enumerate(PT):
                b = 4 + j % 2
                fill("pt", b, j // 2)
                for q, (t0, rows) in enumerate(TOK):
                    mm = nc.tensor.transpose(bank[b][0:n, t0:t0 + rows], pm[0:rows, q, s_:s_ + n], ident[0:rows, 0:rows])
                mm.then_inc(bank_ready[b], 1)

            def y_rows(c):
                for half, tiles in ((0, PT[0:3]), (1, PT[3:5])):
                    b = 4 + 2 * (c % 2) + half
                    fill("unsort", b, c // 2)
                    for m, (s_, n) in enumerate(tiles):
                        mm = nc.tensor.transpose(bank[b][0:n, m * P:(m + 1) * P], ys[:, c, s_:s_ + n], ident[:])
                    mm.then_inc(bank_ready[b], 1)

            y_rows(0)
            pe.wait_ge(bank_free[4], use("pt", 4, 2))
            pe.wait_ge(bank_free[5], use("pt", 5, 1))
            for c in range(KC):
                if c + 1 < KC:
                    y_rows(c + 1)
                for half in range(2):
                    b = 4 + 2 * (c % 2) + half
                    pe.wait_ge(bank_free[b], use("unsort", b, c // 2))
                fill("unsort", c % 4, c // 4)
                for j, (s_, n) in enumerate(PT):
                    mm = nc.tensor.matmul(bank[c % 4][:, 0:T], ytok[0:n, c % 2, j * P:(j + 1) * P], pt[0:n, j],
                                          start=(j == 0), stop=(j == 4))
                mm.then_inc(bank_ready[c % 4], 1)
            ones_sum("n3", hT, 4, range(KC), squares=12)
            pe.wait_ge(S["y_fin"], KC)
            for n in range(12):
                q, c4, b = n // 4, n % 4, 4 + n % 4
                t0, rows = TOK[q]
                fill("y", b, n // 4)
                for j in range(4):
                    mm = nc.tensor.transpose(bank[b][0:rows, j * P:(j + 1) * P], xT[:, 4 * c4 + j, t0:t0 + rows], ident[:])
                mm.then_inc(bank_ready[b], 1)

        @block.vector
        def _(ve):
            def flat(ap):
                return ap.rearrange("p k n -> p (k n)")

            def take(name, b, k=0):
                ve.wait_ge(bank_ready[b], use(name, b, k))

            ve.sem_inc(S["hid_ready"], 1)
            ve.sem_inc(S["ys_done"], 1)
            dve.mark(ve.memset(dt_tok[:], 0.0))
            dve.mark(ve.memset(wend[:], 0.0))
            ve.memset(vrow, 0.0).then_inc(S["vrow_zero"], 1)
            for c in range(KC):
                b = c % 4
                take("x", b, c // 4)
                ve.tensor_copy(xT[:, c], bank[b][:, 0:T]).then_inc(bank_free[b], 1)
            take("vec", 5)
            ve.tensor_copy(vcol[:, 0:512], bank[5][:]).then_inc(bank_free[5], 1)
            take("vec", 6)
            ve.tensor_copy(vcol[:, 512:896], bank[6][:, 0:384]).then_inc(bank_free[6], 1)
            for c in range(KC):
                b = 4 + c % 4
                take("cst", b, c // 4)
                ve.tensor_copy(usamp[:, c, :, 0:CK - 1],
                               bank[b][:, 0:240].rearrange("p (b l) -> p b l", b=NB)).then_inc(bank_free[b], 1)
            ve.wait_ge(bank_free[7], use("cst", 7, 3))
            ve.sem_inc(S["usamp_ready"], 1)
            dve.mark(ve.memset(upad[:, :, 0:CK - 1], 0.0))
            dve.link(ve, ve.memset(part_glu, 0.0))
            ve.sem_inc(S["part_zero"], 1)

            def inv_rms(name, b, n, width):
                take(name, b)
                ve.tensor_scalar(stat[:], bank[b][:, 0:T], 1.0 / width, EPS, ALU.mult, ALU.add).then_inc(S["mean_ready"], 1)
                ve.wait_ge(S["root_ready"], n)
                ve.sem_inc(bank_free[b], 1)
                dve.link(ve, ve.reciprocal(rs[:], rs[:]))

            def normalise():
                for q in range(4):
                    dve.link(ve, ve.tensor_tensor(hT[:, 4 * q:4 * q + 4], xT[:, 4 * q:4 * q + 4],
                                                  rs[:].unsqueeze(1).broadcast_to([P, 4, T]), ALU.mult))
                    ve.sem_inc(S["hn_ready"], 1)

            def scales(gvec, scale):
                dve.link(ve, ve.scalar_tensor_tensor(out=scaleA[:], in0=mod[:, scale:scale + KC], scalar=1.0,
                                                     in1=bc(gvec, NSEQ), op0=ALU.add, op1=ALU.mult))
                ve.sem_inc(S["scale_ready"], 1)

            def modulate_samples(shift):
                for q in range(4):
                    c4 = slice(4 * q, 4 * q + 4)
                    hs_ = bl(hT[:, c4, NP:T])
                    dve.link(ve, ve.tensor_tensor(hs_, hs_, bc(scaleA[:, c4, 1:NSEQ], NL), ALU.mult))
                    ve.tensor_tensor(hs_, hs_, bc(mod[:, shift + 4 * q:shift + 4 * q + 4, 1:NSEQ], NL), ALU.add).then_inc(
                        S["hs_ready"], 1)

            inv_rms("n1", 4, 1, D)
            normalise()
            for b in (6, 7):
                ve.wait_ge(bank_free[b], use("ada", b, 7))
            scales(G_MIX, KC)
            modulate_samples(0)

            cacc = [stat, rs]
            with ve.Fori(0, GLU_N) as i:
                with dve.loop(i, GLU_N, 2 * (2 + 2 * CK)):
                    for q in range(2):
                        for j in range(2):
                            n, c = 2 * q + j, i * 4 + (2 * q + j)
                            ve.wait_ge(bank_ready[j], i * 2 + (use("glu", j) + q))
                            ve.wait_ge(bank_free[2 + j], i * 2 + (use("glu", 2 + j) + q))
                            dve.mark(ve.tensor_tensor(upad[:, n, CK - 1:], bank[j][:, 0:NP], sgl[:, n, 0:NP], ALU.mult))
                            ve.tensor_tensor(flat(utail[:, ds(c, 1), 0:CK - 1]), bank[j][:, NP - CK + 1:NP],
                                             sgl[:, n, NP - CK + 1:NP], ALU.mult)
                            ve.tensor_tensor(flat(utail[:, ds(c, 1), CK - 1:]), bank[j][:, NP:T], sgl[:, n, NP:T], ALU.mult)
                            ve.tensor_tensor(usamp[:, ds(c, 1), :, CK - 1:].rearrange("p k b l -> p (k b) l"),
                                             bank[j][:, NP:T].rearrange("p (b l) -> p b l", b=NB),
                                             sgl[:, n, NP:T].rearrange("p (b l) -> p b l", b=NB),
                                             ALU.mult).then_inc(bank_free[j], 1)
                        for k in range(CK):
                            for j in range(2):
                                n, c = 2 * q + j, i * 4 + (2 * q + j)
                                tap = vcol[:, ds(c + (CW0 + k * KC), 1)]
                                u = upad[:, n, k:k + NP]
                                dve.wait(ve, back=1)
                                if k == 0:
                                    ins = ve.tensor_scalar(cacc[j][:, 0:NP], u, tap, vcol[:, ds(c + (P + 40), 1)],
                                                           ALU.mult, ALU.add)
                                else:
                                    out = cacc[j][:, 0:NP] if k < CK - 1 else flat(vb[:, ds(c, 1), 0:NP])
                                    ins = ve.scalar_tensor_tensor(out=out, in0=u, scalar=tap, in1=cacc[j][:, 0:NP],
                                                                  op0=ALU.mult, op1=ALU.add)
                                dve.mark(ins)
            dve.wait(ve)
            ve.sem_inc(S["conv_ready"], 1)

            take("tail", 7)
            dve.link(ve, ve.memset(part_mix, 0.0))
            ve.sem_inc(S["part_zero"], 1)
            take("ln", 4)
            dve.link(ve, ve.tensor_scalar(stat[:], bank[4][:, 0:T], 1.0 / D, None, ALU.mult))
            ve.sem_inc(bank_free[4], 1)
            ve.wait_ge(S["vsamp_ready"], 1)
            for q in range(4):
                v_ = vb[:, 4 * q:4 * q + 4]
                dve.mark(ve.tensor_tensor(v_, v_, stat[:].unsqueeze(1).broadcast_to([P, 4, T]), ALU.subtract))
                dve.wait(ve)
                ve.sem_inc(S["centred"], 1)
            inv_rms("lnsq", 5, 2, D)
            for q in range(4):
                v_ = vb[:, 4 * q:4 * q + 4]
                ve.tensor_tensor(v_, v_, rs[:].unsqueeze(1).broadcast_to([P, 4, T]), ALU.mult).then_inc(S["v_ready"], 1)
            take("dt", 6)
            ve.wait_ge(S["small_loaded"], 96)
            dve.mark(ve.tensor_tensor(dt_tok[:, 0:2], bank[6][:, 0:2 * H].rearrange("p (q h) -> p q h", q=2),
                                      rows_bc[:, 0:1].broadcast_to([P, 2, H]), ALU.add))
            dve.link(ve, ve.tensor_tensor(dt_tok[0:NS, 2], bank[6][0:NS, 2 * H:3 * H], rows_bc[0:NS, 0], ALU.add))
            ve.sem_inc(bank_free[6], 1)
            ve.scalar_tensor_tensor(out=sp_abs, in0=dt_tok[:], scalar=-1.0, in1=dt_tok[:], op0=ALU.mult,
                                    op1=ALU.max).then_inc(S["dt_abs"], 1)
            ve.wait_ge(S["dt_exp"], 1)
            dve.link(ve, ve.tensor_scalar(sp_u, sp_e, 1.0, None, ALU.add))
            ve.sem_inc(S["one_plus"], 1)
            dve.link(ve, ve.tensor_scalar(sp_d, sp_u, -1.0, None, ALU.add))
            dve.link(ve, ve.tensor_scalar(sp_z, sp_d, 0.0, None, ALU.is_equal))
            dve.link(ve, ve.tensor_tensor(sp_z, sp_z, sp_e, ALU.mult))
            dve.link(ve, ve.tensor_scalar(sp_d, sp_d, 1e-30, None, ALU.max))
            dve.link(ve, ve.reciprocal(sp_d, sp_d))
            dve.link(ve, ve.tensor_tensor(sp_m, sp_e, sp_d, ALU.mult))
            ve.wait_ge(S["dt_log"], 1)
            dve.link(ve, ve.tensor_tensor(sp_m, sp_m, sp_ln, ALU.mult))
            dve.link(ve, ve.tensor_tensor(sp_m, sp_m, sp_z, ALU.add))
            dve.link(ve, ve.scalar_tensor_tensor(out=dt_tok[:], in0=dt_tok[:], scalar=0.0, in1=sp_m, op0=ALU.max,
                                                 op1=ALU.add))
            ve.wait_ge(S["a_exp"], 1)
            ve.scalar_tensor_tensor(out=dtA[:], in0=dt_tok[:], scalar=-1.0, in1=rows_bc[:, 1:2].broadcast_to([P, 3, H]),
                                    op0=ALU.mult, op1=ALU.mult).then_inc(S["dta_ready"], 1)
            for b in range(4):
                ve.wait_ge(bank_free[b], use("gc", b, 3))
            with ve.Fori(0, 2) as i:
                for c in range(8):
                    b = c % 4
                    ve.wait_ge(bank_ready[b], i * 2 + (use("co", b) + c // 4))
                    g_ = flat(gb[:, ds(i * 8 + c, 1)])
                    ve.tensor_tensor(g_, g_, bank[b][:, 0:T], ALU.mult).then_inc(bank_free[b], 1)

            take("cum", 7)
            cum = bank[7][:, 0:192].rearrange("p (q h) -> p q h", q=6)
            dve.mark(ve.tensor_copy(acum[:, 0:2], cum[:, 0:2]))
            dve.link(ve, ve.tensor_copy(acum[0:NS, 2], cum[0:NS, 2]))
            dve.mark(ve.tensor_tensor(wend[:, 0], cum[:, 3], acum[:, 0], ALU.subtract))
            dve.mark(ve.tensor_tensor(wend[:, 2], cum[:, 4], acum[:, 1], ALU.subtract))
            dve.link(ve, ve.tensor_tensor(wend[0:NS, 3], cum[0:NS, 5], acum[0:NS, 2], ALU.subtract))
            dve.link(ve, ve.tensor_tensor(wend[:, 1], wend[:, 0], cum[:, 4], ALU.add))
            ve.sem_inc(S["w_arg"], 1)
            ve.sem_inc(bank_free[7], 1)
            ve.wait_ge(S["w_exp"], 1)
            dve.mark(ve.tensor_tensor(wend[:, 0:2], wend[:, 0:2], dt_tok[:, 0:1].broadcast_to([P, 2, H]), ALU.mult))
            dve.link(ve, ve.tensor_tensor(wend[:, 2:4], wend[:, 2:4], dt_tok[:, 1:3], ALU.mult))
            ve.sem_inc(S["w_ready"], 1)

            dve.mark(ve.memset(xraw[:, :, 0:SK - 1], 0.0))
            for half in range(2):
                take("sst", 4 + half)
                ve.tensor_copy(xsamp[:, 12 * half:12 * half + 12, :, 0:SK - 1],
                               bank[4 + half][:, 0:288].rearrange("p (k b l) -> p k b l", k=12, b=NB)).then_inc(
                                   bank_free[4 + half], 1)
            dve.wait(ve)
            with ve.Fori(0, XBC_N) as i:
                with dve.loop(i, XBC_N, 8 * 4):
                    for n in range(8):
                        b, par, c = n % 4, n % 2, i * 8 + n
                        ve.wait_ge(bank_ready[b], i * 2 + (use("xbc", b) + n // 4))
                        dve.mark(ve.tensor_copy(xraw[:, par, SK - 1:], bank[b][:, 0:NP]))
                        ve.tensor_copy(flat(xtail[:, ds(c, 1), 0:SK - 1]), bank[b][:, NP - SK + 1:NP])
                        ve.tensor_copy(xsamp[:, ds(c, 1), :, SK - 1:].rearrange("p k b l -> p (k b) l"),
                                       bank[b][:, NP:T].rearrange("p (b l) -> p b l", b=NB)).then_inc(bank_free[b], 1)
                        if n >= 2:
                            ve.wait_ge(S["xbc_ready"], i * 8 + n)
                        else:
                            ve.wait_ge(S["xbc_ready"], i * 8 + 1)
                        for k in range(SK):
                            tap = vcol[:, ds(c + (SW0 + k * XC), 1)]
                            u = xraw[:, par, k:k + NP]
                            dve.wait(ve)
                            if k == 0:
                                dve.mark(ve.tensor_scalar(acc[:, par], u, tap, None, ALU.mult))
                            else:
                                ins = ve.scalar_tensor_tensor(out=acc[:, par], in0=u, scalar=tap, in1=acc[:, par],
                                                              op0=ALU.mult, op1=ALU.add)
                                if k < SK - 1:
                                    dve.mark(ins)
                                else:
                                    ins.then_inc(S["acc_ready"], 1)
            for b in range(4):
                ve.wait_ge(bank_free[b], use("xbc", b, 2 * XBC_N - 1))
            dve.link(ve, ve.tensor_copy(xtail[:, :, SK - 1:].rearrange("p k (b l) -> p k b l", b=NB),
                                        xsamp[:, :, :, NL:NL + SK - 1]))
            ve.sem_inc(S["xtail_ready"], 1)
            dve.link(ve, ve.tensor_copy(tmps, bc(CONV_B, NS)))
            for k in range(SK):
                w = vcol[:, SW0 + k * XC:SW0 + (k + 1) * XC]
                dve.link(ve, ve.tensor_tensor(bl(uxs), xsamp[:, :, :, k:k + NL], bc(w, NB, NL), ALU.mult))
                dve.link(ve, ve.tensor_tensor(tmps, tmps, uxs, ALU.add))
            ve.sem_inc(S["xpad_ready"], 1)

            ve.wait_ge(S["xtail_out"], 32)
            ve.wait_ge(S["xbc_ready"], XC + 2)
            for b in range(4):
                ve.wait_ge(bank_free[b], use("z2", b, 1))
            with ve.Fori(0, G) as g:
                with dve.loop(g, G, 2 + 4 * 2):
                    ve.wait_ge(bank_ready[3], g * 5 + use("ssd", 3))
                    dve.mark(ve.tensor_tensor(cbm[:, 0:2], bank[3][:, 0:NP].rearrange("p (q n) -> p q n", q=2),
                                              upper[:].unsqueeze(1).broadcast_to([P, 2, P]), ALU.mult))
                    ve.tensor_tensor(cbm[0:NS, 2, 0:NS], bank[3][0:NS, 2 * P:2 * P + NS], ublk[:], ALU.mult).then_inc(
                        bank_free[3], 1)
                    ve.wait_ge(bank_ready[2], g * 5 + use("ssd", 2))
                    ve.wait_ge(bank_ready[1], g * 8 + (use("ssd", 1) - 1))
                    dve.mark(ve.tensor_copy(btok[:, 0:2], bank[2][:, 0:NP].rearrange("p (q n) -> p q n", q=2)))
                    ve.tensor_copy(btok[0:NS, 2], bank[2][0:NS, 2 * P:3 * P]).then_inc(bank_free[2], 1)
                    ve.wait_ge(bank_free[2], g * 5 + use("ssd", 2))
                    ve.tensor_tensor(bexp[0:NS], btok[0:NS, 2:3].broadcast_to([NS, NB, P]), bc(seqsel[:], P),
                                     ALU.mult).then_inc(S["bexp_ready"], 1)
                    for k in range(4):
                        par, c = k % 2, g * 4 + k
                        ve.wait_ge(bank_ready[3], g * 5 + (use("ssd", 3) + 1 + k))
                        ve.wait_ge(bank_ready[7], g * 4 + (use("ssd", 7) - 1 + k))
                        dve.mark(ve.tensor_copy(xtok[:, 0:2], bank[3][:, 0:NP].rearrange("p (q n) -> p q n", q=2)))
                        ve.tensor_copy(xtok[0:NS, 2], bank[3][0:NS, 2 * P:3 * P]).then_inc(bank_free[3], 1)
                        ve.wait_ge(bank_free[3], g * 5 + (use("ssd", 3) + 1 + k))
                        dve.wait(ve)
                        ve.wait_ge(bank_ready[1], g * 8 + (use("ssd", 1) - 1 + 2 * k))
                        for w, q, rows in ((0, 0, P), (1, 0, P), (2, 1, P), (3, 2, NS)):
                            ins = ve.tensor_tensor(xw[0:rows, w].rearrange("p (h q) -> p h q", h=2),
                                                   xtok[0:rows, q].rearrange("p (h q) -> p h q", h=2),
                                                   bc(wend[0:rows, w, ds(g * 8 + 2 * k, 2)], HD), ALU.mult)
                        ins.then_inc(S["xw_ready"], 1)
                        for h in range(2):
                            head = g * 8 + (2 * k + h)
                            ve.wait_ge(bank_ready[5 + h], g * 4 + (use("ssd", 5 + h) + k))
                            for q, (t0, rows) in enumerate(TOK):
                                ins = ve.tensor_scalar(mt[0:rows, h, t0:t0 + rows], bank[5 + h][0:rows, t0:t0 + rows],
                                                       acum[0:rows, q, ds(head, 1)], 0.0, ALU.subtract, ALU.min)
                            ins.then_inc(S["seg_ready"], 1)
                        for h in range(2):
                            head = g * 8 + (2 * k + h)
                            ve.wait_ge(S["exp_ready"], g * 8 + (2 * k + h + 1))
                            for q, (t0, rows) in enumerate(TOK):
                                ve.scalar_tensor_tensor(out=mt[0:rows, h, t0:t0 + rows], in0=mt[0:rows, h, t0:t0 + rows],
                                                        scalar=dt_tok[0:rows, q, ds(head, 1)],
                                                        in1=cbm[0:rows, q, 0:rows], op0=ALU.mult, op1=ALU.mult)
                            ve.wait_ge(bank_free[5 + h], g * 4 + (use("ssd", 5 + h) + k))
                            ve.tensor_tensor(cs[:, h], cs[:, h], flat(xbcT[:, ds(g + (KC + G), 1), P:T]),
                                             ALU.mult).then_inc(S["m_ready"], 1)
                        ve.wait_ge(S["scaled"], g * 4 + (k + 2))
                        for b in range(2):
                            ve.wait_ge(bank_ready[b], g * 8 + (use("ssd", b) + 2 * k + 1))
                            ve.tensor_tensor(s0[:, par, 4 * b:4 * b + 4], s0[:, par, 4 * b:4 * b + 4],
                                             bank[b][:].rearrange("p (b n) -> p b n", b=4), ALU.add).then_inc(
                                                 bank_free[b], 1)
                        ve.wait_ge(bank_ready[7], g * 4 + (use("ssd", 7) + k))
                        dve.link(ve, ve.scalar_tensor_tensor(out=rs[:], in0=flat(xbcT[:, ds(c, 1)]),
                                                             scalar=dcol[:, ds(c, 1)], in1=bank[7][:, 0:T],
                                                             op0=ALU.mult, op1=ALU.add))
                        ve.sem_inc(bank_free[7], 1)
                        ve.tensor_tensor(flat(zb[:, ds(c, 1)]), flat(zb[:, ds(c, 1)]), rs[:], ALU.mult).then_inc(
                            S["y_done"], 1)
            ve.wait_ge(S["sf_out"], 16 * KC)
            dve.link(ve, ve.memset(part_mix, 0.0))
            ve.sem_inc(S["part_zero"], 1)
            for q in range(G):
                take("gn", 4 + q)
                ve.tensor_scalar(grs[:, q], bank[4 + q][:, 0:T], 1.0 / (D // G), EPS, ALU.mult, ALU.add).then_inc(
                    S["gmean_ready"], 1)
            ve.wait_ge(S["y_done"], KC)
            for q in range(G):
                ve.wait_ge(S["groot_ready"], q + 1)
                ve.sem_inc(bank_free[4 + q], 1)
                dve.link(ve, ve.reciprocal(grs[:, q], grs[:, q]))
                for c in range(4 * q, 4 * q + 4):
                    dve.mark(ve.scalar_tensor_tensor(out=zb[:, c], in0=zb[:, c], scalar=SSD_G[:, c:c + 1],
                                                     in1=grs[:, q], op0=ALU.mult, op1=ALU.mult))
            dve.wait(ve)
            ve.sem_inc(S["y_ready"], 1)
            ve.wait_ge(bank_free[4], use("ssd", 4, KC - 1))
            with ve.Fori(0, 2) as i:
                with dve.loop(i, 2, 8):
                    for c in range(8):
                        b = c % 4
                        ve.wait_ge(bank_ready[b], i * 2 + (use("so", b) + c // 4))
                        v_, g_ = flat(vb[:, ds(i * 8 + c, 1)]), flat(gb[:, ds(i * 8 + c, 1)])
                        dve.link(ve, ve.tensor_tensor(v_, v_, bank[b][:, 0:T], ALU.mult))
                        ve.sem_inc(bank_free[b], 1)
                        ve.tensor_tensor(g_, g_, v_, ALU.add).then_inc(S["merged"], 1)

            def add_gated(b, c, gate, done):
                g_ = mod[:, ds(gate, 1)] if not isinstance(gate, int) else mod[:, gate:gate + 1]
                x_ = xT[:, ds(c, 1)] if not isinstance(c, int) else xT[:, c:c + 1]
                x_p, x_s = flat(x_[:, :, 0:NP]), flat(x_[:, :, NP:T])
                dve.mark(ve.scalar_tensor_tensor(out=x_p, in0=bank[b][:, 0:NP], scalar=g_[:, :, 0:1], in1=x_p,
                                                 op0=ALU.mult, op1=ALU.add))
                tmp = (rs, stat)[b % 2][:, NP:T]
                dve.link(ve, ve.tensor_tensor(tmp.rearrange("p (b l) -> p b l", b=NB),
                                              bank[b][:, NP:T].rearrange("p (b l) -> p b l", b=NB),
                                              bc(flat(g_[:, :, 1:NSEQ]), NL), ALU.mult))
                ve.sem_inc(bank_free[b], 1)
                ve.tensor_tensor(x_s, x_s, tmp, ALU.add).then_inc(S[done], 1)

            with ve.Fori(0, 2) as i:
                with dve.loop(i, 2, 16):
                    for c in range(8):
                        b = c % 4
                        ve.wait_ge(bank_ready[b], i * 2 + (use("wo", b) + c // 4))
                        add_gated(b, i * 8 + c, i * 8 + (2 * KC + c), "x_mid")
            ve.wait_ge(S["x_mid"], KC)
            scales(G_FFN, 4 * KC)
            inv_rms("n2", 4, 3, D)
            normalise()
            modulate_samples(3 * KC)

            neg, m1_, m2_ = small[0], small[1], small[2]
            for par in range(2):
                ve.wait_ge(st_out[par], 128)
            ve.wait_ge(S["sf_out"], 16 * KC)
            dve.link(ve, ve.memset(lg, 0.0))
            take("route", 5)
            dve.mark(ve.tensor_tensor(lg[:, 0:2], bank[5][:, 0:72].rearrange("p (q n) -> p q n", q=2),
                                      rbias[:].unsqueeze(1).broadcast_to([P, 2, 36]), ALU.add))
            dve.link(ve, ve.tensor_tensor(lg[0:NS, 2], bank[5][0:NS, 72:108], rbias[0:NS], ALU.add))
            ve.sem_inc(bank_free[5], 1)
            ve.wait_ge(S["pooled"], 1)
            gmax, gsum, gtop, gfirst, emax, esum, p1, p2, first1, first2, ptot, gA, gB, sA, sB, eA, eB = tiny[:17]
            cand, ohg = small[3][:, :, 0:NG], small[4][:, :, 0:NG]
            oh1, oh2, prob, left, cand8 = [small[5 + n][:, :, 0:EG] for n in range(5)]

            def iota(n):
                return iota_e[:, 0:n].unsqueeze(1).broadcast_to([P, 3, n])

            def first_of(onehot, cnd, values, top, idx, n):
                dve.link(ve, ve.tensor_tensor(cnd, values, bc(top, n), ALU.is_equal))
                dve.link(ve, ve.scalar_tensor_tensor(out=cnd, in0=cnd, scalar=-64.0, in1=iota(n), op0=ALU.mult,
                                                     op1=ALU.add))
                dve.link(ve, ve.tensor_reduce(idx, cnd, AX_X, ALU.min))
                dve.link(ve, ve.tensor_tensor(onehot, cnd, bc(idx, n), ALU.is_equal))

            dve.link(ve, ve.tensor_reduce(gmax, lg[:, :, 0:NG], AX_X, ALU.max))
            first_of(ohg, cand, lg[:, :, 0:NG], gmax, gfirst, NG)
            dve.link(ve, ve.tensor_tensor(lg[:, :, 0:NG], lg[:, :, 0:NG], bc(gmax, NG), ALU.subtract))
            ve.sem_inc(S["e_arg"], 1)
            chosen_l = small[10].rearrange("p q (g e) -> p q g e", g=NG)
            dve.link(ve, ve.tensor_tensor(chosen_l, lg[:, :, NG:36].rearrange("p q (g e) -> p q g e", g=NG),
                                          bc(ohg, EG), ALU.mult))
            dve.link(ve, ve.tensor_reduce(sel, chosen_l.rearrange("p q g e -> p q e g"), AX_X, ALU.add))
            dve.link(ve, ve.tensor_reduce(emax, sel, AX_X, ALU.max))
            dve.link(ve, ve.tensor_tensor(sel, sel, bc(emax, EG), ALU.subtract))
            ve.sem_inc(S["e_arg"], 1)
            ve.wait_ge(S["gexp"], 1)
            dve.link(ve, ve.tensor_reduce(gsum, lg[:, :, 0:NG], AX_X, ALU.add))
            dve.link(ve, ve.reciprocal(gtop, gsum))
            ve.wait_ge(S["eexp"], 1)
            dve.link(ve, ve.tensor_reduce(esum, sel, AX_X, ALU.add))
            dve.link(ve, ve.reciprocal(esum, esum))
            dve.link(ve, ve.tensor_tensor(prob, sel, bc(esum, EG), ALU.mult))
            dve.link(ve, ve.tensor_reduce(p1, prob, AX_X, ALU.max))
            first_of(oh1, cand8, prob, p1, first1, EG)
            dve.link(ve, ve.scalar_tensor_tensor(out=left, in0=oh1, scalar=-2.0, in1=prob, op0=ALU.mult, op1=ALU.add))
            dve.link(ve, ve.tensor_reduce(p2, left, AX_X, ALU.max))
            first_of(oh2, cand8, left, p2, first2, EG)
            dve.link(ve, ve.tensor_tensor(ptot, p1, p2, ALU.add))
            dve.link(ve, ve.reciprocal(ptot, ptot))
            dve.link(ve, ve.tensor_tensor(ptot, ptot, gtop, ALU.mult))
            dve.mark(ve.tensor_tensor(gA, p1, ptot, ALU.mult))
            dve.mark(ve.tensor_tensor(gB, p2, ptot, ALU.mult))
            for m_, oh in ((m1_, oh1), (m2_, oh2)):
                dve.mark(ve.tensor_tensor(m_.rearrange("p q (g e) -> p q g e", g=NG), bc(ohg, EG),
                                          oh.unsqueeze(2).broadcast_to([P, 3, NG, EG]), ALU.mult))
            dve.wait(ve)
            ve.tensor_tensor(chosen, m1_, m2_, ALU.add).then_inc(S["cnt_ready"], 1)
            take("route", 6)
            dve.link(ve, ve.tensor_copy(cntb[0:NE], bank[6][0:NE, 0:1].broadcast_to([NE, P])))
            ve.sem_inc(bank_free[6], 1)
            ve.sem_inc(S["cnt_ready"], 1)
            pos = small[11]
            dve.mark(ve.memset(pos, 0.0))
            dve.link(ve, ve.memset(meta, 0.0))
            take("route", 7)
            dve.mark(ve.tensor_copy(pos[:, 0:2], bank[7][:, 0:64].rearrange("p (q e) -> p q e", q=2)))
            dve.mark(ve.tensor_copy(pos[0:NS, 2], bank[7][0:NS, 64:96]))
            dve.mark(ve.tensor_copy(meta[:, 0, 0:NE], bank[7][:, 128:160]))
            dve.mark(ve.tensor_scalar(meta[:, 1, 0:NE], bank[7][:, 96:128], float(SLOTS - WIN), None, ALU.min))
            dve.link(ve, ve.tensor_scalar(meta[:, 2, 0:NE], bank[7][:, 96:128], float(SLOTS - T), None, ALU.min))
            ve.sem_inc(bank_free[7], 1)
            dve.link(ve, ve.tensor_copy(meta_i[:], meta))
            ve.sem_inc(S["meta_ready"], 1)
            for m_, s_, e_ in ((m1_, sA, eA), (m2_, sB, eB)):
                dve.link(ve, ve.tensor_tensor(neg, pos, m_, ALU.mult))
                dve.link(ve, ve.tensor_reduce(s_, neg, AX_X, ALU.add))
                dve.link(ve, ve.tensor_tensor(neg, m_, iota(NE), ALU.mult))
                dve.link(ve, ve.tensor_reduce(e_, neg, AX_X, ALU.add))
            for q, (t0, rows) in enumerate(TOK):
                def at_pair(out, s_, val=None):
                    ins = ve.tensor_scalar(out[0:rows, q] if out is not tq else tq[0:rows], iota_s[0:rows],
                                           s_[0:rows, q:q + 1], None if val is None else val[0:rows, q:q + 1],
                                           ALU.is_equal, *(() if val is None else (ALU.mult,)))
                    dve.link(ve, ins)

                at_pair(pm, sA)
                dve.mark(ve.scalar_tensor_tensor(out=pm[0:rows, q], in0=iota_s[0:rows], scalar=sB[0:rows, q:q + 1],
                                                 in1=pm[0:rows, q], op0=ALU.is_equal, op1=ALU.add))
                for out, vA, vB in ((gt, gA, gB), (et, eA, eB)):
                    at_pair(out, sA, vA)
                    at_pair(tq, sB, vB)
                    dve.link(ve, ve.tensor_tensor(out[0:rows, q], out[0:rows, q], tq[0:rows], ALU.add))
            ve.sem_inc(S["sort_ready"], 1)
            for b, dst in enumerate((gbc[:, 0:T], gbc[:, T:], ebc[:, 0:T], ebc[:, T:])):
                take("gates", b)
                ve.tensor_copy(dst, bank[b][:, 0:T]).then_inc(bank_free[b], 1)
            dve.mark(ve.memset(ys, 0.0))
            for c in range(KC):
                for half in range(2):
                    b = 2 * (c % 2) + half
                    take("gather", b, c // 2)
                    ve.tensor_copy(hs[:, c, T * half:T * (half + 1)], bank[b][:, 0:T]).then_inc(bank_free[b], 1)
            dve.wait(ve)
            for b in range(4):
                ve.wait_ge(bank_free[b], use("gather", b, 7))

            def window(e):
                w0 = ve.value_load(meta_i[0:1, 1, ds(e, 1)], min_val=0, max_val=SLOTS - WIN)
                return w0

            dve.link(ve, ve.memset(hid, 0.0))
            w_first = ve.value_load(meta_i[0:1, 1, 0:1], min_val=0, max_val=SLOTS - WIN)
            ve.tensor_copy(hwin[:, 0], hs[:, :, ds(w_first, WIN)]).then_inc(S["win_ready"], 1)
            with ve.Fori(0, 8) as i:
                with dve.loop(i, 8, 4 * 3):
                    for k in range(4):
                        nxt = ve.value_load(meta_i[0:1, 1, ds(i * 4 + (k + 1), 1)], min_val=0, max_val=SLOTS - WIN)
                        ve.wait_ge(S["u_done"], i * 4 + (k + 1))
                        ve.tensor_copy(hwin[:, (k + 1) % 2], hs[:, :, ds(nxt, WIN)]).then_inc(S["win_ready"], 1)
                        n_pairs = ve.value_load(meta_i[0:1, 0, ds(i * 4 + k, 1)], min_val=0, max_val=T)
                        wn = ve.value_load(meta_i[0:1, 1, ds(i * 4 + k, 1)], min_val=0, max_val=SLOTS - WIN)
                        ww = ve.value_load(meta_i[0:1, 2, ds(i * 4 + k, 1)], min_val=0, max_val=SLOTS - T)
                        mine = iota_e[:, ds(i * 4 + k, 1)]
                        count = dve.n
                        with ve.If(n_pairs > WIN):
                            dve.link(ve, ve.scalar_tensor_tensor(out=gwin, in0=ebc[:, ds(ww, T)], scalar=mine,
                                                                 in1=gbc[:, ds(ww, T)], op0=ALU.is_equal, op1=ALU.mult))
                            ve.wait_ge(S["u_done"], i * 4 + (k + 2))
                            dve.mark(ve.tensor_tensor(hid[:, 0], bank[5][:, 0:T], gwin, ALU.mult))
                            dve.link(ve, ve.tensor_tensor(hid[:, 1], bank[7][:, 0:T], gwin, ALU.mult))
                            ve.wait_ge(S["sil_ready"], i * 4 + (k + 2))
                            ve.tensor_tensor(hid, hid, sil, ALU.mult).then_inc(S["hid_ready"], 1)
                            ve.sem_inc(S["prod_ready"], 1)
                            ve.wait_ge(S["ys_done"], i * 4 + (k + 1))
                            for c in range(KC):
                                ve.wait_ge(S["wide_ready"], i * 64 + (16 * k + c + 1))
                                y_ = ys[:, c, ds(ww, T)]
                                ve.tensor_tensor(y_, y_, bank[c % 4][:, 0:T], ALU.add).then_inc(S["wide_free"], 1)
                            ve.wait_ge(S["wide_free"], i * 64 + 16 * (k + 1))
                            ve.sem_inc(S["ys_done"], 1)
                        n_after, dve.n = dve.n, count
                        with ve.Else():
                            dve.link(ve, ve.scalar_tensor_tensor(out=gwin[:, 0:WIN], in0=ebc[:, ds(wn, WIN)], scalar=mine,
                                                                 in1=gbc[:, ds(wn, WIN)], op0=ALU.is_equal, op1=ALU.mult))
                            ve.wait_ge(S["u_done"], i * 4 + (k + 2))
                            ve.wait_ge(S["sil_ready"], i * 4 + (k + 2))
                            ve.tensor_tensor(sil[:, 1, 0:P], bank[5][:, 0:P], sil[:, 0, 0:P], ALU.mult).then_inc(
                                S["prod_ready"], 1)
                            ve.wait_ge(S["prod_turned"], i * 4 + (k + 1))
                            ve.tensor_tensor(hid[:, :, 0:WIN], bank[6][:, 0:P].rearrange("p (f w) -> p f w", f=2),
                                             gwin[:, 0:WIN].unsqueeze(1).broadcast_to([P, 2, WIN]), ALU.mult).then_inc(
                                                 S["hid_ready"], 1)
                            ve.wait_ge(S["ys_done"], i * 4 + (k + 1))
                            ve.wait_ge(S["d_ready"], i * 4 + (k + 1))
                            for q in range(4):
                                y_ = ys[:, 4 * q:4 * q + 4, ds(wn, WIN)]
                                ins = ve.tensor_tensor(y_, y_, bank[q][:].rearrange("p (c w) -> p c w", c=4)[:, :, 0:WIN], ALU.add)
                            ins.then_inc(S["ys_done"], 1)
                            ve.sem_inc(S["wide_free"], 16)
                            dve.skip(ve, 2)
                        assert dve.n == n_after

            for j in range(5):
                n = min(P, SLOTS - P * j)
                take("pt", 4 + j % 2, j // 2)
                ve.tensor_copy(pt[0:n, j], bank[4 + j % 2][0:n, 0:T]).then_inc(bank_free[4 + j % 2], 1)
            for c in range(KC):
                take("unsort", c % 4, c // 4)
                add_gated(c % 4, c, 5 * KC + c, "moe_ready")
            ve.wait_ge(S["moe_ready"], KC)
            inv_rms("n3", 4, 4, D)
            for c in range(KC):
                ve.scalar_tensor_tensor(out=xT[:, c], in0=xT[:, c], scalar=FIN_G[:, c:c + 1], in1=rs[:],
                                        op0=ALU.mult, op1=ALU.mult).then_inc(S["y_fin"], 1)


_OUTS = [
    (1, NP, D), (NB, NL, D), (1, 1, H, HD, P), (1, 1, SK - 1, 3072), (1, 1, CK - 1, D),
    (1, NB, H, HD, P), (1, NB, SK - 1, 3072), (1, NB, CK - 1, D),
]


def kernel(**inputs):
    import numpy as _np
    import concourse.bacc as _bacc
    from concourse import mybir as _mybir
    from concourse.bass_utils import run_bass_kernel_spmd as _run

    nc = _bacc.Bacc("TRN2", target_bir_lowering=False, num_devices=1)
    arrays, a = {}, {}
    for name, x in inputs.items():
        x = _np.ascontiguousarray(x)
        arrays[f"in_{name}"] = x
        a[name] = nc.dram_tensor(f"in_{name}", x.shape, _mybir.dt.from_np(x.dtype), kind="ExternalInput").ap()
    outs = [nc.dram_tensor(f"out_{i}", shape, _mybir.dt.float32, kind="ExternalOutput").ap()
            for i, shape in enumerate(_OUTS)]
    hybrid_step(nc, a, outs)
    r = _run(nc, [arrays], core_ids=[0])
    return tuple(r.results[0][f"out_{i}"] for i in range(len(_OUTS)))
```

```python
from contextlib import ExitStack, contextmanager, nullcontext

import concourse.bass as bass
from concourse import mybir

F32 = mybir.dt.float32
I32 = mybir.dt.int32
ALU = mybir.AluOpType
ACT = mybir.ActivationFunctionType
AX_X = mybir.AxisListType.X
ds = bass.ds

P = 128
D = 2048
KC = D // P
NP = 256
NB, NL = 8, 4
NS = NB * NL
T = NP + NS
NSEQ = 1 + NB
XC = 3072 // P
H = 32
G = 4
HD = 64
CK = 31
SK = 4
NE = 32
NG = 4
EG = 8
EPS = 1e-6
SLOTS = 2 * T
WIN = 64
UC = 256
RING = 4
TOK = [(0, P), (P, P), (NP, NS)]

Z0, X0, DT0, GLU0 = 0, D, D + 3072, D + 3072 + H
GS0, GC0 = GLU0 + 2 * D, GLU0 + 3 * D

GLU_N, XBC_N = 4, 3

MIXED = "pappappappap"
SO_UNITS = "aaaapppppppp"
PHASES = [("ada", 3, "aaaa"), ("ada2", 1, "aaaa"), ("glu", 2, MIXED), ("gc", 1, MIXED), ("z1", 1, "papapapa"),
          ("co", 1, MIXED), ("xbc", 3, "pppp"), ("z2", 1, "pppp"), ("gs", 2, "pppp"), ("so", 1, SO_UNITS),
          ("wo", 1, MIXED), ("rt", 1, "aaaa")]


def phase_uses(name):
    steps, units = {n: (s, u) for n, s, u in PHASES}[name]
    return {**{b: steps * units.count("p") // 2 for b in range(4)},
            **{b: steps * units.count("a") // 2 for b in range(4, 8)}}


class Count:

    def __init__(self, sem):
        self.sem, self.n, self.off = sem, 0, 0

    def mark(self, ins):
        ins.then_inc(self.sem, 1)
        self.n += 1

    def wait(self, eng, back=0):
        eng.wait_ge(self.sem, self.off + self.n - back)

    def link(self, eng, ins):
        self.mark(ins)
        self.wait(eng)

    def skip(self, eng, n):
        eng.sem_inc(self.sem, n)
        self.n += n

    @contextmanager
    def loop(self, i, trips, per):
        start = self.n
        self.off = i * per
        yield
        assert self.n == start + per, self.n - start
        self.n, self.off = start + trips * per, 0


USES = [
    ("x", {0: 4, 1: 4, 2: 4, 3: 4}), ("c", {4: 1}), ("vec", {5: 1, 6: 1}),
    ("n1", {4: 1}), ("ada", phase_uses("ada")), ("ada2", phase_uses("ada2")),
    ("cst", {0: 4, 1: 4, 2: 4, 3: 4}), ("glu", phase_uses("glu")), ("tail", {4: 1, 5: 1, 6: 1, 7: 1}),
    ("gc", phase_uses("gc")), ("ln", {4: 1}), ("z1", phase_uses("z1")), ("lnsq", {5: 1}), ("dt", {6: 1}),
    ("co", phase_uses("co")), ("cum", {7: 1}), ("sst", {4: 1, 5: 1}), ("xbc", phase_uses("xbc")),
    ("z2", phase_uses("z2")), ("xtail", {4: 2, 5: 2, 6: 1, 7: 1}), ("ssd", {0: 32, 1: 32, 2: 20, 3: 20, 4: 16, 5: 16, 6: 16, 7: 16}),
    ("gn", {0: 1, 1: 1, 2: 1, 3: 1}), ("so", phase_uses("so")),
    ("wo", phase_uses("wo")), ("n2", {0: 1}), ("route", {1: 1, 2: 1, 3: 1}), ("rt", phase_uses("rt")),
    ("gather", {b: 8 for b in range(6)}), ("gates", {0: 1, 1: 1, 2: 1, 3: 1}),
    ("pt", {4: 3, 5: 2}), ("unsort", {0: 8, 1: 8, 2: 12, 3: 1, 4: 8, 5: 8, 6: 8, 7: 8}),
    ("n3", {4: 1}),
]


def uses_before():
    at, out = {b: 0 for b in range(8)}, {}
    for name, banks in USES:
        out[name] = dict(at)
        for b, n in banks.items():
            at[b] += n
    return out


def hybrid_step(nc, a, o):
    with ExitStack() as ctx:
        def sb(name, shape, dt=F32):
            return ctx.enter_context(nc.sbuf_tensor(name, shape, dt))

        def sem(name):
            return ctx.enter_context(nc.semaphore(name))

        ring = sb("ring", [P, RING, KC, UC])
        xT = sb("xT", [P, KC, T])
        hT = sb("hT", [P, KC, T])
        ident = sb("ident", [P, P])
        ones = sb("ones", [P, P])
        upper = sb("upper", [P, P])
        seqsel = sb("seqsel", [NS, NB])
        blk = sb("blk", [NS, NS])
        ublk = sb("ublk", [NS, NS])
        vcol = sb("vcol", [P, 7 * P])
        mod = sb("mod", [P, 6 * KC, NSEQ])
        scaleA = sb("scaleA", [P, KC, NSEQ])
        rs = sb("rs", [P, T])
        stat = sb("stat", [P, T])
        dcol = sb("dcol", [P, KC])
        dt_tok = sb("dt_tok", [P, 3, H])
        dtA = sb("dtA", [P, 3, H])
        acum = sb("acum", [P, 3, H])
        wend = sb("wend", [P, 4, H])
        rows_bc = sb("rows_bc", [P, 2, H])
        rbias = sb("rbias", [P, 36])
        meta_i = sb("meta_i", [P, 3, NE + 1], I32)
        WORK = 24000
        work = sb("work", [P, WORK])

        def carve(at, *dims):
            n = 1
            for x in dims:
                n *= x
            assert at + n <= WORK, (at, n)
            v = work[:, at:at + n]
            if len(dims) == 2:
                v = v.rearrange("p (a b) -> p a b", a=dims[0])
            if len(dims) == 3:
                v = v.rearrange("p (a b c) -> p a b c", a=dims[0], b=dims[1])
            if len(dims) == 4:
                v = v.rearrange("p (a b c d) -> p a b c d", a=dims[0], b=dims[1], c=dims[2])
            return v

        BIG = KC * T
        zb = carve(0, KC, T)
        vb = carve(BIG, KC, T)
        xbcT = carve(BIG, XC, T)
        gb = carve(BIG + XC * T, KC, T)
        TMP = BIG + XC * T + BIG
        sq = zb
        xrow = carve(0, 3, D)
        crow = carve(3 * D, D)
        vrow = carve(4 * D, 7, P)
        cstrow = carve(4 * D + 7 * P + KC * NSEQ, 2, D)
        t = TMP
        usamp = carve(t, KC, NB, CK - 1 + NL); t += KC * NB * (CK - 1 + NL)
        upad = carve(t, 4, CK - 1 + NP); t += 4 * (CK - 1 + NP)
        sgl = carve(t, 4, T); t += 4 * T
        utail = carve(t, KC, CK - 1 + NS); t += KC * (CK - 1 + NS)
        assert t == TMP + 7640
        cT = carve(t, KC, NSEQ); t += KC * NSEQ
        fold = carve(t, NSEQ)
        part_glu = carve(TMP - 2 * UC, 2, UC)
        part_mix = carve(TMP + 6862, 2, UC)
        tmpc = carve(0, KC, NS)
        uvs = carve(KC * NS, KC, NS)
        tailrow = carve(2 * KC * NS, D)
        sq_ln = carve(TMP, KC, T)
        wdt = carve(TMP + KC * T, KC, H)
        t = TMP
        xsamp = carve(t, XC, NB, SK - 1 + NL); t += XC * NB * (SK - 1 + NL)
        xraw = carve(t, 2, SK - 1 + NP); t += 2 * (SK - 1 + NP)
        xtail = carve(t, XC, SK - 1 + NB * (SK - 1)); t += XC * (SK - 1) * (1 + NB)
        sstrow = carve(t, XC * P); t += XC * P
        acc = carve(t, 2, NP); t += 2 * NP
        tmps = carve(t, XC, NS); t += XC * NS
        uxs = carve(t, XC, NS); t += XC * NS
        t = TMP
        s0 = carve(t, 2, NB, P); t += 2 * NB * P
        s0T = carve(t, NB, P); t += NB * P
        bexp = carve(t, NB, P); t += NB * P
        xst = carve(t, T); t += T
        bst = carve(t, T); t += T
        xtok = carve(t, 3, P); t += 3 * P
        btok = carve(t, 3, P); t += 3 * P
        cbm = carve(t, 3, P); t += 3 * P
        mt = carve(t, 2, T); t += 2 * T
        cs = carve(t, 2, P + NS); t += 2 * (P + NS)
        xw = carve(t, 4, P); t += 4 * P
        s1T = carve(t, P); t += P
        sfin = carve(t, P); t += P
        dax = carve(t, P); t += P
        dec = carve(t, NB); t += NB
        ud = [stat, rs]
        hs = carve(0, KC, SLOTS)
        ys = carve(KC * SLOTS, KC, SLOTS)
        t = 2 * KC * SLOTS
        gbc = carve(t, SLOTS); t += SLOTS
        ebc = carve(t, SLOTS); t += SLOTS
        pm = carve(t, 3, SLOTS); t += 3 * SLOTS
        iota_e = carve(t, NE); t += NE
        strict = carve(t, P); t += P
        meta = carve(t, 3, NE + 1); t += 3 * (NE + 1)
        rt = t
        htok = carve(t, 2, 3 * P); t += 2 * 3 * P
        gwin = carve(rt, T)
        sil = carve(rt + T, 2, T)
        hid = carve(rt + 3 * T, 2, T)
        assert rt + 5 * T <= WORK
        hwin = hT[:, :, 0:2 * WIN].rearrange("p k (two w) -> p two k w", two=2)
        t = KC * SLOTS
        wr = carve(t, KC, 36); t += KC * 36
        lg = carve(t, 3, 36); t += 108
        small = [carve(t + 96 * n, 3, 32) for n in range(14)]; t += 96 * 14
        tiny = [carve(t + 4 * n, 3) for n in range(20)]; t += 80
        iota_s = carve(t, SLOTS); t += SLOTS
        gt = carve(t, 3, SLOTS); t += 3 * SLOTS
        et = carve(t, 3, SLOTS); t += 3 * SLOTS
        tq = carve(t, SLOTS); t += SLOTS
        cntb = carve(t, P); t += P
        gmax, gsum, gtop, gfirst, emax, esum, p1, p2, first1, first2, ptot, gA, gB, sA, sB, eA, eB = tiny[:17]
        sel = carve(t, 3, EG); t += 3 * EG
        chosen = small[12]
        sp_abs, sp_e, sp_u, sp_ln, sp_d, sp_z, sp_m = [carve(TMP + KC * T + KC * H + 96 * n, 3, H) for n in range(7)]
        grs = carve(TMP + 4096, G, T)
        pt = carve(0, 5, T)
        ytok = carve(5 * T, 2, 5 * P)
        gx = carve(5 * T + 2 * 5 * P, KC, T)
        yrow = [carve(KC * SLOTS + 4 * SLOTS * j, 3, 4 * P) for j in range(4)]
        yrow_q = [work[:, KC * SLOTS:2 * KC * SLOTS].rearrange("p (j n) -> p j n", j=4)[:, :, 4 * P * q:4 * P * (q + 1)]
                  for q in range(3)]
        rcol = carve(rt, 3)

        bank = [ctx.enter_context(nc.psum_tensor(f"bank{b}", [P, 512], F32)) for b in range(8)]

        slot_loaded = [sem(f"slot_loaded{s}") for s in range(RING)]
        bank_ready = [sem(f"bank_ready{b}") for b in range(8)]
        bank_free = [sem(f"bank_free{b}") for b in range(8)]
        base = uses_before()

        def use(name, b, k=0):
            return base[name][b] + 1 + k

        pool = Count(sem("pool_step"))
        dve = Count(sem("dve_step"))
        act = Count(sem("act_step"))
        S = {n: sem(n) for n in (
            "consts_ready x_loaded c_loaded v_loaded vrow_zero small_loaded cst_loaded usamp_ready "
            "squares_ready mean_ready root_ready h_ready conv_ready y_fin vsamp_ready tail_out v_ready "
            "centred wdt_loaded dt_abs dt_exp dt_log one_plus dta_ready w_arg w_exp w_ready a_exp sst_loaded "
            "xpad_ready acc_ready xbc_ready xtail_ready xrow_ready xtail_out bst_ready xst_ready ud_ready "
            "dax_ready seg_ready exp_ready m_ready xw_ready bexp_ready scaled sf_out y_done x_used gx_ready "
            "sig_ready small_first pairs_ready gt_ready prod_ready prod_turned scale_ready hn_ready hs_ready "
            "hd_ready gsq_ready gmean_ready groot_ready y_ready merged x_mid wr_loaded gexp eexp cnt_ready "
            "meta_ready sort_ready ys_zero win_ready g_ready u_done sil_ready hid_ready d_ready ys_done "
            "wide_ready wide_free part_zero sf_free moe_ready out_rows out_done state_copy tail_rows e_arg "
            "pooled vb_free").split()}
        s0_loaded = [sem(f"s0_loaded{p}") for p in range(2)]
        st_out = [sem(f"st_out{p}") for p in range(2)]

        w_ada = a["w_ada"][0].rearrange("(k p) n -> p k n", p=P)
        w_in = a["w_in"][0].rearrange("(k p) n -> p k n", p=P)
        w_co = a["w_conf_out"][0].rearrange("(k p) n -> p k n", p=P)
        w_so = a["w_ssd_out"][0].rearrange("(k p) n -> p k n", p=P)
        w_o = a["w_o"][0].rearrange("(k p) n -> p k n", p=P)
        wg_e = a["w_exp_gate"][0].rearrange("e (k p) n -> p e k n", p=P)
        wu_e = a["w_exp_up"][0].rearrange("e (k p) n -> p e k n", p=P)
        wd_e = a["w_exp_down"][0].rearrange("e (f p) n -> p e f n", p=P)
        (y_p, y_s, ssm_p, sconv_p, cconv_p, ssm_s, sconv_s, cconv_s) = o
        s0_d = a["state_ssm"][0].rearrange("b (c h) q n -> (h q) c b n", h=2)
        s1_d = ssm_s[0].rearrange("b (c h) q n -> (h q) c b n", h=2)
        ssm_pd = ssm_p[0, 0].rearrange("(c h) q n -> (h q) c n", h=2)

        def bc(ap, *dims):
            shape = list(ap.shape)
            for d_ in dims:
                ap = ap.unsqueeze(len(shape))
                shape.append(d_)
            return ap.broadcast_to(shape)

        def vec(tile, at, n=KC):
            return vcol[:, tile * P + at:tile * P + at + n]

        B_ADA, G_MIX, G_FFN = vec(0, 0, 96), vec(0, 96), vec(0, 112)
        CONV_B, SSD_G, CONF_B = vec(1, 0, XC), vec(1, 24), vec(1, 40)
        LN_G, LN_B, FIN_G = vec(1, 56), vec(1, 72), vec(1, 88)
        SW0, CW0 = 2 * P, 3 * P

        def bl(ap):
            return ap.rearrange("p k (b l) -> p k b l", b=NB)

        VIEWS = {"gc": (w_in, GC0), "co": (w_co, 0), "z1": (w_in, Z0), "z2": (w_in, Z0 + D // 2), "xbc": (w_in, X0), "gs": (w_in, GS0),
                 "so": (w_so, 0), "wo": (w_o, 0)}
        ring0, ada0, rnd, au = {}, {}, 0, 0
        for name, steps, units in PHASES:
            ring0[name], ada0[name] = rnd, au
            rnd += steps * len(units) // RING
            au += steps * units.count("a")
        assert au == 6 * D // UC
        MOE_R = rnd

        def place(units, u):
            kind = units[u]
            n, many = units[:u].count(kind), units.count(kind)
            if kind == "p":
                return n, (2 * n + 1) % 4, (2 * n + 1) // 4, many // 2
            return n, 4 + n % 2, n // 2, many // 2

        def steps_of(eng, steps):
            return eng.Fori(0, steps) if steps > 1 else nullcontext(0)

        block = ctx.enter_context(nc.Block())

        @block.sync
        def _(sp):
            def unit(name, units, i, u):
                n, _, _, _ = place(units, u)
                if units[u] == "a":
                    src = w_ada[:, :, ds(i * (units.count("a") * UC) + (ada0[name] + n) * UC, UC)]
                elif name == "glu":
                    src = w_in[:, :, ds(i * (units.count("p") * UC // 2) + (GLU0 + (n % 2) * D + (n // 2) * UC), UC)]
                else:
                    w, c0 = VIEWS[name]
                    src = w[:, :, ds(i * (units.count("p") * UC) + (c0 + n * UC), UC)]
                sp.dma_start(ring[:, u % RING], src).then_inc(slot_loaded[u % RING], 16)

            def slot_used(name, units, i, u):
                _, b, k, per = place(units, u)
                sp.wait_ge(bank_ready[b], i * per + use(name, b, k))

            def stream(name, head=True, rest=True):
                n = [p[0] for p in PHASES].index(name)
                _, steps, units = PHASES[n]
                if head:
                    for u in range(RING):
                        if n:
                            before, s_, u_ = PHASES[n - 1]
                            slot_used(before, u_, s_ - 1, len(u_) - RING + u)
                        unit(name, units, 0, u)
                if rest:
                    for u in range(RING, len(units)):
                        slot_used(name, units, 0, u - RING)
                        unit(name, units, 0, u)
                    if steps > 1:
                        with sp.Fori(1, steps) as i:
                            for u in range(len(units)):
                                if u < RING:
                                    _, b, k, per = place(units, len(units) - RING + u)
                                    sp.wait_ge(bank_ready[b], i * per + (use(name, b, k) - per))
                                else:
                                    slot_used(name, units, i, u - RING)
                                unit(name, units, i, u)

            sp.dma_start(xrow[:, 0:2], a["x_prompt"][0].rearrange("(q p) n -> p q n", p=P)).then_inc(S["x_loaded"], 16)
            sp.dma_start(xrow[0:NS, 2], a["x_sample"].rearrange("b l n -> (b l) n")).then_inc(S["x_loaded"], 16)
            sp.dma_start(crow[0:1], a["c_prompt"]).then_inc(S["c_loaded"], 16)
            sp.dma_start(crow[1:NSEQ], a["c_sample"]).then_inc(S["c_loaded"], 16)
            sp.wait_ge(S["small_first"], 1)
            stream("ada")
            stream("ada2")
            stream("glu")
            stream("gc")
            sp.wait_ge(S["tail_rows"], 4)
            sp.dma_start(cconv_p[0, 0], tailrow[0:CK - 1]).then_inc(S["out_done"], 16)
            for b in range(NB):
                sp.dma_start(cconv_s[0, b, CK - 1 - NL:CK - 1],
                             tailrow[CK - 1 + NL * b:CK - 1 + NL * (b + 1)]).then_inc(S["tail_out"], 16)
            stream("z1", rest=False)
            sp.wait_ge(S["vsamp_ready"], 1)
            sp.wait_ge(S["conv_ready"], 1)
            sp.wait_ge(bank_free[7], use("tail", 7))
            sp.dma_start(wdt, w_in[:, :, DT0:DT0 + H], allow_slow_non_contiguous=True).then_inc(S["wdt_loaded"], 16)
            stream("z1", head=False)
            stream("co", rest=False)
            sp.wait_ge(S["dta_ready"], 1)
            sp.dma_start(sstrow[0:NB * (SK - 1)], a["state_ssd_conv"][0].rearrange("b k n -> (b k) n")).then_inc(
                S["sst_loaded"], 16)
            stream("co", head=False)
            stream("xbc")
            stream("z2")
            sp.wait_ge(S["xrow_ready"], 6)
            sp.dma_start(sconv_p[0, 0], sstrow[0:SK - 1]).then_inc(S["xtail_out"], 16)
            sp.dma_start(sconv_s[0].rearrange("b k n -> (b k) n"),
                         sstrow[SK - 1:(SK - 1) * (1 + NB)]).then_inc(S["xtail_out"], 16)
            def load_state(c):
                sp.dma_start(s0[:, c % 2], s0_d[:, c:c + 1].rearrange("p c b n -> p (c b) n")).then_inc(
                    s0_loaded[c % 2], 16)

            for u in range(RING):
                if u == 2:
                    sp.wait_ge(S["xtail_out"], 32)
                    sp.wait_ge(S["xbc_ready"], XC + 2)
                    load_state(0)
                    load_state(1)
                slot_used("z2", "pppp", 0, u)
                unit("gs", "pppp", 0, u)
            for c in range(KC):
                sp.wait_ge(bank_free[2], use("ssd", 2, c + c // 4 + 1))
                sp.dma_start(ssm_pd[:, c:c + 1].rearrange("p c n -> p (c n)"), sfin).then_inc(S["sf_out"], 16)
                for b in range(2):
                    sp.wait_ge(bank_free[b], use("ssd", b, 2 * c + 1))
                sp.dma_start(s1_d[:, c:c + 1].rearrange("p c b n -> p (c b) n"), s0[:, c % 2]).then_inc(st_out[c % 2], 16)
                if c % 2 == 1:
                    sp.wait_ge(bank_ready[4], use("ssd", 4, c))
                    u = c // 2
                    unit(*(("gs", "pppp", 1, u) if u < RING else ("so", SO_UNITS, 0, u - RING)))
                if c + 2 < KC:
                    sp.wait_ge(st_out[c % 2], 16 * (c // 2 + 1))
                    load_state(c + 2)
                sp.wait_ge(S["sf_out"], 16 * (c + 1))
                sp.sem_inc(S["sf_free"], 1)
            stream("so", head=False)
            stream("wo")
            stream("rt")
            sp.wait_ge(S["merged"], KC)
            sp.wait_ge(bank_ready[3], use("wo", 3, 3))
            sp.dma_start(wr[:, :, 0:NG], a["w_group_router"][0].rearrange("(k p) n -> p k n", p=P),
                         allow_slow_non_contiguous=True).then_inc(S["wr_loaded"], 16)
            sp.dma_start(wr[:, :, NG:36], a["w_expert_router"][0].rearrange("(k p) n -> p k n", p=P),
                         allow_slow_non_contiguous=True).then_inc(S["wr_loaded"], 16)

            def expert_unit(e, kind, s):
                if kind < 2:
                    src = (wg_e, wu_e)[kind][:, ds(e, 1)].rearrange("p e k n -> p (e k) n")
                    dst = ring[:, s]
                else:
                    src = wd_e[:, ds(e, 1)].rearrange("p e f n -> p (e f) n")
                    dst = ring[:, s].rearrange("p k n -> p (k n)").rearrange("p (f n) -> p f n", f=2)
                sp.dma_start(dst, src).then_inc(slot_loaded[s], 16)

            used_by = [S["g_ready"], S["u_done"], S["ys_done"]]
            ahead = [0, 1, 1]
            for u in range(RING):
                units = PHASES[-1][2]
                slot_used(PHASES[-1][0], units, 0, len(units) - RING + u)
                expert_unit(u // 3, u % 3, u)
            for u in range(RING, 12):
                sp.wait_ge(used_by[(u - 4) % 3], (u - 4) // 3 + 1 + ahead[(u - 4) % 3])
                expert_unit(u // 3, u % 3, u % RING)
            with sp.Fori(1, 8) as i:
                for u in range(12):
                    sp.wait_ge(used_by[(u - 4) % 3], i * 4 + ((u - 4) // 3 + 1 + ahead[(u - 4) % 3]))
                    expert_unit(i * 4 + u // 3, u % 3, u % RING)

            sp.wait_ge(S["out_rows"], 1)
            sp.dma_start(y_p[0, 0:P].rearrange("p (j n) -> p j n", j=4), yrow_q[0]).then_inc(S["out_done"], 16)
            sp.wait_ge(S["y_fin"], 1)
            sp.dma_start(y_p[0, P:NP].rearrange("p (j n) -> p j n", j=4), yrow_q[1]).then_inc(S["out_done"], 16)
            sp.wait_ge(S["out_rows"], 2)
            sp.dma_start(y_s.rearrange("b l (j n) -> (b l) j n", j=4), yrow_q[2][0:NS]).then_inc(S["out_done"], 16)
            sp.wait_ge(S["out_done"], 64)
            sp.wait_ge(S["tail_out"], 128)
            sp.wait_ge(S["state_copy"], 16)
            for par in range(2):
                sp.wait_ge(st_out[par], 128)
            sp.wait_ge(S["sf_out"], 16 * KC)

        @block.gpsimd
        def _(gp):
            gp.sem_inc(S["scaled"], 1)
            pool.mark(gp.memset(ones[:], 1.0))
            pool.mark(gp.memset(ident[:], 0.0))
            pool.link(gp, gp.memset(blk[:], 1.0))
            pool.mark(gp.affine_select(out=ident[:], in_=ident[:], compare_op=ALU.not_equal, fill=1.0, base=0,
                                       pattern=[[-1, P]], channel_multiplier=1))
            pool.mark(gp.affine_select(out=upper[:], in_=ones[:], compare_op=ALU.is_ge, fill=0.0, base=0,
                                       pattern=[[1, P]], channel_multiplier=-1))

            def by_seq(dst, src, inner):
                pool.link(gp, gp.affine_select(out=dst, in_=src, compare_op=ALU.is_ge, fill=0.0, base=0,
                                               pattern=[[-NL, NB], [0, inner]], channel_multiplier=1))
                pool.link(gp, gp.affine_select(out=dst, in_=dst, compare_op=ALU.is_ge, fill=0.0, base=NL - 1,
                                               pattern=[[NL, NB], [0, inner]], channel_multiplier=-1))

            blk3 = blk[:].rearrange("p (b l) -> p b l", b=NB)
            by_seq(blk3, blk3, NL)
            pool.link(gp, gp.tensor_copy(seqsel[:], blk3[:, :, 0]))
            pool.link(gp, gp.memset(fold, 0.0))
            for q in range(4):
                pool.link(gp, gp.affine_select(out=fold, in_=fold, compare_op=ALU.not_equal, fill=1.0, base=-32 * q,
                                               pattern=[[-1, NSEQ]], channel_multiplier=1))
            gp.tensor_tensor(ublk[:], blk[:], upper[0:NS, 0:NS], ALU.mult).then_inc(S["consts_ready"], 1)

            def modulate_samples(n, shift):
                gp.wait_ge(S["scale_ready"], n + 1)
                for q in range(4):
                    c4 = slice(4 * q, 4 * q + 4)
                    hs_ = bl(hT[:, c4, NP:T])
                    gp.wait_ge(S["hn_ready"], 4 * n + q + 1)
                    pool.link(gp, gp.tensor_tensor(hs_, hs_, bc(scaleA[:, c4, 1:NSEQ], NL), ALU.mult))
                    gp.tensor_tensor(hs_, hs_, bc(mod[:, shift + 4 * q:shift + 4 * q + 4, 1:NSEQ], NL), ALU.add).then_inc(
                        S["hs_ready"], 1)

            modulate_samples(0, 0)
            gp.dma_start(cconv_s[0, :, 0:CK - 1 - NL], a["state_conf_conv"][0, :, NL:CK - 1]).then_inc(S["state_copy"], 16)

            for j in range(2):
                gp.wait_ge(bank_free[j], use("glu", j, 2 * GLU_N - 1))
            gp.wait_ge(S["usamp_ready"], 1)
            acc_s = uvs[:, :, :]
            pool.link(gp, gp.tensor_copy(acc_s, bc(CONF_B, NS)))
            for k in range(CK):
                w = vcol[:, CW0 + k * KC:CW0 + (k + 1) * KC]
                pool.link(gp, gp.tensor_tensor(bl(tmpc), usamp[:, :, :, k:k + NL], bc(w, NB, NL), ALU.mult))
                pool.link(gp, gp.tensor_tensor(acc_s, acc_s, tmpc, ALU.add))
            gp.tensor_copy(vb[:, :, NP:T], acc_s).then_inc(S["vsamp_ready"], 1)

            gp.wait_ge(S["w_ready"], 1)
            gp.wait_ge(S["xtail_out"], 32)
            gp.wait_ge(S["xbc_ready"], XC + 2)
            with gp.Fori(0, G) as g:
                for k in range(4):
                    par = k % 2
                    gp.wait_ge(bank_ready[2], g * 5 + (use("ssd", 2) + k))
                    gp.tensor_copy(dax[0:NS].rearrange("p (h q) -> p h q", h=2),
                                   bc(dtA[0:NS, 2, ds(g * 8 + 2 * k, 2)], HD)).then_inc(S["dax_ready"], 1)
                    for h in range(2):
                        head = g * 8 + (2 * k + h)
                        gp.wait_ge(bank_ready[5 + h], g * 4 + (use("ssd", 5 + h) - 1 + k))
                        gp.tensor_tensor(ud[h][:, 0:NP].rearrange("p (q i) -> p q i", q=2),
                                         upper[:].unsqueeze(1).broadcast_to([P, 2, P]),
                                         dtA[:, 0:2, ds(head, 1)].broadcast_to([P, 2, P]),
                                         ALU.mult).then_inc(S["ud_ready"], 1)
                        gp.tensor_tensor(ud[h][0:NS, NP:T], ublk[:],
                                         dtA[0:NS, 2, ds(head, 1)].broadcast_to([NS, NS]),
                                         ALU.mult).then_inc(S["ud_ready"], 1)
                    gp.wait_ge(bank_ready[1], g * 8 + (use("ssd", 1) + 2 * k))
                    gp.wait_ge(bank_free[2], g * 5 + (use("ssd", 2) + 1 + k))
                    gp.tensor_tensor(s0[:, par], s0[:, par], bc(dec, P), ALU.mult).then_inc(S["scaled"], 1)

            gp.wait_ge(S["merged"], KC)
            gp.wait_ge(bank_ready[3], use("wo", 3, 3))
            for par in range(2):
                gp.wait_ge(st_out[par], 128)
            gp.wait_ge(S["sf_out"], 16 * KC)
            gp.iota(iota_s, pattern=[[1, SLOTS]], base=0, channel_multiplier=0, allow_small_or_imprecise_dtypes=True)
            gp.iota(iota_e, pattern=[[1, NE]], base=0, channel_multiplier=0, allow_small_or_imprecise_dtypes=True)
            gp.affine_select(out=strict, in_=ones[:], compare_op=ALU.is_gt, fill=0.0, base=0,
                             pattern=[[1, P]], channel_multiplier=-1).then_inc(S["pooled"], 1)
            modulate_samples(1, 3 * KC)
            gp.wait_ge(S["pairs_ready"], 1)
            for q, (t0, rows) in enumerate(TOK):
                for out, vA, vB in ((gt, gA, gB), (et, eA, eB)):
                    for dst, s_, v_ in ((out[0:rows, q], sA, vA), (tq[0:rows], sB, vB)):
                        pool.link(gp, gp.tensor_scalar(dst, iota_s[0:rows], s_[0:rows, q:q + 1], v_[0:rows, q:q + 1],
                                                       ALU.is_equal, ALU.mult))
                    pool.link(gp, gp.tensor_tensor(out[0:rows, q], out[0:rows, q], tq[0:rows], ALU.add))
            gp.sem_inc(S["gt_ready"], 1)
            for b in range(4):
                gp.wait_ge(bank_ready[b], use("gates", b))
            gp.memset(ys, 0.0).then_inc(S["ys_zero"], 1)

        @block.scalar
        def _(ac):
            ac.wait_ge(S["vrow_zero"], 1)
            at = 0
            for tile, at, name, n in ((0, 0, "b_ada", 96), (0, 96, "norm_mix_g", KC), (0, 112, "norm_ffn_g", KC),
                                      (1, 0, "ssd_conv_b", XC), (1, 24, "ssd_norm_g", KC), (1, 40, "conf_conv_b", KC),
                                      (1, 56, "conf_ln_g", KC), (1, 72, "conf_ln_b", KC)):
                ac.dma_start(vrow[at:at + n, tile], a[name][0].rearrange("(r p) -> r p", p=P)).then_inc(S["v_loaded"], 16)
            ac.dma_start(vrow[88:104, 1], a["final_norm_g"].rearrange("(r p) -> r p", p=P)).then_inc(S["v_loaded"], 16)
            ac.dma_start(vrow[0:96, 2], a["ssd_conv_w"][0].rearrange("k (r p) -> (k r) p", p=P)).then_inc(S["v_loaded"], 16)
            cw = a["conf_conv_w"][0].rearrange("k (r p) -> (k r) p", p=P)
            for t_ in range(4):
                n = min(P, CK * KC - P * t_)
                ac.dma_start(vrow[0:n, 3 + t_], cw[P * t_:P * t_ + n]).then_inc(S["v_loaded"], 16)
            ac.sem_inc(S["small_first"], 1)
            for half in range(2):
                ac.dma_start(cstrow[0:120, half],
                             a["state_conf_conv"][0, 4 * half:4 * half + 4].rearrange("b k n -> (b k) n")).then_inc(
                                 S["cst_loaded"], 16)
                ac.dma_start(dcol[HD * half:HD * half + HD, :],
                             a["ssd_d"][0].rearrange("(c h) -> h c", h=2)[half:half + 1].broadcast_to([HD, KC]),
                             allow_slow_non_contiguous=True).then_inc(S["small_loaded"], 16)
            ac.dma_start(rows_bc[:, 0], a["ssd_dt_bias"].broadcast_to([P, H])).then_inc(S["small_loaded"], 16)
            ac.dma_start(rows_bc[:, 1], a["ssd_a_log"].broadcast_to([P, H])).then_inc(S["small_loaded"], 16)
            ac.dma_start(rbias[:, 0:NG], a["b_group_router"].broadcast_to([P, NG])).then_inc(S["small_loaded"], 16)
            ac.dma_start(rbias[:, NG:36], a["b_expert_router"].broadcast_to([P, NE])).then_inc(S["small_loaded"], 16)

            ac.sem_inc(S["sil_ready"], 1)
            ac.sem_inc(S["xbc_ready"], 1)
            ac.wait_ge(bank_ready[4], use("c", 4))
            ac.activation(cT.rearrange("p k n -> p (k n)"), bank[4][:, 0:KC * NSEQ], ACT.Silu).then_inc(bank_free[4], 1)

            def walk(name, part, on_unit=None, before=None):
                steps, units = {n: (s_, u_) for n, s_, u_ in PHASES}[name]
                na = units.count("a")

                def modulation(i, n):
                    b = 6 + n % 2
                    ac.wait_ge(bank_ready[b], i * (na // 2) + use(name, b, n // 2))
                    for j in range(2):
                        c = i * (2 * na) + (2 * (ada0[name] + n) + j)
                        ins = ac.activation(mod[:, ds(c, 1)].rearrange("p k n -> p (k n)"),
                                            bank[b][:, NSEQ * j:NSEQ * (j + 1)], ACT.Identity, bias=vcol[:, ds(c, 1)])
                    ins.then_inc(bank_free[b], 1)

                with steps_of(ac, steps) as i:
                    owed = None
                    for u, kind in enumerate(units):
                        n, b, k, per = place(units, u)
                        if before:
                            before(u)
                        if kind == "a":
                            ac.wait_ge(bank_ready[b], i * per + use(name, b, k))
                            ac.wait_ge(bank_ready[b + 2], i * per + (use(name, b + 2, k) - 1))
                            for q in range(4):
                                rows = slice(32 * q, 32 * q + NSEQ)
                                ins = ac.activation(part[rows, n % 2], bank[b][rows, 0:UC], ACT.Copy)
                            ins.then_inc(bank_free[b], 1)
                        elif on_unit:
                            on_unit(i, n)
                        if owed is not None:
                            modulation(i, owed)
                        owed = n if kind == "a" else None
                    if owed is not None:
                        modulation(i, owed)

            def square(src, dst, of_quarter=None, done=0):
                for q in range(4):
                    if of_quarter:
                        ac.wait_ge(S[of_quarter[0]], done + of_quarter[1] * (q + 1))
                    ac.activation(dst[:, 4 * q:4 * q + 4], src[:, 4 * q:4 * q + 4], ACT.Square).then_inc(
                        S["squares_ready"], 1)

            def root(n, src=stat, dst=rs):
                ac.wait_ge(S["mean_ready"], n)
                ac.activation(dst[:], src[:], ACT.Sqrt).then_inc(S["root_ready"], 1)

            for b in range(4):
                ac.wait_ge(bank_free[b], use("x", b, 3))
            square(xT, sq)
            root(1)
            ac.wait_ge(S["part_zero"], 1)
            walk("ada", part_glu)
            walk("ada2", part_glu)

            def modulate_prompt(n, shift):
                ac.wait_ge(S["scale_ready"], n + 1)
                for c in range(KC // 2, KC):
                    if c % 4 == 0:
                        ac.wait_ge(S["hn_ready"], 4 * n + c // 4 + 1)
                    ac.activation(hT[:, c, 0:NP], hT[:, c, 0:NP], ACT.Identity, scale=scaleA[:, c, 0:1],
                                  bias=mod[:, shift + c, 0:1]).then_inc(S["h_ready"], 1)

            modulate_prompt(0, 0)

            def glu_gate(i, u):
                if u % 2 == 0:
                    return
                q = u // 2
                for j in range(2):
                    n = 2 * (q % 2) + j
                    ac.wait_ge(bank_ready[2 + j], i * 4 + (use("glu", 2 + j) + q))
                    ac.wait_ge(bank_free[j], i * 4 + (use("glu", j) - 2 + q))
                    ac.activation(sgl[:, n], bank[2 + j][:, 0:T], ACT.Sigmoid).then_inc(bank_free[2 + j], 1)

            def to_buffer(name, dst, func):
                def on_unit(i, u):
                    for j in range(2):
                        c = 2 * u + j
                        b = c % 4
                        ac.wait_ge(bank_ready[b], use(name, b, c // 4))
                        ac.activation(dst[:, c], bank[b][:, 0:T], func).then_inc(bank_free[b], 1)
                return on_unit

            walk("glu", part_glu, glu_gate)
            for q in range(4):
                ac.wait_ge(bank_ready[4 + q], use("tail", 4 + q))
                act.mark(ac.activation(tailrow[0:CK - 1 + NS, 512 * q:512 * q + 512], bank[4 + q][0:CK - 1 + NS], ACT.Copy))
                act.wait(ac)
                ac.sem_inc(bank_free[4 + q], 1)
                ac.sem_inc(S["tail_rows"], 1)
            ac.wait_ge(S["part_zero"], 2)
            walk("gc", part_mix, to_buffer("gc", gb, ACT.Sigmoid))
            ac.wait_ge(S["tail_out"], 128)
            ac.wait_ge(S["out_done"], 16)
            square(vb, sq_ln, ("centred", 1))
            walk("z1", part_mix, to_buffer("z1", zb, ACT.Silu))
            root(2)
            for c in range(KC):
                if c % 4 == 0:
                    ac.wait_ge(S["v_ready"], c // 4 + 1)
                ac.activation(vb[:, c], vb[:, c], ACT.Silu, bias=LN_B[:, c:c + 1], scale=LN_G[:, c:c + 1]).then_inc(
                    S["vb_free"], 1)
            ac.wait_ge(S["small_loaded"], 96)
            ac.activation(rows_bc[:, 1], rows_bc[:, 1], ACT.Exp).then_inc(S["a_exp"], 1)
            ac.wait_ge(S["dt_abs"], 1)
            ac.activation(sp_e, sp_abs, ACT.Exp, scale=-1.0).then_inc(S["dt_exp"], 1)
            ac.wait_ge(S["one_plus"], 1)
            ac.activation(sp_ln, sp_u, ACT.Ln).then_inc(S["dt_log"], 1)
            walk("co", part_mix)
            ac.wait_ge(S["w_arg"], 1)
            ac.activation(wend[:], wend[:], ACT.Exp).then_inc(S["w_exp"], 1)
            with ac.Fori(0, XBC_N) as i:
                for c in range(8):
                    ac.wait_ge(S["acc_ready"], i * 8 + c + 1)
                    ac.activation(xbcT[:, ds(i * 8 + c, 1), 0:NP].rearrange("p k n -> p (k n)"), acc[:, c % 2],
                                  ACT.Silu, bias=vcol[:, ds(P + i * 8 + c, 1)]).then_inc(S["xbc_ready"], 1)
            ac.wait_ge(S["xpad_ready"], 1)
            ac.activation(xbcT[:, :, NP:T], tmps, ACT.Silu).then_inc(S["xbc_ready"], 1)
            def copy_x(g, k, transposed):
                ac.wait_ge(bank_ready[3], transposed)
                ac.activation(xst, xbcT[:, ds(g * 4 + k, 1)].rearrange("p k n -> p (k n)"), ACT.Copy).then_inc(
                    S["xst_ready"], 1)

            def copy_b(g):
                ac.activation(bst, xbcT[:, ds(KC + g, 1)].rearrange("p k n -> p (k n)"), ACT.Copy).then_inc(
                    S["bst_ready"], 1)

            def xtail_rows():
                for n in range(6):
                    b = 4 + n % 4
                    ac.wait_ge(bank_ready[b], use("xtail", b, n // 4))
                    act.mark(ac.activation(sstrow[0:(SK - 1) * (1 + NB), 512 * n:512 * n + 512],
                                           bank[b][0:(SK - 1) * (1 + NB)], ACT.Copy))
                    act.wait(ac)
                    ac.sem_inc(bank_free[b], 1)
                    ac.sem_inc(S["xrow_ready"], 1)

            z2_silu = to_buffer("z2", zb[:, KC // 2:], ACT.Silu)

            def z2_unit(i, n):
                if n == 2:
                    xtail_rows()
                if n == 3:
                    ac.wait_ge(S["xtail_out"], 32)
                    copy_b(0)
                    copy_x(0, 0, use("ssd", 3) - 1)
                z2_silu(i, n)

            walk("z2", None, z2_unit)

            ac.sem_inc(S["sf_free"], 1)
            with ac.Fori(0, G) as g:
                for k in range(4):
                    ac.wait_ge(bank_ready[7], g * 4 + (use("ssd", 7) - 1 + k))
                    for b in range(2):
                        ac.wait_ge(bank_ready[b], g * 8 + (use("ssd", b) + 2 * k))
                        ac.activation(s0T[:, 4 * b:4 * b + 4], bank[b][:].rearrange("p (b n) -> p b n", b=4),
                                      ACT.Copy).then_inc(bank_free[b], 1)
                    for h in range(2):
                        ac.wait_ge(S["seg_ready"], g * 8 + (2 * k + h + 1))
                        ac.activation(mt[:, h, 0:NP], mt[:, h, 0:NP], ACT.Exp)
                        ac.activation(mt[0:NS, h, NP:T], mt[0:NS, h, NP:T], ACT.Exp).then_inc(S["exp_ready"], 1)
                        ac.activation(cs[:, h], bank[5 + h][:, P:T], ACT.Exp).then_inc(bank_free[5 + h], 1)
                    if k == 3:
                        copy_b(g + 1)
                    ac.wait_ge(bank_ready[2], g * 5 + (use("ssd", 2) + 1 + k))
                    ac.wait_ge(S["sf_free"], g * 4 + (k + 1))
                    ac.wait_ge(S["scaled"], g * 4 + k + 1)
                    ac.activation(s1T, bank[2][:, 0:P], ACT.Copy)
                    ac.activation(sfin, bank[2][:, P:2 * P], ACT.Copy)
                    ac.activation(dec, bank[2][:, 2 * P:2 * P + NB], ACT.Exp).then_inc(bank_free[2], 1)
                    copy_x(g, k + 1, g * 5 + (use("ssd", 3) + 1 + k))
                    ac.wait_ge(bank_ready[4], g * 4 + (use("ssd", 4) + k))
                    ac.wait_ge(S["y_done"], g * 4 + (k + 1))
                    ac.sem_inc(S["x_used"], 1)
                    ac.activation(vb[:, ds(g * 4 + k, 1)].rearrange("p k n -> p (k n)"), bank[4][:, 0:T],
                                  ACT.Copy).then_inc(bank_free[4], 1)
            ac.wait_ge(S["y_done"], KC)
            for q in range(4):
                ac.activation(hT[:, 4 * q:4 * q + 4], zb[:, 4 * q:4 * q + 4], ACT.Square).then_inc(S["gsq_ready"], 1)
            for q in range(4):
                ac.wait_ge(S["gmean_ready"], q + 1)
                ac.activation(grs[:, q], grs[:, q], ACT.Sqrt).then_inc(S["groot_ready"], 1)
            ac.wait_ge(S["part_zero"], 3)

            def gate_sigmoid(u):
                if u == 4:
                    ac.wait_ge(bank_free[4], use("ssd", 4, KC - 1))
                    for q in range(4):
                        ac.activation(vb[:, 4 * q:4 * q + 4], vb[:, 4 * q:4 * q + 4], ACT.Sigmoid).then_inc(
                            S["sig_ready"], 1)

            walk("so", part_mix, before=gate_sigmoid)
            walk("wo", part_mix)
            ac.wait_ge(S["merged"], KC)
            square(xT, sq, ("x_mid", 4))
            root(3)

            def modulation_and_router(u):
                if u == 1:
                    modulate_prompt(1, 3 * KC)
                if u == 3:
                    ac.wait_ge(S["e_arg"], 1)
                    ac.activation(lg[:, :, 0:NG], lg[:, :, 0:NG], ACT.Exp).then_inc(S["gexp"], 1)
                    ac.wait_ge(S["e_arg"], 2)
                    ac.activation(sel[:], sel[:], ACT.Exp).then_inc(S["eexp"], 1)

            walk("rt", part_mix, before=modulation_and_router)
            for c in range(KC):
                ac.wait_ge(bank_ready[4 + c % 2], use("gather", 4 + c % 2, c // 2))
                if c >= 2:
                    ac.wait_ge(bank_ready[2 * (c % 2) + 1], use("gather", 2 * (c % 2) + 1, c // 2 - 1))
                ac.activation(htok[:, c % 2, 0:2 * P], bank[4 + c % 2][:, 0:2 * P], ACT.Copy)
                ac.activation(htok[0:NS, c % 2, 2 * P:3 * P], bank[4 + c % 2][0:NS, 2 * P:3 * P], ACT.Copy).then_inc(
                    bank_free[4 + c % 2], 1)
            with ac.Fori(0, 8) as i:
                for k in range(4):
                    ac.wait_ge(S["g_ready"], i * 4 + (k + 1))
                    ac.wait_ge(S["hid_ready"], i * 4 + (k + 1))
                    n_pairs = ac.value_load(meta_i[0:1, 0, ds(i * 4 + k, 1)], min_val=0, max_val=T)
                    with ac.If(n_pairs > WIN):
                        ac.activation(sil[:, 0], bank[4][:, 0:T], ACT.Silu)
                        ac.activation(sil[:, 1], bank[6][:, 0:T], ACT.Silu).then_inc(S["sil_ready"], 1)
                    with ac.Else():
                        ac.activation(sil[:, 0, 0:P], bank[4][:, 0:P], ACT.Silu).then_inc(S["sil_ready"], 1)
            def sorted_rows(c):
                for b in range(2):
                    bb = 4 + 2 * (c % 2) + b
                    ac.wait_ge(bank_ready[bb], use("unsort", bb, c // 2))
                    if c >= 2:
                        ac.wait_ge(bank_ready[c % 2], use("unsort", c % 2, c // 2 - 1))
                    if b == 0:
                        ac.activation(ytok[:, c % 2, 0:3 * P], bank[bb][:, 0:3 * P], ACT.Copy).then_inc(bank_free[bb], 1)
                    else:
                        ac.activation(ytok[:, c % 2, 3 * P:4 * P], bank[bb][:, 0:P], ACT.Copy)
                        ac.activation(ytok[0:HD, c % 2, 4 * P:5 * P], bank[bb][0:HD, P:2 * P], ACT.Copy).then_inc(
                            bank_free[bb], 1)

            def result_rows(j, q):
                rows = TOK[q][1]
                ac.wait_ge(bank_ready[2], use("unsort", 2, 3 * j + q))
                ac.activation(yrow[j][0:rows, q], bank[2][0:rows], ACT.Copy).then_inc(bank_free[2], 1)

            def result_squares(j):
                ac.wait_ge(S["moe_ready"], 4 * j + 4)
                ac.activation(hT[:, 4 * j:4 * j + 4], xT[:, 4 * j:4 * j + 4], ACT.Square).then_inc(S["squares_ready"], 1)

            sorted_rows(0)
            for c in range(KC):
                if c + 1 < KC:
                    sorted_rows(c + 1)
                if c >= 4:
                    j = c // 4 - 1
                    if c % 4 == 0:
                        result_squares(j)
                    if c % 4 < 3:
                        result_rows(j, c % 4)
            result_squares(3)
            root(4)
            for q in range(3):
                result_rows(3, q)
            ac.wait_ge(bank_free[4], use("n3", 4))
            ac.wait_ge(bank_free[2], use("unsort", 2, 11))
            ac.activation(yrow_q[0], yrow_q[0], ACT.Identity, scale=rcol[:, 0:1]).then_inc(S["out_rows"], 1)
            ac.activation(yrow_q[2][0:NS], yrow_q[2][0:NS], ACT.Identity, scale=rcol[0:NS, 2:3]).then_inc(S["out_rows"], 1)


        @block.tensor
        def _(pe):
            def fill(name, b, k=0):
                pe.wait_ge(bank_free[b], use(name, b, k) - 1)

            def project(name, rhs=None, before=None, rhs_ready=None):
                steps, units = {n: (s_, u_) for n, s_, u_ in PHASES}[name]

                def fold_sums(i, n):
                    b = 6 + n % 2
                    per = units.count("a") // 2
                    pe.wait_ge(bank_free[b - 2], i * per + use(name, b - 2, n // 2))
                    pe.wait_ge(bank_free[b], i * per + (use(name, b, n // 2) - 1))
                    part = part_glu if name in ("ada", "ada2", "glu") else part_mix
                    for j in range(2):
                        mm = nc.tensor.matmul(bank[b][:, NSEQ * j:NSEQ * (j + 1)], part[:, n % 2, j * P:(j + 1) * P],
                                              fold, start=True, stop=True)
                    mm.then_inc(bank_ready[b], 1)

                with steps_of(pe, steps) as i:
                    owed = None
                    for u, kind in enumerate(units):
                        if before:
                            before(u)
                        s, r = u % RING, u // RING
                        n, last, k, per = place(units, u)
                        pe.wait_ge(slot_loaded[s], i * (16 * len(units) // RING) + 16 * (ring0[name] + r + 1))
                        if kind == "p":
                            for j in range(2):
                                c = 2 * n + j
                                b = c % 4
                                pe.wait_ge(bank_free[b], i * per + (use(name, b, c // 4) - 1))
                                for kk in range(KC):
                                    if rhs_ready and n == 0 and j == 0 and kk % 4 == 0:
                                        for what, per_quarter in rhs_ready:
                                            if per_quarter(kk // 4 + 1) > 0:
                                                pe.wait_ge(S[what], per_quarter(kk // 4 + 1))
                                    mm = nc.tensor.matmul(bank[b][:, 0:T], ring[:, s, kk, j * P:(j + 1) * P], rhs[:, kk],
                                                          start=(kk == 0), stop=(kk == KC - 1))
                                mm.then_inc(bank_ready[b], 1)
                        else:
                            pe.wait_ge(bank_free[last], i * per + (use(name, last, k) - 1))
                            for kk in range(KC):
                                q = kk % 4
                                mm = nc.tensor.matmul(bank[last][32 * q:32 * q + NSEQ, 0:UC], cT[:, kk], ring[:, s, kk],
                                                      start=(kk < 4), stop=(kk >= KC - 4))
                            mm.then_inc(bank_ready[last], 1)
                        if owed is not None:
                            fold_sums(i, owed)
                        owed = n if kind == "a" else None
                    if owed is not None:
                        fold_sums(i, owed)

            def ones_sum(name, src, b, chunks, squares=None):
                fill(name, b)
                for n, c in enumerate(chunks):
                    if squares is not None and c % 4 == 0:
                        pe.wait_ge(S["squares_ready"], squares + c // 4 + 1)
                    mm = nc.tensor.matmul(bank[b][:, 0:T], ones[:], src[:, c], start=(n == 0), stop=(n == len(chunks) - 1))
                mm.then_inc(bank_ready[b], 1)

            pe.sem_inc(S["u_done"], 1)
            pe.wait_ge(S["consts_ready"], 1)
            pe.wait_ge(S["x_loaded"], 32)
            for c in range(KC):
                b = c % 4
                fill("x", b, c // 4)
                for q, (t0, rows) in enumerate(TOK):
                    mm = nc.tensor.transpose(bank[b][:, t0:t0 + rows], xrow[0:rows, q, c * P:(c + 1) * P],
                                             ident[0:rows, 0:rows])
                mm.then_inc(bank_ready[b], 1)
            pe.wait_ge(S["c_loaded"], 32)
            fill("c", 4)
            for c in range(KC):
                mm = nc.tensor.transpose(bank[4][:, NSEQ * c:NSEQ * (c + 1)], crow[0:NSEQ, c * P:(c + 1) * P],
                                         ident[0:NSEQ, 0:NSEQ])
            mm.then_inc(bank_ready[4], 1)
            pe.wait_ge(S["v_loaded"], 14 * 16)
            for b, tiles in ((5, range(4)), (6, range(4, 7))):
                fill("vec", b)
                for n, t_ in enumerate(tiles):
                    mm = nc.tensor.transpose(bank[b][:, n * P:(n + 1) * P], vrow[:, t_], ident[:])
                mm.then_inc(bank_ready[b], 1)
            pe.wait_ge(bank_free[4], use("c", 4))
            ones_sum("n1", sq, 4, range(KC), squares=0)
            project("ada")

            def conf_states(u):
                if u != 1:
                    return
                pe.wait_ge(S["cst_loaded"], 32)
                for c in range(KC):
                    b = c % 4
                    fill("cst", b, c // 4)
                    for half in range(2):
                        mm = nc.tensor.transpose(bank[b][:, 120 * half:120 * half + 120],
                                                 cstrow[0:120, half, c * P:(c + 1) * P], ident[0:120, 0:120])
                    mm.then_inc(bank_ready[b], 1)

            project("ada2", before=conf_states)
            project("glu", hT, rhs_ready=[("hs_ready", lambda q: q), ("hd_ready", lambda q: min(4 * q, KC // 2)),
                                          ("h_ready", lambda q: 4 * q - KC // 2)])
            for j in range(2):
                pe.wait_ge(bank_free[j], use("glu", j, 2 * GLU_N - 1))
            for q in range(4):
                fill("tail", 4 + q)
                for n in range(4):
                    mm = nc.tensor.transpose(bank[4 + q][0:CK - 1 + NS, n * P:(n + 1) * P], utail[:, 4 * q + n], ident[:])
                mm.then_inc(bank_ready[4 + q], 1)
            project("gc", hT)
            pe.wait_ge(S["conv_ready"], 1)
            pe.wait_ge(S["vsamp_ready"], 1)
            ones_sum("ln", vb, 4, range(KC))
            project("z1", hT)
            ones_sum("lnsq", sq_ln, 5, range(KC), squares=4)
            pe.wait_ge(S["wdt_loaded"], 16)
            fill("dt", 6)
            for q, (t0, rows) in enumerate(TOK):
                for k in range(KC):
                    mm = nc.tensor.matmul(bank[6][0:rows, H * q:H * (q + 1)], hT[:, k, t0:t0 + rows], wdt[:, k],
                                          start=(k == 0), stop=(k == KC - 1))
            mm.then_inc(bank_ready[6], 1)
            project("co", vb, rhs_ready=[("vb_free", lambda q: 4 * q)])
            pe.wait_ge(S["dta_ready"], 1)
            fill("cum", 7)
            for q, (lhs, rows) in enumerate(((upper[:], P), (upper[:], P), (ublk[:], NS))):
                nc.tensor.matmul(bank[7][0:rows, H * q:H * (q + 1)], lhs, dtA[0:rows, q], start=True, stop=True)
            for q, (lhs, rows) in enumerate(((ones[:], P), (ones[:], P), (blk[:], NS))):
                mm = nc.tensor.matmul(bank[7][0:rows, H * (3 + q):H * (4 + q)], lhs, dtA[0:rows, q], start=True, stop=True)
            mm.then_inc(bank_ready[7], 1)
            pe.wait_ge(S["sst_loaded"], 16)
            R = NB * (SK - 1)
            for half in range(2):
                fill("sst", 4 + half)
                for n in range(12):
                    c = 12 * half + n
                    mm = nc.tensor.transpose(bank[4 + half][:, R * n:R * (n + 1)], sstrow[0:R, c * P:(c + 1) * P],
                                             ident[0:R, 0:R])
                mm.then_inc(bank_ready[4 + half], 1)
            project("xbc", hT)
            def xtail_to_rows(u):
                if u != 2:
                    return
                pe.wait_ge(S["xtail_ready"], 1)
                R = (SK - 1) * (1 + NB)
                for n in range(6):
                    b = 4 + n % 4
                    fill("xtail", b, n // 4)
                    for j in range(4):
                        mm = nc.tensor.transpose(bank[b][0:R, j * P:(j + 1) * P], xtail[:, 4 * n + j], ident[:])
                    mm.then_inc(bank_ready[b], 1)

            project("z2", hT, before=xtail_to_rows)

            pe.wait_ge(S["w_ready"], 1)
            pe.wait_ge(S["xbc_ready"], XC + 2)
            def of(g, per, at):
                return g[0] * (2 * per) + (g[1] * per + at)

            with pe.Fori(0, G // 2) as i:
                for gg in range(2):
                    g = (i, gg)
                    pe.wait_ge(S["bst_ready"], of(g, 1, 1))
                    pe.wait_ge(bank_free[3], of(g, 5, use("ssd", 3) - 1))
                    for q, (t0, rows) in enumerate(TOK):
                        mm = nc.tensor.matmul(bank[3][0:rows, q * P:q * P + rows], bst[:, t0:t0 + rows],
                                              xbcT[:, ds(of(g, 1, KC + G), 1), t0:t0 + rows].rearrange("p k n -> p (k n)"),
                                              start=True, stop=True)
                    mm.then_inc(bank_ready[3], 1)
                    pe.wait_ge(bank_free[2], of(g, 5, use("ssd", 2) - 1))
                    for q, (t0, rows) in enumerate(TOK):
                        mm = nc.tensor.transpose(bank[2][0:rows, q * P:(q + 1) * P], bst[:, t0:t0 + rows], ident[:])
                    mm.then_inc(bank_ready[2], 1)
                    for k in range(4):
                        par = k % 2
                        pe.wait_ge(S["xst_ready"], of(g, 4, k + 1))
                        pe.wait_ge(bank_free[3], of(g, 5, use("ssd", 3) + k))
                        for q, (t0, rows) in enumerate(TOK):
                            mm = nc.tensor.transpose(bank[3][0:rows, q * P:(q + 1) * P], xst[:, t0:t0 + rows], ident[:])
                        mm.then_inc(bank_ready[3], 1)
                        pe.wait_ge(s0_loaded[par], of(g, 32, 16 * (k // 2) + 16))
                        for b in range(2):
                            pe.wait_ge(bank_free[b], of(g, 8, use("ssd", b) - 1 + 2 * k))
                            for n in range(4):
                                mm = nc.tensor.transpose(bank[b][:, n * P:(n + 1) * P], s0[:, par, 4 * b + n], ident[:])
                            mm.then_inc(bank_ready[b], 1)
                        for h in range(2):
                            pe.wait_ge(S["ud_ready"], of(g, 16, 4 * k + 2 * h + 2))
                            pe.wait_ge(bank_free[5 + h], of(g, 4, use("ssd", 5 + h) - 1 + k))
                            nc.tensor.matmul(bank[5 + h][:, 0:NP], ones[:], ud[h][:, 0:NP], start=True, stop=True)
                            nc.tensor.matmul(bank[5 + h][:, NP:T], ones[0:NS, :], ud[h][0:NS, NP:T],
                                             start=True, stop=True).then_inc(bank_ready[5 + h], 1)
                        if k % 2 == 0:
                            pe.wait_ge(slot_loaded[2 * gg + k // 2], i * 16 + 16 * (ring0["gs"] + 1))
                        pe.wait_ge(bank_free[4], of(g, 4, use("ssd", 4) - 1 + k))
                        for kk in range(KC):
                            mm = nc.tensor.matmul(bank[4][:, 0:T], ring[:, 2 * gg + k // 2, kk, par * P:(par + 1) * P],
                                                  hT[:, kk], start=(kk == 0), stop=(kk == KC - 1))
                        mm.then_inc(bank_ready[4], 1)
                        pe.wait_ge(S["xw_ready"], of(g, 4, k + 1))
                        pe.wait_ge(S["dax_ready"], of(g, 4, k + 1))
                        pe.wait_ge(bank_free[2], of(g, 5, use("ssd", 2) + k))
                        nc.tensor.matmul(bank[2][:, 0:P], btok[:, 0], xw[:, 0], start=True, stop=True)
                        nc.tensor.matmul(bank[2][:, P:2 * P], xw[:, 1], btok[:, 0], start=True, stop=False)
                        nc.tensor.matmul(bank[2][:, P:2 * P], xw[:, 2], btok[:, 1], start=False, stop=True)
                        nc.tensor.matmul(bank[2][:, 2 * P:2 * P + NB], dax[0:NS], seqsel[:], start=True,
                                         stop=True).then_inc(bank_ready[2], 1)
                        pe.wait_ge(S["bexp_ready"], of(g, 1, 1))
                        for b in range(2):
                            pe.wait_ge(bank_free[b], of(g, 8, use("ssd", b) + 2 * k))
                            nc.tensor.matmul(bank[b][:], xw[0:NS, 3], bexp[0:NS, 4 * b:4 * b + 4], start=True,
                                             stop=True).then_inc(bank_ready[b], 1)
                        pe.wait_ge(S["m_ready"], of(g, 8, 2 * k + 2))
                        pe.wait_ge(bank_free[2], of(g, 5, use("ssd", 2) + 1 + k))
                        pe.wait_ge(bank_free[7], of(g, 4, use("ssd", 7) - 1 + k))
                        for h in range(2):
                            hc = slice(HD * h, HD * (h + 1))
                            y = bank[7][hc]
                            nc.tensor.matmul(y[:, 0:P], xtok[:, 0, hc], mt[:, h, 0:P], start=True, stop=True)
                            nc.tensor.matmul(y[:, P:NP], xtok[:, 1, hc], mt[:, h, P:NP], start=True, stop=False)
                            nc.tensor.matmul(y[:, P:NP], s1T[:, hc], cs[:, h, 0:P], start=False, stop=True)
                            nc.tensor.matmul(y[:, NP:T], xtok[0:NS, 2, hc], mt[0:NS, h, NP:T], start=True, stop=True)
                            for b in range(NB):
                                mm = nc.tensor.matmul(y[:, NP + NL * b:NP + NL * (b + 1)], s0T[:, b, hc],
                                                      cs[:, h, P + NL * b:P + NL * (b + 1)], start=False,
                                                      stop=True, skip_group_check=True)
                        mm.then_inc(bank_ready[7], 1)

            def group_sums(u):
                if u == 1:
                    for q in range(G):
                        pe.wait_ge(S["gsq_ready"], q + 1)
                        ones_sum("gn", hT, q, range(4 * q, 4 * q + 4))

            project("so", zb, before=group_sums, rhs_ready=[("y_ready", lambda q: q)])
            pe.wait_ge(S["merged"], KC)
            project("wo", gb)
            def norm_and_logits(u):
                if u == 0:
                    ones_sum("n2", sq, 0, range(KC), squares=8)
                if u == 2:
                    logits()

            def logits():
                pe.wait_ge(S["wr_loaded"], 32)
                fill("route", 1)
                for q, (t0, rows) in enumerate(TOK):
                    if q == 2:
                        pe.wait_ge(S["hs_ready"], 8)
                    for k in range(KC):
                        if q == 0 and k % 4 == 0:
                            pe.wait_ge(*((S["hd_ready"], KC // 2 + k + 4) if k < KC // 2 else (S["h_ready"], k + 4)))
                        mm = nc.tensor.matmul(bank[1][0:rows, 36 * q:36 * (q + 1)], hT[:, k, t0:t0 + rows], wr[:, k],
                                              start=(k == 0), stop=(k == KC - 1))
                mm.then_inc(bank_ready[1], 1)

            project("rt", before=norm_and_logits)
            pe.wait_ge(S["cnt_ready"], 1)
            pe.wait_ge(S["pooled"], 1)
            fill("route", 2)
            for q, (t0, rows) in enumerate(TOK):
                mm = nc.tensor.matmul(bank[2][0:NE, 0:1], chosen[0:rows, q], ones[0:rows, 0:1], start=(q == 0), stop=(q == 2))
            mm.then_inc(bank_ready[2], 1)
            pe.wait_ge(S["cnt_ready"], 2)
            fill("route", 3)
            for q, (t0, rows) in enumerate(TOK):
                out = bank[3][0:rows, NE * q:NE * (q + 1)]
                nc.tensor.matmul(out, cntb[0:NE, 0:rows], strict[0:NE, 0:NE], start=True, stop=False)
                for q2 in range(q):
                    nc.tensor.matmul(out, ones[:, 0:rows], chosen[:, q2], start=False, stop=False)
                nc.tensor.matmul(out, strict[0:rows, 0:rows], chosen[0:rows, q], start=False, stop=True)
            nc.tensor.matmul(bank[3][:, 96:128], cntb[0:NE], strict[0:NE, 0:NE], start=True, stop=True)
            nc.tensor.matmul(bank[3][:, 128:160], cntb[0:NE], ident[0:NE, 0:NE], start=True, stop=True).then_inc(
                bank_ready[3], 1)
            def to_rows(c):
                b = 4 + c % 2
                fill("gather", b, c // 2)
                for q, (t0, rows) in enumerate(TOK):
                    mm = nc.tensor.transpose(bank[b][0:rows, q * P:(q + 1) * P], hT[:, c, t0:t0 + rows], ident[:])
                mm.then_inc(bank_ready[b], 1)

            to_rows(0)
            for c in range(KC):
                if c + 1 < KC:
                    to_rows(c + 1)
                pe.wait_ge(bank_free[4 + c % 2], use("gather", 4 + c % 2, c // 2))
                for half in range(2):
                    b = 2 * (c % 2) + half
                    fill("gather", b, c // 2)
                    for q, (t0, rows) in enumerate(TOK):
                        if c == 0 and half == 0:
                            pe.wait_ge(S["sort_ready"], q + 1)
                        mm = nc.tensor.matmul(bank[b][:, 0:T], htok[0:rows, c % 2, q * P:(q + 1) * P],
                                              pm[0:rows, q, T * half:T * (half + 1)], start=(q == 0), stop=(q == 2))
                    mm.then_inc(bank_ready[b], 1)

            pe.wait_ge(S["gt_ready"], 1)
            for b in range(4):
                fill("gates", b)
                src = (gt, et)[b // 2]
                for q, (t0, rows) in enumerate(TOK):
                    mm = nc.tensor.matmul(bank[b][:, 0:T], ones[0:rows, :], src[0:rows, q, T * (b % 2):T * (b % 2 + 1)],
                                          start=(q == 0), stop=(q == 2))
                mm.then_inc(bank_ready[b], 1)

            for b in range(4):
                fill("unsort", b)
            for b in (4, 5):
                fill("pt", b)
            pe.wait_ge(S["meta_ready"], 1)
            with pe.Fori(0, 8) as i:
                for k in range(4):
                    u = 3 * k
                    slots = [(u + n) % RING for n in range(3)]
                    landed = [i * 48 + (MOE_R + (u + n) // RING + 1) * 16 for n in range(3)]
                    n_pairs = pe.value_load(meta_i[0:1, 0, ds(i * 4 + k, 1)], min_val=0, max_val=T)
                    w_gate, w_up = ring[:, slots[0]], ring[:, slots[1]]
                    w_down = ring[:, slots[2]].rearrange("p k n -> p (k n)").rearrange("p (f n) -> p f n", f=2)
                    pe.wait_ge(slot_loaded[slots[0]], landed[0])
                    pe.wait_ge(S["win_ready"], i * 4 + (k + 1))
                    pe.wait_ge(S["sil_ready"], i * 4 + (k + 1))
                    with pe.If(n_pairs > WIN):
                        w0 = pe.value_load(meta_i[0:1, 2, ds(i * 4 + k, 1)], min_val=0, max_val=SLOTS - T)
                        for n, (w, done, gone) in enumerate(((w_gate, "g_ready", "sil_ready"), (w_up, "u_done", "hid_ready"))):
                            if n:
                                pe.wait_ge(slot_loaded[slots[1]], landed[1])
                                pe.wait_ge(S["hid_ready"], i * 4 + (k + 1))
                            for f in range(2):
                                for kk in range(KC):
                                    mm = nc.tensor.matmul(bank[4 + n + 2 * f][:, 0:T], w[:, kk, f * P:(f + 1) * P],
                                                          hs[:, kk, ds(w0, T)], start=(kk == 0), stop=(kk == KC - 1))
                            mm.then_inc(S[done], 1)
                        pe.wait_ge(slot_loaded[slots[2]], landed[2])
                        pe.wait_ge(S["hid_ready"], i * 4 + (k + 2))
                        pe.wait_ge(S["ys_done"], i * 4 + (k + 1))
                        for c in range(KC):
                            if c >= 4:
                                pe.wait_ge(S["wide_free"], i * 64 + (16 * k + c - 3))
                            for f in range(2):
                                mm = nc.tensor.matmul(bank[c % 4][:, 0:T], w_down[:, f, c * P:(c + 1) * P], hid[:, f],
                                                      start=(f == 0), stop=(f == 1))
                            mm.then_inc(S["wide_ready"], 1)
                        pe.sem_inc(S["d_ready"], 1)
                        pe.sem_inc(S["prod_turned"], 1)
                    with pe.Else():
                        for n, (w, done) in enumerate(((w_gate, "g_ready"), (w_up, "u_done"))):
                            if n:
                                pe.wait_ge(slot_loaded[slots[1]], landed[1])
                                pe.wait_ge(S["hid_ready"], i * 4 + (k + 1))
                            for kk in range(KC):
                                for f in range(2):
                                    mm = nc.tensor.matmul(bank[4 + n][f * WIN:(f + 1) * WIN, 0:P], hwin[:, k % 2, kk],
                                                          w[:, kk, f * P:(f + 1) * P], start=(kk == 0), stop=(kk == KC - 1))
                            mm.then_inc(S[done], 1)
                        pe.wait_ge(S["prod_ready"], i * 4 + (k + 1))
                        nc.tensor.transpose(bank[6][:, 0:P], sil[:, 1, 0:P], ident[:]).then_inc(S["prod_turned"], 1)
                        pe.wait_ge(slot_loaded[slots[2]], landed[2])
                        pe.wait_ge(S["hid_ready"], i * 4 + (k + 2))
                        pe.wait_ge(S["ys_done"], i * 4 + (k + 1))
                        for c in range(KC):
                            for f in range(2):
                                mm = nc.tensor.matmul(bank[c // 4][:, (c % 4) * P:(c % 4 + 1) * P],
                                                      w_down[:, f, c * P:(c + 1) * P], hid[:, f, 0:P],
                                                      start=(f == 0), stop=(f == 1))
                        mm.then_inc(S["d_ready"], 1)
                        pe.sem_inc(S["wide_ready"], 16)

            pe.wait_ge(S["ys_done"], NE + 1)
            PT = [(P * j, min(P, SLOTS - P * j)) for j in range(5)]
            for j, (s_, n) in enumerate(PT):
                b = 4 + j % 2
                fill("pt", b, j // 2)
                for q, (t0, rows) in enumerate(TOK):
                    mm = nc.tensor.transpose(bank[b][0:n, t0:t0 + rows], pm[0:rows, q, s_:s_ + n], ident[0:rows, 0:rows])
                mm.then_inc(bank_ready[b], 1)

            def y_rows(c):
                for half, tiles in ((0, PT[0:3]), (1, PT[3:5])):
                    b = 4 + 2 * (c % 2) + half
                    fill("unsort", b, c // 2)
                    for m, (s_, n) in enumerate(tiles):
                        mm = nc.tensor.transpose(bank[b][0:n, m * P:(m + 1) * P], ys[:, c, s_:s_ + n], ident[:])
                    mm.then_inc(bank_ready[b], 1)

            y_rows(0)
            pe.wait_ge(bank_free[4], use("pt", 4, 2))
            pe.wait_ge(bank_free[5], use("pt", 5, 1))
            def result_rows(j, q):
                t0, rows = TOK[q]
                pe.wait_ge(S["gx_ready"], 4 * j + 4)
                fill("unsort", 2, 3 * j + q)
                for n in range(4):
                    mm = nc.tensor.transpose(bank[2][0:rows, n * P:(n + 1) * P], gx[:, 4 * j + n, t0:t0 + rows], ident[:])
                mm.then_inc(bank_ready[2], 1)

            def square_sums(j):
                pe.wait_ge(S["squares_ready"], 12 + j + 1)
                if j == 0:
                    fill("unsort", 3)
                for n in range(4):
                    mm = nc.tensor.matmul(bank[3][:, 0:T], ones[:], hT[:, 4 * j + n], start=(j == 0 and n == 0),
                                          stop=(j == 3 and n == 3))
                if j == 3:
                    mm.then_inc(bank_ready[3], 1)

            for c in range(KC):
                if c + 1 < KC:
                    y_rows(c + 1)
                for half in range(2):
                    b = 4 + 2 * (c % 2) + half
                    pe.wait_ge(bank_free[b], use("unsort", b, c // 2))
                fill("unsort", c % 2, c // 2)
                for j, (s_, n) in enumerate(PT):
                    mm = nc.tensor.matmul(bank[c % 2][:, 0:T], ytok[0:n, c % 2, j * P:(j + 1) * P], pt[0:n, j],
                                          start=(j == 0), stop=(j == 4))
                mm.then_inc(bank_ready[c % 2], 1)
                if c >= 4:
                    if c % 4 < 3:
                        result_rows(c // 4 - 1, c % 4)
                    else:
                        square_sums(c // 4 - 1)
            square_sums(3)
            for q in range(3):
                result_rows(3, q)
            pe.wait_ge(S["y_ready"], G + 1)
            fill("n3", 4)
            for q, (t0, rows) in enumerate(TOK):
                mm = nc.tensor.transpose(bank[4][0:rows, q * P:(q + 1) * P], rs[:, t0:t0 + rows], ident[:])
            mm.then_inc(bank_ready[4], 1)

        @block.vector
        def _(ve):
            def flat(ap):
                return ap.rearrange("p k n -> p (k n)")

            def take(name, b, k=0):
                ve.wait_ge(bank_ready[b], use(name, b, k))

            ve.sem_inc(S["hid_ready"], 1)
            ve.sem_inc(S["ys_done"], 1)
            dve.mark(ve.memset(dt_tok[:], 0.0))
            dve.mark(ve.memset(wend[:], 0.0))
            ve.memset(vrow, 0.0).then_inc(S["vrow_zero"], 1)
            for c in range(KC):
                b = c % 4
                take("x", b, c // 4)
                ve.tensor_copy(xT[:, c], bank[b][:, 0:T]).then_inc(bank_free[b], 1)
            take("vec", 5)
            ve.tensor_copy(vcol[:, 0:512], bank[5][:]).then_inc(bank_free[5], 1)
            take("vec", 6)
            ve.tensor_copy(vcol[:, 512:896], bank[6][:, 0:384]).then_inc(bank_free[6], 1)
            dve.mark(ve.memset(upad[:, :, 0:CK - 1], 0.0))
            dve.link(ve, ve.memset(part_glu, 0.0))
            ve.sem_inc(S["part_zero"], 1)

            def inv_rms(name, b, n, width):
                take(name, b)
                ve.tensor_scalar(stat[:], bank[b][:, 0:T], 1.0 / width, EPS, ALU.mult, ALU.add).then_inc(S["mean_ready"], 1)
                ve.wait_ge(S["root_ready"], n)
                ve.sem_inc(bank_free[b], 1)
                dve.link(ve, ve.reciprocal(rs[:], rs[:]))

            def normalise(q):
                dve.link(ve, ve.tensor_tensor(hT[:, 4 * q:4 * q + 4], xT[:, 4 * q:4 * q + 4],
                                              rs[:].unsqueeze(1).broadcast_to([P, 4, T]), ALU.mult))
                ve.sem_inc(S["hn_ready"], 1)

            def scales(gvec, scale):
                dve.link(ve, ve.scalar_tensor_tensor(out=scaleA[:], in0=mod[:, scale:scale + KC], scalar=1.0,
                                                     in1=bc(gvec, NSEQ), op0=ALU.add, op1=ALU.mult))
                ve.sem_inc(S["scale_ready"], 1)

            def modulate_prompt(q, shift):
                for c in range(4 * q, 4 * q + 4):
                    ve.tensor_scalar(hT[:, c, 0:NP], hT[:, c, 0:NP], scaleA[:, c, 0:1], mod[:, shift + c, 0:1],
                                     ALU.mult, ALU.add).then_inc(S["hd_ready"], 1)

            inv_rms("n1", 4, 1, D)
            for q in range(4):
                normalise(q)
            for c in range(KC):
                b = c % 4
                take("cst", b, c // 4)
                ve.tensor_copy(usamp[:, c, :, 0:CK - 1],
                               bank[b][:, 0:240].rearrange("p (b l) -> p b l", b=NB)).then_inc(bank_free[b], 1)
            ve.wait_ge(bank_free[3], use("cst", 3, 3))
            ve.sem_inc(S["usamp_ready"], 1)
            for b in (6, 7):
                ve.wait_ge(bank_free[b], use("ada2", b, 1))
            scales(G_MIX, KC)
            for q in range(2):
                modulate_prompt(q, 0)
            cacc = [stat, rs]
            with ve.Fori(0, GLU_N) as i:
                with dve.loop(i, GLU_N, 2 * (2 + 2 * CK)):
                    for q in range(2):
                        for j in range(2):
                            n, c = 2 * q + j, i * 4 + (2 * q + j)
                            ve.wait_ge(bank_ready[j], i * 2 + (use("glu", j) + q))
                            ve.wait_ge(bank_free[2 + j], i * 2 + (use("glu", 2 + j) + q))
                            dve.mark(ve.tensor_tensor(upad[:, n, CK - 1:], bank[j][:, 0:NP], sgl[:, n, 0:NP], ALU.mult))
                            ve.tensor_tensor(flat(utail[:, ds(c, 1), 0:CK - 1]), bank[j][:, NP - CK + 1:NP],
                                             sgl[:, n, NP - CK + 1:NP], ALU.mult)
                            ve.tensor_tensor(flat(utail[:, ds(c, 1), CK - 1:]), bank[j][:, NP:T], sgl[:, n, NP:T], ALU.mult)
                            ve.tensor_tensor(usamp[:, ds(c, 1), :, CK - 1:].rearrange("p k b l -> p (k b) l"),
                                             bank[j][:, NP:T].rearrange("p (b l) -> p b l", b=NB),
                                             sgl[:, n, NP:T].rearrange("p (b l) -> p b l", b=NB),
                                             ALU.mult).then_inc(bank_free[j], 1)
                        for k in range(CK):
                            for j in range(2):
                                n, c = 2 * q + j, i * 4 + (2 * q + j)
                                tap = vcol[:, ds(c + (CW0 + k * KC), 1)]
                                u = upad[:, n, k:k + NP]
                                dve.wait(ve, back=1)
                                if k == 0:
                                    ins = ve.tensor_scalar(cacc[j][:, 0:NP], u, tap, vcol[:, ds(c + (P + 40), 1)],
                                                           ALU.mult, ALU.add)
                                else:
                                    out = cacc[j][:, 0:NP] if k < CK - 1 else flat(vb[:, ds(c, 1), 0:NP])
                                    ins = ve.scalar_tensor_tensor(out=out, in0=u, scalar=tap, in1=cacc[j][:, 0:NP],
                                                                  op0=ALU.mult, op1=ALU.add)
                                dve.mark(ins)
            dve.wait(ve)
            ve.sem_inc(S["conv_ready"], 1)

            take("tail", 7)
            dve.link(ve, ve.memset(part_mix, 0.0))
            ve.sem_inc(S["part_zero"], 1)
            take("ln", 4)
            dve.link(ve, ve.tensor_scalar(stat[:], bank[4][:, 0:T], 1.0 / D, None, ALU.mult))
            ve.sem_inc(bank_free[4], 1)
            ve.wait_ge(S["vsamp_ready"], 1)
            for q in range(4):
                v_ = vb[:, 4 * q:4 * q + 4]
                dve.mark(ve.tensor_tensor(v_, v_, stat[:].unsqueeze(1).broadcast_to([P, 4, T]), ALU.subtract))
                dve.wait(ve)
                ve.sem_inc(S["centred"], 1)
            inv_rms("lnsq", 5, 2, D)
            for q in range(4):
                v_ = vb[:, 4 * q:4 * q + 4]
                ve.tensor_tensor(v_, v_, rs[:].unsqueeze(1).broadcast_to([P, 4, T]), ALU.mult).then_inc(S["v_ready"], 1)
            take("dt", 6)
            ve.wait_ge(S["small_loaded"], 96)
            dve.mark(ve.tensor_tensor(dt_tok[:, 0:2], bank[6][:, 0:2 * H].rearrange("p (q h) -> p q h", q=2),
                                      rows_bc[:, 0:1].broadcast_to([P, 2, H]), ALU.add))
            dve.link(ve, ve.tensor_tensor(dt_tok[0:NS, 2], bank[6][0:NS, 2 * H:3 * H], rows_bc[0:NS, 0], ALU.add))
            ve.sem_inc(bank_free[6], 1)
            ve.scalar_tensor_tensor(out=sp_abs, in0=dt_tok[:], scalar=-1.0, in1=dt_tok[:], op0=ALU.mult,
                                    op1=ALU.max).then_inc(S["dt_abs"], 1)
            ve.wait_ge(S["dt_exp"], 1)
            dve.link(ve, ve.tensor_scalar(sp_u, sp_e, 1.0, None, ALU.add))
            ve.sem_inc(S["one_plus"], 1)
            dve.link(ve, ve.tensor_scalar(sp_d, sp_u, -1.0, None, ALU.add))
            dve.link(ve, ve.tensor_scalar(sp_z, sp_d, 0.0, None, ALU.is_equal))
            dve.link(ve, ve.tensor_tensor(sp_z, sp_z, sp_e, ALU.mult))
            dve.link(ve, ve.tensor_scalar(sp_d, sp_d, 1e-30, None, ALU.max))
            dve.link(ve, ve.reciprocal(sp_d, sp_d))
            dve.link(ve, ve.tensor_tensor(sp_m, sp_e, sp_d, ALU.mult))
            ve.wait_ge(S["dt_log"], 1)
            dve.link(ve, ve.tensor_tensor(sp_m, sp_m, sp_ln, ALU.mult))
            dve.link(ve, ve.tensor_tensor(sp_m, sp_m, sp_z, ALU.add))
            dve.link(ve, ve.scalar_tensor_tensor(out=dt_tok[:], in0=dt_tok[:], scalar=0.0, in1=sp_m, op0=ALU.max,
                                                 op1=ALU.add))
            ve.wait_ge(S["a_exp"], 1)
            ve.scalar_tensor_tensor(out=dtA[:], in0=dt_tok[:], scalar=-1.0, in1=rows_bc[:, 1:2].broadcast_to([P, 3, H]),
                                    op0=ALU.mult, op1=ALU.mult).then_inc(S["dta_ready"], 1)
            for b in range(4):
                ve.wait_ge(bank_free[b], use("gc", b, 3))
            with ve.Fori(0, 2) as i:
                for c in range(8):
                    b = c % 4
                    ve.wait_ge(bank_ready[b], i * 2 + (use("co", b) + c // 4))
                    g_ = flat(gb[:, ds(i * 8 + c, 1)])
                    ve.tensor_tensor(g_, g_, bank[b][:, 0:T], ALU.mult).then_inc(bank_free[b], 1)

            take("cum", 7)
            cum = bank[7][:, 0:192].rearrange("p (q h) -> p q h", q=6)
            dve.mark(ve.tensor_copy(acum[:, 0:2], cum[:, 0:2]))
            dve.link(ve, ve.tensor_copy(acum[0:NS, 2], cum[0:NS, 2]))
            dve.mark(ve.tensor_tensor(wend[:, 0], cum[:, 3], acum[:, 0], ALU.subtract))
            dve.mark(ve.tensor_tensor(wend[:, 2], cum[:, 4], acum[:, 1], ALU.subtract))
            dve.link(ve, ve.tensor_tensor(wend[0:NS, 3], cum[0:NS, 5], acum[0:NS, 2], ALU.subtract))
            dve.link(ve, ve.tensor_tensor(wend[:, 1], wend[:, 0], cum[:, 4], ALU.add))
            ve.sem_inc(S["w_arg"], 1)
            ve.sem_inc(bank_free[7], 1)
            ve.wait_ge(S["w_exp"], 1)
            dve.mark(ve.tensor_tensor(wend[:, 0:2], wend[:, 0:2], dt_tok[:, 0:1].broadcast_to([P, 2, H]), ALU.mult))
            dve.link(ve, ve.tensor_tensor(wend[:, 2:4], wend[:, 2:4], dt_tok[:, 1:3], ALU.mult))
            ve.sem_inc(S["w_ready"], 1)

            dve.mark(ve.memset(xraw[:, :, 0:SK - 1], 0.0))
            for half in range(2):
                take("sst", 4 + half)
                ve.tensor_copy(xsamp[:, 12 * half:12 * half + 12, :, 0:SK - 1],
                               bank[4 + half][:, 0:288].rearrange("p (k b l) -> p k b l", k=12, b=NB)).then_inc(
                                   bank_free[4 + half], 1)
            dve.wait(ve)
            with ve.Fori(0, XBC_N) as i:
                with dve.loop(i, XBC_N, 8 * 4):
                    for n in range(8):
                        b, par, c = n % 4, n % 2, i * 8 + n
                        ve.wait_ge(bank_ready[b], i * 2 + (use("xbc", b) + n // 4))
                        dve.mark(ve.tensor_copy(xraw[:, par, SK - 1:], bank[b][:, 0:NP]))
                        ve.tensor_copy(flat(xtail[:, ds(c, 1), 0:SK - 1]), bank[b][:, NP - SK + 1:NP])
                        ve.tensor_copy(xsamp[:, ds(c, 1), :, SK - 1:].rearrange("p k b l -> p (k b) l"),
                                       bank[b][:, NP:T].rearrange("p (b l) -> p b l", b=NB)).then_inc(bank_free[b], 1)
                        if n >= 2:
                            ve.wait_ge(S["xbc_ready"], i * 8 + n)
                        else:
                            ve.wait_ge(S["xbc_ready"], i * 8 + 1)
                        for k in range(SK):
                            tap = vcol[:, ds(c + (SW0 + k * XC), 1)]
                            u = xraw[:, par, k:k + NP]
                            dve.wait(ve)
                            if k == 0:
                                dve.mark(ve.tensor_scalar(acc[:, par], u, tap, None, ALU.mult))
                            else:
                                ins = ve.scalar_tensor_tensor(out=acc[:, par], in0=u, scalar=tap, in1=acc[:, par],
                                                              op0=ALU.mult, op1=ALU.add)
                                if k < SK - 1:
                                    dve.mark(ins)
                                else:
                                    ins.then_inc(S["acc_ready"], 1)
            for b in range(4):
                ve.wait_ge(bank_free[b], use("xbc", b, 2 * XBC_N - 1))
            dve.link(ve, ve.tensor_copy(xtail[:, :, SK - 1:].rearrange("p k (b l) -> p k b l", b=NB),
                                        xsamp[:, :, :, NL:NL + SK - 1]))
            ve.sem_inc(S["xtail_ready"], 1)
            dve.link(ve, ve.tensor_copy(tmps, bc(CONV_B, NS)))
            for k in range(SK):
                w = vcol[:, SW0 + k * XC:SW0 + (k + 1) * XC]
                dve.link(ve, ve.tensor_tensor(bl(uxs), xsamp[:, :, :, k:k + NL], bc(w, NB, NL), ALU.mult))
                dve.link(ve, ve.tensor_tensor(tmps, tmps, uxs, ALU.add))
            ve.sem_inc(S["xpad_ready"], 1)

            ve.wait_ge(S["xtail_out"], 32)
            ve.wait_ge(S["xbc_ready"], XC + 2)
            for b in range(4):
                ve.wait_ge(bank_free[b], use("z2", b, 1))
            with ve.Fori(0, G) as g:
                with dve.loop(g, G, 2 + 4 * 2):
                    ve.wait_ge(bank_ready[3], g * 5 + use("ssd", 3))
                    dve.mark(ve.tensor_tensor(cbm[:, 0:2], bank[3][:, 0:NP].rearrange("p (q n) -> p q n", q=2),
                                              upper[:].unsqueeze(1).broadcast_to([P, 2, P]), ALU.mult))
                    ve.tensor_tensor(cbm[0:NS, 2, 0:NS], bank[3][0:NS, 2 * P:2 * P + NS], ublk[:], ALU.mult).then_inc(
                        bank_free[3], 1)
                    ve.wait_ge(bank_ready[2], g * 5 + use("ssd", 2))
                    ve.wait_ge(bank_ready[1], g * 8 + (use("ssd", 1) - 1))
                    dve.mark(ve.tensor_copy(btok[:, 0:2], bank[2][:, 0:NP].rearrange("p (q n) -> p q n", q=2)))
                    ve.tensor_copy(btok[0:NS, 2], bank[2][0:NS, 2 * P:3 * P]).then_inc(bank_free[2], 1)
                    ve.wait_ge(bank_free[2], g * 5 + use("ssd", 2))
                    ve.tensor_tensor(bexp[0:NS], btok[0:NS, 2:3].broadcast_to([NS, NB, P]), bc(seqsel[:], P),
                                     ALU.mult).then_inc(S["bexp_ready"], 1)
                    for k in range(4):
                        par, c = k % 2, g * 4 + k
                        ve.wait_ge(bank_ready[3], g * 5 + (use("ssd", 3) + 1 + k))
                        ve.wait_ge(bank_ready[7], g * 4 + (use("ssd", 7) - 1 + k))
                        dve.mark(ve.tensor_copy(xtok[:, 0:2], bank[3][:, 0:NP].rearrange("p (q n) -> p q n", q=2)))
                        ve.tensor_copy(xtok[0:NS, 2], bank[3][0:NS, 2 * P:3 * P]).then_inc(bank_free[3], 1)
                        ve.wait_ge(bank_free[3], g * 5 + (use("ssd", 3) + 1 + k))
                        dve.wait(ve)
                        ve.wait_ge(bank_ready[1], g * 8 + (use("ssd", 1) - 1 + 2 * k))
                        for w, q, rows in ((0, 0, P), (1, 0, P), (2, 1, P), (3, 2, NS)):
                            ins = ve.tensor_tensor(xw[0:rows, w].rearrange("p (h q) -> p h q", h=2),
                                                   xtok[0:rows, q].rearrange("p (h q) -> p h q", h=2),
                                                   bc(wend[0:rows, w, ds(g * 8 + 2 * k, 2)], HD), ALU.mult)
                        ins.then_inc(S["xw_ready"], 1)
                        for h in range(2):
                            head = g * 8 + (2 * k + h)
                            ve.wait_ge(bank_ready[5 + h], g * 4 + (use("ssd", 5 + h) + k))
                            for q, (t0, rows) in enumerate(TOK):
                                ins = ve.tensor_scalar(mt[0:rows, h, t0:t0 + rows], bank[5 + h][0:rows, t0:t0 + rows],
                                                       acum[0:rows, q, ds(head, 1)], 0.0, ALU.subtract, ALU.min)
                            ins.then_inc(S["seg_ready"], 1)
                        for h in range(2):
                            head = g * 8 + (2 * k + h)
                            ve.wait_ge(S["exp_ready"], g * 8 + (2 * k + h + 1))
                            for q, (t0, rows) in enumerate(TOK):
                                ve.scalar_tensor_tensor(out=mt[0:rows, h, t0:t0 + rows], in0=mt[0:rows, h, t0:t0 + rows],
                                                        scalar=dt_tok[0:rows, q, ds(head, 1)],
                                                        in1=cbm[0:rows, q, 0:rows], op0=ALU.mult, op1=ALU.mult)
                            ve.wait_ge(bank_free[5 + h], g * 4 + (use("ssd", 5 + h) + k))
                            ve.tensor_tensor(cs[:, h], cs[:, h], flat(xbcT[:, ds(g + (KC + G), 1), P:T]),
                                             ALU.mult).then_inc(S["m_ready"], 1)
                        ve.wait_ge(S["scaled"], g * 4 + (k + 2))
                        for b in range(2):
                            ve.wait_ge(bank_ready[b], g * 8 + (use("ssd", b) + 2 * k + 1))
                            ve.tensor_tensor(s0[:, par, 4 * b:4 * b + 4], s0[:, par, 4 * b:4 * b + 4],
                                             bank[b][:].rearrange("p (b n) -> p b n", b=4), ALU.add).then_inc(
                                                 bank_free[b], 1)
                        ve.wait_ge(bank_ready[7], g * 4 + (use("ssd", 7) + k))
                        x_ = flat(xbcT[:, ds(c, 1)])
                        dve.link(ve, ve.scalar_tensor_tensor(out=x_, in0=x_,
                                                             scalar=dcol[:, ds(c, 1)], in1=bank[7][:, 0:T],
                                                             op0=ALU.mult, op1=ALU.add))
                        ve.sem_inc(bank_free[7], 1)
                        ve.tensor_tensor(flat(zb[:, ds(c, 1)]), flat(zb[:, ds(c, 1)]), x_, ALU.mult).then_inc(
                            S["y_done"], 1)
            ve.wait_ge(S["sf_out"], 16 * KC)
            dve.link(ve, ve.memset(part_mix, 0.0))
            ve.sem_inc(S["part_zero"], 1)
            for q in range(G):
                take("gn", q)
                ve.tensor_scalar(grs[:, q], bank[q][:, 0:T], 1.0 / (D // G), EPS, ALU.mult, ALU.add).then_inc(
                    S["gmean_ready"], 1)
            ve.wait_ge(S["y_done"], KC)
            for q in range(G):
                ve.wait_ge(S["groot_ready"], q + 1)
                ve.sem_inc(bank_free[q], 1)
                dve.link(ve, ve.reciprocal(grs[:, q], grs[:, q]))
                for c in range(4 * q, 4 * q + 4):
                    dve.mark(ve.scalar_tensor_tensor(out=zb[:, c], in0=zb[:, c], scalar=SSD_G[:, c:c + 1],
                                                     in1=grs[:, q], op0=ALU.mult, op1=ALU.mult))
                dve.wait(ve)
                ve.sem_inc(S["y_ready"], 1)
            ve.wait_ge(S["sig_ready"], 4)
            with ve.Fori(0, 2) as i:
                with dve.loop(i, 2, 8):
                    for c in range(8):
                        b = c % 4
                        ve.wait_ge(bank_ready[b], i * 2 + (use("so", b) + c // 4))
                        v_, g_ = flat(vb[:, ds(i * 8 + c, 1)]), flat(gb[:, ds(i * 8 + c, 1)])
                        dve.link(ve, ve.tensor_tensor(v_, v_, bank[b][:, 0:T], ALU.mult))
                        ve.sem_inc(bank_free[b], 1)
                        ve.tensor_tensor(g_, g_, v_, ALU.add).then_inc(S["merged"], 1)

            def add_gated(b, c, gate, done):
                g_ = mod[:, ds(gate, 1)] if not isinstance(gate, int) else mod[:, gate:gate + 1]
                x_ = xT[:, ds(c, 1)] if not isinstance(c, int) else xT[:, c:c + 1]
                x_p, x_s = flat(x_[:, :, 0:NP]), flat(x_[:, :, NP:T])
                dve.mark(ve.scalar_tensor_tensor(out=x_p, in0=bank[b][:, 0:NP], scalar=g_[:, :, 0:1], in1=x_p,
                                                 op0=ALU.mult, op1=ALU.add))
                tmp = (rs, stat)[b % 2][:, NP:T]
                dve.link(ve, ve.tensor_tensor(tmp.rearrange("p (b l) -> p b l", b=NB),
                                              bank[b][:, NP:T].rearrange("p (b l) -> p b l", b=NB),
                                              bc(flat(g_[:, :, 1:NSEQ]), NL), ALU.mult))
                ve.sem_inc(bank_free[b], 1)
                ve.tensor_tensor(x_s, x_s, tmp, ALU.add).then_inc(S[done], 1)

            with ve.Fori(0, 2) as i:
                with dve.loop(i, 2, 16):
                    for c in range(8):
                        b = c % 4
                        ve.wait_ge(bank_ready[b], i * 2 + (use("wo", b) + c // 4))
                        add_gated(b, i * 8 + c, i * 8 + (2 * KC + c), "x_mid")
            ve.wait_ge(S["x_mid"], KC)
            scales(G_FFN, 4 * KC)
            inv_rms("n2", 0, 3, D)
            for q in range(4):
                normalise(q)
                if q < 2:
                    modulate_prompt(q, 3 * KC)

            neg, m1_, m2_ = small[0], small[1], small[2]
            for par in range(2):
                ve.wait_ge(st_out[par], 128)
            ve.wait_ge(S["sf_out"], 16 * KC)
            dve.link(ve, ve.memset(lg, 0.0))
            take("route", 1)
            dve.mark(ve.tensor_tensor(lg[:, 0:2], bank[1][:, 0:72].rearrange("p (q n) -> p q n", q=2),
                                      rbias[:].unsqueeze(1).broadcast_to([P, 2, 36]), ALU.add))
            dve.link(ve, ve.tensor_tensor(lg[0:NS, 2], bank[1][0:NS, 72:108], rbias[0:NS], ALU.add))
            ve.sem_inc(bank_free[1], 1)
            ve.wait_ge(S["pooled"], 1)
            cand, ohg = small[3][:, :, 0:NG], small[4][:, :, 0:NG]
            oh1, oh2, prob, left, cand8 = [small[5 + n][:, :, 0:EG] for n in range(5)]

            def iota(n):
                return iota_e[:, 0:n].unsqueeze(1).broadcast_to([P, 3, n])

            def first_of(onehot, cnd, values, top, idx, n):
                dve.link(ve, ve.tensor_tensor(cnd, values, bc(top, n), ALU.is_equal))
                dve.link(ve, ve.scalar_tensor_tensor(out=cnd, in0=cnd, scalar=-64.0, in1=iota(n), op0=ALU.mult,
                                                     op1=ALU.add))
                dve.link(ve, ve.tensor_reduce(idx, cnd, AX_X, ALU.min))
                dve.link(ve, ve.tensor_tensor(onehot, cnd, bc(idx, n), ALU.is_equal))

            dve.link(ve, ve.tensor_reduce(gmax, lg[:, :, 0:NG], AX_X, ALU.max))
            first_of(ohg, cand, lg[:, :, 0:NG], gmax, gfirst, NG)
            dve.link(ve, ve.tensor_tensor(lg[:, :, 0:NG], lg[:, :, 0:NG], bc(gmax, NG), ALU.subtract))
            ve.sem_inc(S["e_arg"], 1)
            chosen_l = small[10].rearrange("p q (g e) -> p q g e", g=NG)
            dve.link(ve, ve.tensor_tensor(chosen_l, lg[:, :, NG:36].rearrange("p q (g e) -> p q g e", g=NG),
                                          bc(ohg, EG), ALU.mult))
            dve.link(ve, ve.tensor_reduce(sel, chosen_l.rearrange("p q g e -> p q e g"), AX_X, ALU.add))
            dve.link(ve, ve.tensor_reduce(emax, sel, AX_X, ALU.max))
            dve.link(ve, ve.tensor_tensor(sel, sel, bc(emax, EG), ALU.subtract))
            ve.sem_inc(S["e_arg"], 1)
            ve.wait_ge(S["gexp"], 1)
            dve.link(ve, ve.tensor_reduce(gsum, lg[:, :, 0:NG], AX_X, ALU.add))
            dve.link(ve, ve.reciprocal(gtop, gsum))
            ve.wait_ge(S["eexp"], 1)
            dve.link(ve, ve.tensor_reduce(esum, sel, AX_X, ALU.add))
            dve.link(ve, ve.reciprocal(esum, esum))
            dve.link(ve, ve.tensor_tensor(prob, sel, bc(esum, EG), ALU.mult))
            dve.link(ve, ve.tensor_reduce(p1, prob, AX_X, ALU.max))
            first_of(oh1, cand8, prob, p1, first1, EG)
            dve.link(ve, ve.scalar_tensor_tensor(out=left, in0=oh1, scalar=-2.0, in1=prob, op0=ALU.mult, op1=ALU.add))
            dve.link(ve, ve.tensor_reduce(p2, left, AX_X, ALU.max))
            first_of(oh2, cand8, left, p2, first2, EG)
            dve.link(ve, ve.tensor_tensor(ptot, p1, p2, ALU.add))
            dve.link(ve, ve.reciprocal(ptot, ptot))
            dve.link(ve, ve.tensor_tensor(ptot, ptot, gtop, ALU.mult))
            dve.mark(ve.tensor_tensor(gA, p1, ptot, ALU.mult))
            dve.mark(ve.tensor_tensor(gB, p2, ptot, ALU.mult))
            for m_, oh in ((m1_, oh1), (m2_, oh2)):
                dve.mark(ve.tensor_tensor(m_.rearrange("p q (g e) -> p q g e", g=NG), bc(ohg, EG),
                                          oh.unsqueeze(2).broadcast_to([P, 3, NG, EG]), ALU.mult))
            dve.wait(ve)
            ve.tensor_tensor(chosen, m1_, m2_, ALU.add).then_inc(S["cnt_ready"], 1)
            take("route", 2)
            dve.link(ve, ve.tensor_copy(cntb[0:NE], bank[2][0:NE, 0:1].broadcast_to([NE, P])))
            ve.sem_inc(bank_free[2], 1)
            ve.sem_inc(S["cnt_ready"], 1)
            pos = small[11]
            dve.mark(ve.memset(pos, 0.0))
            dve.link(ve, ve.memset(meta, 0.0))
            take("route", 3)
            dve.mark(ve.tensor_copy(pos[:, 0:2], bank[3][:, 0:64].rearrange("p (q e) -> p q e", q=2)))
            dve.mark(ve.tensor_copy(pos[0:NS, 2], bank[3][0:NS, 64:96]))
            dve.mark(ve.tensor_copy(meta[:, 0, 0:NE], bank[3][:, 128:160]))
            dve.mark(ve.tensor_scalar(meta[:, 1, 0:NE], bank[3][:, 96:128], float(SLOTS - WIN), None, ALU.min))
            dve.link(ve, ve.tensor_scalar(meta[:, 2, 0:NE], bank[3][:, 96:128], float(SLOTS - T), None, ALU.min))
            ve.sem_inc(bank_free[3], 1)
            dve.link(ve, ve.tensor_copy(meta_i[:], meta))
            ve.sem_inc(S["meta_ready"], 1)
            for m_, s_, e_ in ((m1_, sA, eA), (m2_, sB, eB)):
                dve.link(ve, ve.tensor_tensor(neg, pos, m_, ALU.mult))
                dve.link(ve, ve.tensor_reduce(s_, neg, AX_X, ALU.add))
            for q, (t0, rows) in enumerate(TOK):
                dve.link(ve, ve.tensor_scalar(pm[0:rows, q], iota_s[0:rows], sA[0:rows, q:q + 1], None, ALU.is_equal))
                dve.mark(ve.scalar_tensor_tensor(out=pm[0:rows, q], in0=iota_s[0:rows], scalar=sB[0:rows, q:q + 1],
                                                 in1=pm[0:rows, q], op0=ALU.is_equal, op1=ALU.add))
                dve.wait(ve)
                ve.sem_inc(S["sort_ready"], 1)
            for m_, e_ in ((m1_, eA), (m2_, eB)):
                dve.link(ve, ve.tensor_tensor(neg, m_, iota(NE), ALU.mult))
                dve.link(ve, ve.tensor_reduce(e_, neg, AX_X, ALU.add))
            ve.sem_inc(S["pairs_ready"], 1)
            for c in range(KC):
                for half in range(2):
                    b = 2 * (c % 2) + half
                    take("gather", b, c // 2)
                    ve.tensor_copy(hs[:, c, T * half:T * (half + 1)], bank[b][:, 0:T]).then_inc(bank_free[b], 1)
            for b, dst in enumerate((gbc[:, 0:T], gbc[:, T:], ebc[:, 0:T], ebc[:, T:])):
                take("gates", b)
                ve.tensor_copy(dst, bank[b][:, 0:T]).then_inc(bank_free[b], 1)
            for b in range(4):
                ve.wait_ge(bank_free[b], use("gates", b))

            dve.link(ve, ve.memset(hid, 0.0))
            w_first = ve.value_load(meta_i[0:1, 1, 0:1], min_val=0, max_val=SLOTS - WIN)
            ve.tensor_copy(hwin[:, 0], hs[:, :, ds(w_first, WIN)]).then_inc(S["win_ready"], 1)
            with ve.Fori(0, 8) as i:
                with dve.loop(i, 8, 4 * 3):
                    for k in range(4):
                        nxt = ve.value_load(meta_i[0:1, 1, ds(i * 4 + (k + 1), 1)], min_val=0, max_val=SLOTS - WIN)
                        ve.wait_ge(S["u_done"], i * 4 + (k + 1))
                        ve.tensor_copy(hwin[:, (k + 1) % 2], hs[:, :, ds(nxt, WIN)]).then_inc(S["win_ready"], 1)
                        n_pairs = ve.value_load(meta_i[0:1, 0, ds(i * 4 + k, 1)], min_val=0, max_val=T)
                        wn = ve.value_load(meta_i[0:1, 1, ds(i * 4 + k, 1)], min_val=0, max_val=SLOTS - WIN)
                        ww = ve.value_load(meta_i[0:1, 2, ds(i * 4 + k, 1)], min_val=0, max_val=SLOTS - T)
                        mine = iota_e[:, ds(i * 4 + k, 1)]
                        count = dve.n
                        with ve.If(n_pairs > WIN):
                            dve.link(ve, ve.scalar_tensor_tensor(out=gwin, in0=ebc[:, ds(ww, T)], scalar=mine,
                                                                 in1=gbc[:, ds(ww, T)], op0=ALU.is_equal, op1=ALU.mult))
                            ve.wait_ge(S["u_done"], i * 4 + (k + 2))
                            dve.mark(ve.tensor_tensor(hid[:, 0], bank[5][:, 0:T], gwin, ALU.mult))
                            dve.link(ve, ve.tensor_tensor(hid[:, 1], bank[7][:, 0:T], gwin, ALU.mult))
                            ve.wait_ge(S["sil_ready"], i * 4 + (k + 2))
                            ve.tensor_tensor(hid, hid, sil, ALU.mult).then_inc(S["hid_ready"], 1)
                            ve.sem_inc(S["prod_ready"], 1)
                            ve.wait_ge(S["ys_zero"], 1)
                            ve.wait_ge(S["ys_done"], i * 4 + (k + 1))
                            for c in range(KC):
                                ve.wait_ge(S["wide_ready"], i * 64 + (16 * k + c + 1))
                                y_ = ys[:, c, ds(ww, T)]
                                ve.tensor_tensor(y_, y_, bank[c % 4][:, 0:T], ALU.add).then_inc(S["wide_free"], 1)
                            ve.wait_ge(S["wide_free"], i * 64 + 16 * (k + 1))
                            ve.sem_inc(S["ys_done"], 1)
                        n_after, dve.n = dve.n, count
                        with ve.Else():
                            dve.link(ve, ve.scalar_tensor_tensor(out=gwin[:, 0:WIN], in0=ebc[:, ds(wn, WIN)], scalar=mine,
                                                                 in1=gbc[:, ds(wn, WIN)], op0=ALU.is_equal, op1=ALU.mult))
                            ve.wait_ge(S["u_done"], i * 4 + (k + 2))
                            ve.wait_ge(S["sil_ready"], i * 4 + (k + 2))
                            ve.tensor_tensor(sil[:, 1, 0:P], bank[5][:, 0:P], sil[:, 0, 0:P], ALU.mult).then_inc(
                                S["prod_ready"], 1)
                            ve.wait_ge(S["prod_turned"], i * 4 + (k + 1))
                            ve.tensor_tensor(hid[:, :, 0:WIN], bank[6][:, 0:P].rearrange("p (f w) -> p f w", f=2),
                                             gwin[:, 0:WIN].unsqueeze(1).broadcast_to([P, 2, WIN]), ALU.mult).then_inc(
                                                 S["hid_ready"], 1)
                            ve.wait_ge(S["ys_zero"], 1)
                            ve.wait_ge(S["ys_done"], i * 4 + (k + 1))
                            ve.wait_ge(S["d_ready"], i * 4 + (k + 1))
                            for q in range(4):
                                y_ = ys[:, 4 * q:4 * q + 4, ds(wn, WIN)]
                                ins = ve.tensor_tensor(y_, y_, bank[q][:].rearrange("p (c w) -> p c w", c=4)[:, :, 0:WIN], ALU.add)
                            ins.then_inc(S["ys_done"], 1)
                            ve.sem_inc(S["wide_free"], 16)
                            dve.skip(ve, 2)
                        assert dve.n == n_after

            for j in range(5):
                n = min(P, SLOTS - P * j)
                take("pt", 4 + j % 2, j // 2)
                ve.tensor_copy(pt[0:n, j], bank[4 + j % 2][0:n, 0:T]).then_inc(bank_free[4 + j % 2], 1)
            for c in range(KC):
                take("unsort", c % 2, c // 2)
                add_gated(c % 2, c, 5 * KC + c, "moe_ready")
                ve.wait_ge(S["moe_ready"], c + 1)
                ve.tensor_scalar(gx[:, c], xT[:, c], FIN_G[:, c:c + 1], None, ALU.mult).then_inc(S["gx_ready"], 1)
            inv_rms("unsort", 3, 4, D)
            ve.sem_inc(S["y_ready"], 1)
            take("n3", 4)
            turned = bank[4][:, 0:3 * P].rearrange("p (q n) -> p q n", q=3)[:, :, 0]
            dve.mark(ve.tensor_copy(rcol[:, 0:2], turned[:, 0:2]))
            dve.link(ve, ve.tensor_copy(rcol[0:NS, 2:3], turned[0:NS, 2:3]))
            ve.sem_inc(bank_free[4], 1)
            ve.wait_ge(bank_free[2], use("unsort", 2, 11))
            ve.tensor_scalar(yrow_q[1], yrow_q[1], rcol[:, 1:2], None, ALU.mult).then_inc(S["y_fin"], 1)


_OUTS = [
    (1, NP, D), (NB, NL, D), (1, 1, H, HD, P), (1, 1, SK - 1, 3072), (1, 1, CK - 1, D),
    (1, NB, H, HD, P), (1, NB, SK - 1, 3072), (1, NB, CK - 1, D),
]


def kernel(**inputs):
    import numpy as _np
    import concourse.bacc as _bacc
    from concourse import mybir as _mybir
    from concourse.bass_utils import run_bass_kernel_spmd as _run

    nc = _bacc.Bacc("TRN2", target_bir_lowering=False, num_devices=1)
    arrays, a = {}, {}
    for name, x in inputs.items():
        x = _np.ascontiguousarray(x)
        arrays[f"in_{name}"] = x
        a[name] = nc.dram_tensor(f"in_{name}", x.shape, _mybir.dt.from_np(x.dtype), kind="ExternalInput").ap()
    outs = [nc.dram_tensor(f"out_{i}", shape, _mybir.dt.float32, kind="ExternalOutput").ap()
            for i, shape in enumerate(_OUTS)]
    hybrid_step(nc, a, outs)
    r = _run(nc, [arrays], core_ids=[0])
    return tuple(r.results[0][f"out_{i}"] for i in range(len(_OUTS)))
```
